# Optimizing a Trainium2 kernel written in Bass

```python
import math
import jax, jax.numpy as jnp
from jax import lax
import numpy as np
import jax
import jax.numpy as jnp

D_MODEL = 1024
BATCH = 1
SEQ = 256
DEPTH = 2

N_A = DEPTH // 2
N_B = DEPTH - N_A
POOL_WINDOWS = (2, 4, 8, 16)
POOL_GROUP = D_MODEL // len(POOL_WINDOWS)
N_HEADS = 16
HEAD_DIM = 64
N_KV_GROUPS = 4
HEADS_PER_GROUP = N_HEADS // N_KV_GROUPS
CMP_STRIDE = 16
CMP_LEN = 2 * CMP_STRIDE
CMP_HIDDEN = 128
SLC_BLOCK = 64
N_SELECT = 16
WINDOW = 512
Q_BLOCK = 64
N_BRANCH = 3
ROPE_THETA = 500000.0
ROT_DIM = HEAD_DIM // 4
D_FF = 2816
CONV_W = 3
PLE_DIM = 256

EPS = 1e-6
NEG = -1e30
FORCE_SCORE = 1e4


def rmsnorm(x, g):
    xf = x.astype(jnp.float32)
    y = xf * lax.rsqrt(jnp.mean(xf * xf, axis=-1, keepdims=True) + EPS) * g.astype(jnp.float32)
    return y.astype(x.dtype)

def rope_tables(pos):
    inv_freq = ROPE_THETA ** (-jnp.arange(0, ROT_DIM, 2, dtype=jnp.float32) / ROT_DIM)
    ang = pos.astype(jnp.float32)[..., None] * inv_freq
    return jnp.cos(ang), jnp.sin(ang)

def rope(x, cos, sin):
    xf = x.astype(jnp.float32)
    half = ROT_DIM // 2
    x1, x2, xp = xf[..., :half], xf[..., half:ROT_DIM], xf[..., ROT_DIM:]
    out = jnp.concatenate([x1 * cos - x2 * sin, x2 * cos + x1 * sin, xp], axis=-1)
    return out.astype(x.dtype)

def masked_softmax(s, mask):
    s = jnp.where(mask, s, NEG)
    m = jnp.max(s, axis=-1, keepdims=True)
    e = jnp.where(mask, jnp.exp(s - m), 0.0)
    return e / jnp.maximum(jnp.sum(e, axis=-1, keepdims=True), 1e-30)

def pool_mixer(h, w, scale):
    B, S, D = h.shape
    c = jnp.cumsum(h.astype(jnp.float32), axis=1)
    c = jnp.pad(c, ((0, 0), (1, 0), (0, 0)))
    t = jnp.arange(S)
    outs = []
    for gi, win in enumerate(POOL_WINDOWS):
        sl = slice(gi * POOL_GROUP, (gi + 1) * POOL_GROUP)
        cg = c[..., sl]
        lo = jnp.maximum(t + 1 - win, 0)
        cnt = jnp.minimum(t + 1, win).astype(jnp.float32)
        avg = (cg[:, t + 1] - cg[:, lo]) / cnt[:, None]
        u = (avg - h[..., sl].astype(jnp.float32)).astype(h.dtype)
        outs.append(jnp.einsum('bsc,cd->bsd', u, w[gi]))
    return jnp.concatenate(outs, axis=-1) * scale

def conv_ffn(h, w_up, conv_w, conv_b, w_down):
    S = h.shape[1]
    u = h @ w_up
    up = jnp.pad(u, ((0, 0), (CONV_W - 1, 0), (0, 0)))
    u = sum(conv_w[j] * up[:, j:j + S] for j in range(CONV_W)) + conv_b
    a, g = u[..., :D_FF], u[..., D_FF:]
    return (jax.nn.silu(g) * a) @ w_down

def compress(blocks, pos_emb, w1, w2):
    z = blocks + pos_emb
    z = z.reshape(z.shape[:3] + (CMP_LEN * HEAD_DIM,))
    return jax.nn.gelu(z @ w1) @ w2

def nsa_shared_kv(x, positions, norm_kv, w_kv, cmp_pos_k, cmp_w1_k, cmp_w2_k, cmp_pos_v, cmp_w1_v, cmp_w2_v):
    B, S, _ = x.shape
    h = rmsnorm(x, norm_kv)
    kv = (h @ w_kv).reshape(B, S, 2 * N_BRANCH, N_KV_GROUPS, HEAD_DIM).transpose(2, 0, 3, 1, 4)
    k_c, v_c, k_s, v_s, k_w, v_w = [kv[i] for i in range(2 * N_BRANCH)]
    cos, sin = rope_tables(positions)
    k_s = rope(k_s, cos[:, None], sin[:, None])
    k_w = rope(k_w, cos[:, None], sin[:, None])
    n_chunk = S // CMP_STRIDE
    n_cmp = n_chunk - 1
    def blocks_of(z):
        ch = z.reshape(B, N_KV_GROUPS, n_chunk, CMP_STRIDE, HEAD_DIM)
        return jnp.concatenate([ch[:, :, :-1], ch[:, :, 1:]], axis=3)
    kc = compress(blocks_of(k_c), cmp_pos_k, cmp_w1_k, cmp_w2_k)
    vc = compress(blocks_of(v_c), cmp_pos_v, cmp_w1_v, cmp_w2_v)
    end_idx = CMP_STRIDE * jnp.arange(n_cmp) + CMP_LEN - 1
    cos_c, sin_c = rope_tables(positions[:, end_idx])
    kc = rope(kc, cos_c[:, None], sin_c[:, None])
    n_slc = S // SLC_BLOCK
    ks_blk = k_s.reshape(B, N_KV_GROUPS, n_slc, SLC_BLOCK, HEAD_DIM)
    vs_blk = v_s.reshape(B, N_KV_GROUPS, n_slc, SLC_BLOCK, HEAD_DIM)
    pad = ((0, 0), (0, 0), (WINDOW, 0), (0, 0))
    kw_pad, vw_pad = jnp.pad(k_w, pad), jnp.pad(v_w, pad)
    return (kc, vc, ks_blk, vs_blk, kw_pad, vw_pad)

def nsa_attention(h, w_in, w_out, cos, sin, kv):
    kc, vc, ks_blk, vs_blk, kw_pad, vw_pad = kv
    B, S, _ = h.shape
    n_cmp = kc.shape[2]
    n_slc = ks_blk.shape[2]
    n_top = min(N_SELECT, n_slc)
    scale = HEAD_DIM ** -0.5
    proj = h @ w_in
    q = proj[..., :N_HEADS * HEAD_DIM].reshape(B, S, N_HEADS, HEAD_DIM)
    q = rope(q, cos[:, :, None], sin[:, :, None])
    q = q.reshape(B, S, N_KV_GROUPS, HEADS_PER_GROUP, HEAD_DIM).transpose(0, 2, 3, 1, 4)
    gates = jax.nn.sigmoid(proj[..., N_HEADS * HEAD_DIM:].astype(jnp.float32))
    gates = gates.reshape(B, S, N_KV_GROUPS, HEADS_PER_GROUP, N_BRANCH).transpose(0, 2, 3, 1, 4)

    c_idx = jnp.arange(n_cmp)
    c_end = CMP_STRIDE * c_idx + CMP_LEN - 1
    blk = jnp.arange(n_slc)
    c_start = CMP_STRIDE * c_idx
    overlap = ((c_start[:, None] < (blk[None] + 1) * SLC_BLOCK)
               & (c_start[:, None] + CMP_LEN > blk[None] * SLC_BLOCK)).astype(jnp.float32)
    gather = jax.vmap(jax.vmap(lambda kb, ix: kb[ix]))

    def block_fn(s):
        t = s + jnp.arange(Q_BLOCK)
        qb = lax.dynamic_slice_in_dim(q, s, Q_BLOCK, axis=3)
        gb = lax.dynamic_slice_in_dim(gates, s, Q_BLOCK, axis=3)
        sc = jnp.einsum('bghqd,bgcd->bghqc', qb, kc).astype(jnp.float32) * scale
        p_c = masked_softmax(sc, c_end[None, :] <= t[:, None])
        o_c = jnp.einsum('bghqc,bgcd->bghqd', p_c.astype(vc.dtype), vc)
        imp = jnp.einsum('bghqc,cn->bgqn', p_c, overlap)
        cur = t // SLC_BLOCK
        forced = (blk[None] == 0) | (blk[None] == cur[:, None]) | (blk[None] == cur[:, None] - 1)
        valid = blk[None] * SLC_BLOCK <= t[:, None]
        score = jnp.where(valid, jnp.where(forced, FORCE_SCORE, imp), NEG)
        vals, idx = lax.top_k(score, n_top)
        ok = vals > 0.5 * NEG
        ks_g = gather(ks_blk, idx).reshape(B, N_KV_GROUPS, Q_BLOCK, n_top * SLC_BLOCK, HEAD_DIM)
        vs_g = gather(vs_blk, idx).reshape(B, N_KV_GROUPS, Q_BLOCK, n_top * SLC_BLOCK, HEAD_DIM)
        kpos = idx[..., None] * SLC_BLOCK + jnp.arange(SLC_BLOCK)
        mask_s = (ok[..., None] & (kpos <= t[:, None, None])).reshape(B, N_KV_GROUPS, Q_BLOCK, n_top * SLC_BLOCK)
        ss = jnp.einsum('bghqd,bgqkd->bghqk', qb, ks_g).astype(jnp.float32) * scale
        p_s = masked_softmax(ss, mask_s[:, :, None])
        o_s = jnp.einsum('bghqk,bgqkd->bghqd', p_s.astype(vs_g.dtype), vs_g)
        kw = lax.dynamic_slice_in_dim(kw_pad, s, WINDOW + Q_BLOCK, axis=2)
        vw = lax.dynamic_slice_in_dim(vw_pad, s, WINDOW + Q_BLOCK, axis=2)
        kpos_w = s - WINDOW + jnp.arange(WINDOW + Q_BLOCK)
        diff = t[:, None] - kpos_w[None]
        mask_w = (diff >= 0) & (diff < WINDOW) & (kpos_w[None] >= 0)
        sw = jnp.einsum('bghqd,bgkd->bghqk', qb, kw).astype(jnp.float32) * scale
        p_w = masked_softmax(sw, mask_w)
        o_w = jnp.einsum('bghqk,bgkd->bghqd', p_w.astype(vw.dtype), vw)
        out = (gb[..., 0:1] * o_c.astype(jnp.float32) + gb[..., 1:2] * o_s.astype(jnp.float32)
               + gb[..., 2:3] * o_w.astype(jnp.float32))
        return out.astype(h.dtype)

    starts = jnp.arange(S // Q_BLOCK) * Q_BLOCK
    o = lax.map(block_fn, starts)
    o = o.transpose(1, 0, 4, 2, 3, 5).reshape(B, S, N_HEADS * HEAD_DIM)
    return o @ w_out

def first_inputs(seed: int = 0) -> dict:
    key = jax.random.key(seed)
    ks = iter(jax.random.split(key, 40))
    f32 = jnp.float32
    def w(shape, fan):
        return jax.random.normal(next(ks), shape, f32) * (fan ** -0.5)
    def gain(shape):
        return 1.0 + 0.05 * jax.random.normal(next(ks), shape, f32)
    def small(shape, s=0.02):
        return s * jax.random.normal(next(ks), shape, f32)
    q_cols = N_HEADS * HEAD_DIM + N_HEADS * N_BRANCH
    return {
        "x": jax.random.normal(next(ks), (BATCH, SEQ, D_MODEL), f32),
        "p": jax.random.normal(next(ks), (DEPTH, BATCH, SEQ, PLE_DIM), f32),
        "positions": jnp.broadcast_to(jnp.arange(SEQ, dtype=jnp.int32), (BATCH, SEQ)),
        "norm_mix": gain((DEPTH, D_MODEL)),
        "pool_w": w((N_A, len(POOL_WINDOWS), POOL_GROUP, POOL_GROUP), POOL_GROUP),
        "pool_scale": gain((N_A, D_MODEL)),
        "norm_kv": gain((D_MODEL,)),
        "w_kv": w((D_MODEL, 2 * N_BRANCH * N_KV_GROUPS * HEAD_DIM), D_MODEL),
        "cmp_pos_k": small((CMP_LEN, HEAD_DIM), 0.1),
        "cmp_w1_k": w((CMP_LEN * HEAD_DIM, CMP_HIDDEN), CMP_LEN * HEAD_DIM),
        "cmp_w2_k": w((CMP_HIDDEN, HEAD_DIM), CMP_HIDDEN),
        "cmp_pos_v": small((CMP_LEN, HEAD_DIM), 0.1),
        "cmp_w1_v": w((CMP_LEN * HEAD_DIM, CMP_HIDDEN), CMP_LEN * HEAD_DIM),
        "cmp_w2_v": w((CMP_HIDDEN, HEAD_DIM), CMP_HIDDEN),
        "w_in_b": w((N_B, D_MODEL, q_cols), D_MODEL),
        "w_out_b": w((N_B, N_HEADS * HEAD_DIM, D_MODEL), N_HEADS * HEAD_DIM),
        "norm_ffn": gain((DEPTH, D_MODEL)),
        "ffn_up": w((DEPTH, D_MODEL, 2 * D_FF), D_MODEL),
        "ffn_conv": w((DEPTH, CONV_W, 2 * D_FF), CONV_W),
        "ffn_conv_b": small((DEPTH, 2 * D_FF)),
        "ffn_down": w((DEPTH, D_FF, D_MODEL), D_FF),
        "norm_ple": gain((DEPTH, D_MODEL)),
        "ple_gate": w((DEPTH, D_MODEL, D_MODEL), D_MODEL),
        "ple_proj": w((DEPTH, PLE_DIM, D_MODEL), PLE_DIM),
        "norm_final": gain((D_MODEL,)),
    }

def first_block(x, p, positions, norm_mix, pool_w, pool_scale, norm_kv, w_kv,
              cmp_pos_k, cmp_w1_k, cmp_w2_k, cmp_pos_v, cmp_w1_v, cmp_w2_v,
              w_in_b, w_out_b, norm_ffn, ffn_up, ffn_conv, ffn_conv_b, ffn_down,
              norm_ple, ple_gate, ple_proj, norm_final):
    cos, sin = rope_tables(positions)
    kv = None
    for i in range(DEPTH):
        if i < N_A:
            x = x + pool_mixer(rmsnorm(x, norm_mix[i]), pool_w[i], pool_scale[i])
        else:
            if i == N_A:
                kv = nsa_shared_kv(x, positions, norm_kv, w_kv, cmp_pos_k, cmp_w1_k, cmp_w2_k,
                                   cmp_pos_v, cmp_w1_v, cmp_w2_v)
            j = i - N_A
            x = x + nsa_attention(rmsnorm(x, norm_mix[i]), w_in_b[j], w_out_b[j], cos, sin, kv)
        x = x + conv_ffn(rmsnorm(x, norm_ffn[i]), ffn_up[i], ffn_conv[i], ffn_conv_b[i], ffn_down[i])
        gate = jax.nn.sigmoid(rmsnorm(x, norm_ple[i]) @ ple_gate[i])
        x = x + gate * (p[i] @ ple_proj[i])
    return rmsnorm(x, norm_final)


GRID_W = 64
CTX_LEN = 256
N_MOD = 6

SSD_HEADS = 16
SSD_HEAD_DIM = 64
SSD_INNER = SSD_HEADS * SSD_HEAD_DIM
SSD_GROUPS = 4
SSD_STATE = 128
SSD_CONV = 5
SSD_CHUNK = 128
SSD_BC = SSD_GROUPS * SSD_STATE
SSD_CONV_DIM = SSD_INNER + 2 * SSD_BC
SSD_STATE_COLS = SSD_CONV_DIM + 2 * SSD_HEADS

CF_CH = 1024
CF_KERNEL = 31

AB_IN = SSD_INNER + SSD_STATE_COLS + 2 * CF_CH
AB_OUT = SSD_INNER + CF_CH

HG_HEADS = 8
HG_DK = 128
HG_DV = D_MODEL // HG_HEADS
HG_KEY = HG_HEADS * HG_DK
HG_VAL = HG_HEADS * HG_DV
HG_CHUNK = 64
HG_IN = HG_KEY + 2 * HG_VAL + 2 * HG_KEY

N_EXPERTS = 16
N_EXPERT_GROUPS = 4
EXPERTS_PER_GROUP = N_EXPERTS // N_EXPERT_GROUPS
TOP_K = 2
D_EXPERT = 512

N_EVEN = (DEPTH + 1) // 2
N_ODD = DEPTH // 2


def rmsnorm_2(x, g):
    xf = x.astype(jnp.float32)
    y = xf * lax.rsqrt(jnp.mean(xf * xf, axis=-1, keepdims=True) + EPS)
    return (y * g.astype(jnp.float32)).astype(x.dtype)

def layernorm(x, g, b):
    xf = x.astype(jnp.float32)
    mu = jnp.mean(xf, axis=-1, keepdims=True)
    xc = xf - mu
    var = jnp.mean(xc * xc, axis=-1, keepdims=True)
    return (xc * lax.rsqrt(var + EPS) * g.astype(jnp.float32) + b.astype(jnp.float32)).astype(x.dtype)

def modulation(cond, w, b):
    m = jax.nn.silu(cond) @ w + b
    return m.reshape(cond.shape[:-1] + (N_MOD, D_MODEL))

def dwconv(x, w, b):
    k = w.shape[0]
    y = lax.conv_general_dilated(x, w[:, None, :].astype(x.dtype), window_strides=(1,),
                                 padding=[(k // 2, k // 2)], dimension_numbers=("NWC", "WIO", "NWC"),
                                 feature_group_count=x.shape[-1])
    return y + b.astype(y.dtype)

def _flip(t):
    return jnp.flip(t, axis=1)

def _same(t):
    return t

def to_col_major(t, rows):
    b, _, ch = t.shape
    return t.reshape(b, rows, GRID_W, ch).transpose(0, 2, 1, 3).reshape(b, rows * GRID_W, ch)

def from_col_major(t, rows):
    b, _, ch = t.shape
    return t.reshape(b, GRID_W, rows, ch).transpose(0, 2, 1, 3).reshape(b, rows * GRID_W, ch)

def _carry_step(s, inp):
    dec, st = inp
    return dec * s + st, s

def ssd_scan(xs, dt, a_neg, bm, cm, s0, with_output):
    bsz, seqlen, nh, hp = xs.shape
    ng, ns = bm.shape[2], bm.shape[3]
    rep = nh // ng
    nc = seqlen // SSD_CHUNK
    la = (dt * a_neg).reshape(bsz, nc, SSD_CHUNK, ng, rep)
    acum = jnp.cumsum(la, axis=2)
    xdt = (xs.astype(jnp.float32) * dt[..., None]).reshape(bsz, nc, SSD_CHUNK, ng, rep, hp)
    bc = bm.astype(jnp.float32).reshape(bsz, nc, SSD_CHUNK, ng, ns)
    to_end = jnp.exp(acum[:, :, -1:] - acum)
    chunk_states = jnp.einsum("bcsgn,bcsgr,bcsgrp->bcgrpn", bc, to_end, xdt).reshape(bsz, nc, nh, hp, ns)
    chunk_decay = jnp.exp(acum[:, :, -1]).reshape(bsz, nc, nh)[..., None, None]
    s_final, s_in = lax.scan(_carry_step, s0, (jnp.moveaxis(chunk_decay, 1, 0), jnp.moveaxis(chunk_states, 1, 0)))
    if not with_output:
        return None, s_final
    s_in = jnp.moveaxis(s_in, 0, 1).reshape(bsz, nc, ng, rep, hp, ns)
    cc = cm.astype(jnp.float32).reshape(bsz, nc, SSD_CHUNK, ng, ns)
    causal = jnp.tril(jnp.ones((SSD_CHUNK, SSD_CHUNK), dtype=bool))[:, :, None, None]
    seg = acum[:, :, :, None] - acum[:, :, None, :]
    decay = jnp.exp(jnp.where(causal, seg, -jnp.inf))
    cb = jnp.einsum("bclgn,bcsgn->bclsg", cc, bc)
    y_diag = jnp.einsum("bclsg,bclsgr,bcsgrp->bclgrp", cb, decay, xdt)
    y_off = jnp.einsum("bclgn,bcgrpn,bclgr->bclgrp", cc, s_in, jnp.exp(acum))
    return (y_diag + y_off).reshape(bsz, seqlen, nh, hp), s_final

def ssd_inputs(p_state, conv_w, conv_b, dt_bias):
    b, n, _ = p_state.shape
    xbc = jax.nn.silu(dwconv(p_state[..., :SSD_CONV_DIM], conv_w, conv_b))
    xs = xbc[..., :SSD_INNER].reshape(b, n, SSD_HEADS, SSD_HEAD_DIM)
    bm = xbc[..., SSD_INNER:SSD_INNER + SSD_BC].reshape(b, n, SSD_GROUPS, SSD_STATE)
    cm = xbc[..., SSD_INNER + SSD_BC:].reshape(b, n, SSD_GROUPS, SSD_STATE)
    dt_raw = p_state[..., SSD_CONV_DIM:].astype(jnp.float32).reshape(b, n, 2, SSD_HEADS)
    dt = jax.nn.softplus(dt_raw + dt_bias.astype(jnp.float32))
    return xs, bm, cm, dt

def ssd_readout(y, xs, z, d_skip, norm_g):
    b, n = y.shape[0], y.shape[1]
    y = y + d_skip.astype(jnp.float32)[:, None] * xs.astype(jnp.float32)
    y = y.reshape(b, n, SSD_INNER) * jax.nn.silu(z.astype(jnp.float32))
    return rmsnorm_2(y, norm_g)

def conformer_conv(v, gate, dw_w, dw_b, ln_g, ln_b, rows):
    u = v * jax.nn.sigmoid(gate)
    b, n, ch = u.shape
    if rows is not None:
        u = u.reshape(b * rows, GRID_W, ch)
    u = dwconv(u, dw_w, dw_b).reshape(b, n, ch)
    return jax.nn.silu(layernorm(u, ln_g, ln_b))

def even_mixer(hc, hl, w_in, conv_w, conv_b, dt_bias, a_log, d_skip, ssd_g,
               cf_w, cf_b, cf_lng, cf_lnb, w_out, rows, need_ctx):
    a_neg = -jnp.exp(a_log.astype(jnp.float32))
    s_lo, s_hi = SSD_INNER, SSD_INNER + SSD_STATE_COLS
    pl = hl @ w_in
    if need_ctx:
        pc = hc @ w_in
        pc_state = pc[..., s_lo:s_hi]
    else:
        pc_state = hc @ w_in[:, s_lo:s_hi]
    xs_l, b_l, c_l, dt_l = ssd_inputs(pl[..., s_lo:s_hi], conv_w, conv_b, dt_bias)
    xs_c, b_c, c_c, dt_c = ssd_inputs(pc_state, conv_w, conv_b, dt_bias)
    bsz = hl.shape[0]
    ys_c, ys_l = [], []
    for d in range(2):
        flip = _flip if d else _same
        s0 = jnp.zeros((bsz, SSD_HEADS, SSD_HEAD_DIM, SSD_STATE), jnp.float32)
        y_c, s_ctx = ssd_scan(flip(xs_c), flip(dt_c[:, :, d]), a_neg[d], flip(b_c), flip(c_c), s0, need_ctx)
        y_l, _ = ssd_scan(flip(xs_l), flip(dt_l[:, :, d]), a_neg[d], flip(b_l), flip(c_l), s_ctx, True)
        ys_l.append(flip(y_l))
        if need_ctx:
            ys_c.append(flip(y_c))
    cf0 = SSD_INNER + SSD_STATE_COLS
    o_ssd = ssd_readout(ys_l[0] + ys_l[1], xs_l, pl[..., :SSD_INNER], d_skip, ssd_g)
    o_cf = conformer_conv(pl[..., cf0:cf0 + CF_CH], pl[..., cf0 + CF_CH:], cf_w, cf_b, cf_lng, cf_lnb, rows)
    y_lat = (jnp.concatenate([o_ssd, o_cf.astype(o_ssd.dtype)], axis=-1) @ w_out).astype(hl.dtype)
    y_ctx = None
    if need_ctx:
        oc_ssd = ssd_readout(ys_c[0] + ys_c[1], xs_c, pc[..., :SSD_INNER], d_skip, ssd_g)
        oc_cf = conformer_conv(pc[..., cf0:cf0 + CF_CH], pc[..., cf0 + CF_CH:], cf_w, cf_b, cf_lng, cf_lnb, None)
        y_ctx = (jnp.concatenate([oc_ssd, oc_cf.astype(oc_ssd.dtype)], axis=-1) @ w_out).astype(hc.dtype)
    return y_ctx, y_lat

def hgrn2_scan(q, k, v, logf, s0, with_output):
    bsz, seqlen, nh, dk = k.shape
    dv = v.shape[-1]
    nc = seqlen // HG_CHUNK

    def chunks(t):
        return t.astype(jnp.float32).reshape(bsz, nc, HG_CHUNK, nh, t.shape[-1])

    kc, vc = chunks(k), chunks(v)
    gcum = jnp.cumsum(chunks(logf), axis=2)
    g_end = gcum[:, :, -1]
    k_end = kc * jnp.exp(g_end[:, :, None] - gcum)
    chunk_states = jnp.einsum("bcshk,bcshv->bchkv", k_end, vc)
    s_final, s_in = lax.scan(_carry_step, s0, (jnp.moveaxis(jnp.exp(g_end)[..., None], 1, 0),
                                               jnp.moveaxis(chunk_states, 1, 0)))
    if not with_output:
        return None, s_final
    s_in = jnp.moveaxis(s_in, 0, 1)
    qc = chunks(q)
    g_mid = gcum[:, :, HG_CHUNK // 2 - 1:HG_CHUNK // 2]
    q_rel = qc * jnp.exp(gcum - g_mid)
    k_rel = kc * jnp.exp(g_mid - gcum)
    causal = jnp.tril(jnp.ones((HG_CHUNK, HG_CHUNK), dtype=bool))
    att = jnp.where(causal, jnp.einsum("bclhk,bcshk->bchls", q_rel, k_rel), 0.0)
    o_intra = jnp.einsum("bchls,bcshv->bclhv", att, vc)
    o_inter = jnp.einsum("bclhk,bchkv->bclhv", qc * jnp.exp(gcum), s_in)
    return (o_intra + o_inter).reshape(bsz, seqlen, nh, dv), s_final

def hgrn2_gates(p_state, lb):
    b, n, _ = p_state.shape
    v = p_state[..., :HG_VAL].reshape(b, n, HG_HEADS, HG_DV)
    f_raw = p_state[..., HG_VAL:].astype(jnp.float32).reshape(b, n, 2, HG_HEADS, HG_DK)
    lbh = lb.reshape(HG_HEADS, HG_DK)
    f = lbh + (1.0 - lbh) * jax.nn.sigmoid(f_raw)
    return v, 1.0 - f, jnp.log(f)

def hgrn2_readout(o, g, norm_g):
    b, n = o.shape[0], o.shape[1]
    return rmsnorm_2(o, norm_g).reshape(b, n, HG_VAL) * jax.nn.silu(g.astype(jnp.float32))

def odd_mixer(hc, hl, w_in, lb, norm_g, w_out, rows, need_ctx):
    st0 = HG_KEY + HG_VAL
    bsz, n_lat = hl.shape[0], hl.shape[1]
    pl = to_col_major(hl, rows) @ w_in
    q_l = jax.nn.silu(pl[..., :HG_KEY]).reshape(bsz, n_lat, HG_HEADS, HG_DK)
    v_l, k_l, lf_l = hgrn2_gates(pl[..., st0:], lb)
    if need_ctx:
        pc = hc @ w_in
        q_c = jax.nn.silu(pc[..., :HG_KEY]).reshape(bsz, hc.shape[1], HG_HEADS, HG_DK)
        pc_state = pc[..., st0:]
    else:
        pc_state = hc @ w_in[:, st0:]
    v_c, k_c, lf_c = hgrn2_gates(pc_state, lb)
    os_c, os_l = [], []
    for d in range(2):
        flip = _flip if d else _same
        s0 = jnp.zeros((bsz, HG_HEADS, HG_DK, HG_DV), jnp.float32)
        qc_d = flip(q_c) if need_ctx else None
        o_c, s_ctx = hgrn2_scan(qc_d, flip(k_c[:, :, d]), flip(v_c), flip(lf_c[:, :, d]), s0, need_ctx)
        o_l, _ = hgrn2_scan(flip(q_l), flip(k_l[:, :, d]), flip(v_l), flip(lf_l[:, :, d]), s_ctx, True)
        os_l.append(flip(o_l))
        if need_ctx:
            os_c.append(flip(o_c))
    y_lat = from_col_major(hgrn2_readout(os_l[0] + os_l[1], pl[..., HG_KEY:st0], norm_g) @ w_out, rows).astype(hl.dtype)
    y_ctx = None
    if need_ctx:
        y_ctx = (hgrn2_readout(os_c[0] + os_c[1], pc[..., HG_KEY:st0], norm_g) @ w_out).astype(hc.dtype)
    return y_ctx, y_lat

def moe(h, router_w, router_b, w_gate, w_up, w_down):
    shp = h.shape
    t = h.reshape(-1, D_MODEL)
    scores = jax.nn.sigmoid((t @ router_w).astype(jnp.float32))
    sel = scores + router_b.astype(jnp.float32)
    grouped = sel.reshape(-1, N_EXPERT_GROUPS, EXPERTS_PER_GROUP)
    group_score = lax.top_k(grouped, TOP_K)[0].sum(-1)
    g_idx = jnp.argmax(group_score, axis=-1)
    idx = jnp.broadcast_to(g_idx[:, None, None], (t.shape[0], 1, EXPERTS_PER_GROUP))
    in_group = jnp.take_along_axis(grouped, idx, axis=1)[:, 0]
    _, local = lax.top_k(in_group, TOP_K)
    expert_idx = g_idx[:, None] * EXPERTS_PER_GROUP + local
    wts = jnp.take_along_axis(scores, expert_idx, axis=1)
    wts = wts / jnp.sum(wts, axis=-1, keepdims=True)
    combine = jnp.sum(jax.nn.one_hot(expert_idx, N_EXPERTS, dtype=jnp.float32) * wts[..., None], axis=1)

    def expert(acc, p):
        wg, wu, wd, gate_col = p
        y = (jax.nn.silu(t @ wg) * (t @ wu)) @ wd
        return acc + gate_col[:, None] * y, None

    out, _ = lax.scan(expert, jnp.zeros(t.shape, jnp.float32), (w_gate, w_up, w_down, combine.T))
    return out.reshape(shp).astype(h.dtype)

def second_inputs(seed: int = 0) -> dict:
    key = jax.random.key(seed)
    ks = jax.random.split(key, 32)
    f32 = jnp.float32

    def dense(k, shape, fan_in, scale=1.0):
        return scale * fan_in ** -0.5 * jax.random.normal(k, shape, f32)

    def gain(k, shape):
        return 1.0 + 0.1 * jax.random.normal(k, shape, f32)

    def small(k, shape, s=0.02):
        return s * jax.random.normal(k, shape, f32)

    dt0 = jnp.exp(jax.random.uniform(ks[14], (N_EVEN, 2, SSD_HEADS), f32, np.log(1e-3), np.log(1e-1)))
    return {
        "x": jax.random.normal(ks[0], (BATCH, SEQ, D_MODEL), f32),
        "c": jax.random.normal(ks[1], (BATCH, D_MODEL), f32),
        "ctx": jax.random.normal(ks[2], (BATCH, CTX_LEN, D_MODEL), f32),
        "c_ctx": jax.random.normal(ks[3], (D_MODEL,), f32),
        "mod_w": dense(ks[4], (DEPTH, D_MODEL, N_MOD * D_MODEL), D_MODEL, 0.5),
        "mod_b": small(ks[5], (DEPTH, N_MOD * D_MODEL)),
        "norm_mix_g": gain(ks[6], (DEPTH, D_MODEL)),
        "norm_ffn_g": gain(ks[7], (DEPTH, D_MODEL)),
        "router_w": dense(ks[8], (D_MODEL, N_EXPERTS), D_MODEL),
        "router_b": small(ks[9], (N_EXPERTS,), 0.01),
        "moe_w_gate": dense(ks[10], (DEPTH, N_EXPERTS, D_MODEL, D_EXPERT), D_MODEL),
        "moe_w_up": dense(ks[11], (DEPTH, N_EXPERTS, D_MODEL, D_EXPERT), D_MODEL),
        "moe_w_down": dense(ks[12], (DEPTH, N_EXPERTS, D_EXPERT, D_MODEL), D_EXPERT),
        "ab_w_in": dense(ks[13], (N_EVEN, D_MODEL, AB_IN), D_MODEL),
        "ssd_conv_w": dense(ks[15], (N_EVEN, SSD_CONV, SSD_CONV_DIM), SSD_CONV),
        "ssd_conv_b": small(ks[16], (N_EVEN, SSD_CONV_DIM)),
        "ssd_dt_bias": dt0 + jnp.log(-jnp.expm1(-dt0)),
        "ssd_a_log": jnp.log(jax.random.uniform(ks[17], (N_EVEN, 2, SSD_HEADS), f32, 1.0, 16.0)),
        "ssd_d": gain(ks[18], (N_EVEN, SSD_HEADS)),
        "ssd_norm_g": gain(ks[19], (N_EVEN, SSD_INNER)),
        "cf_dw_w": dense(ks[20], (N_EVEN, CF_KERNEL, CF_CH), CF_KERNEL),
        "cf_dw_b": small(ks[21], (N_EVEN, CF_CH)),
        "cf_ln_g": gain(ks[22], (N_EVEN, CF_CH)),
        "cf_ln_b": small(ks[23], (N_EVEN, CF_CH)),
        "ab_w_out": dense(ks[24], (N_EVEN, AB_OUT, D_MODEL), AB_OUT),
        "hg_w_in": dense(ks[25], (N_ODD, D_MODEL, HG_IN), D_MODEL),
        "hg_lb": small(ks[26], (DEPTH, HG_KEY), 0.1),
        "hg_norm_g": gain(ks[27], (N_ODD, HG_DV)),
        "hg_w_out": dense(ks[28], (N_ODD, HG_VAL, D_MODEL), HG_VAL),
        "final_norm_g": gain(ks[29], (D_MODEL,)),
    }

def second_block(x, c, ctx, c_ctx, mod_w, mod_b, norm_mix_g, norm_ffn_g, router_w, router_b,
              moe_w_gate, moe_w_up, moe_w_down, ab_w_in, ssd_conv_w, ssd_conv_b, ssd_dt_bias,
              ssd_a_log, ssd_d, ssd_norm_g, cf_dw_w, cf_dw_b, cf_ln_g, cf_ln_b, ab_w_out,
              hg_w_in, hg_lb, hg_norm_g, hg_w_out, final_norm_g):
    rows = x.shape[1] // GRID_W
    lb_all = jnp.cumsum(jax.nn.softmax(hg_lb.astype(jnp.float32), axis=0), axis=0)
    lb_all = lb_all - lb_all[0]
    xl, xc = x, ctx
    for l in range(DEPTH):
        last = l == DEPTH - 1
        j = l // 2
        m_l = modulation(c, mod_w[l], mod_b[l])[:, :, None, :]
        m_c = modulation(c_ctx, mod_w[l], mod_b[l])
        hl = rmsnorm_2(xl, norm_mix_g[l]) * (1.0 + m_l[:, 1]) + m_l[:, 0]
        hc = rmsnorm_2(xc, norm_mix_g[l]) * (1.0 + m_c[1]) + m_c[0]
        if l % 2 == 0:
            y_c, y_l = even_mixer(hc, hl, ab_w_in[j], ssd_conv_w[j], ssd_conv_b[j], ssd_dt_bias[j],
                                  ssd_a_log[j], ssd_d[j], ssd_norm_g[j], cf_dw_w[j], cf_dw_b[j],
                                  cf_ln_g[j], cf_ln_b[j], ab_w_out[j], rows, not last)
        else:
            y_c, y_l = odd_mixer(hc, hl, hg_w_in[j], lb_all[l], hg_norm_g[j], hg_w_out[j], rows, not last)
        xl = xl + m_l[:, 2] * y_l
        hl = rmsnorm_2(xl, norm_ffn_g[l]) * (1.0 + m_l[:, 4]) + m_l[:, 3]
        xl = xl + m_l[:, 5] * moe(hl, router_w, router_b, moe_w_gate[l], moe_w_up[l], moe_w_down[l])
        if not last:
            xc = xc + m_c[2] * y_c
            hc = rmsnorm_2(xc, norm_ffn_g[l]) * (1.0 + m_c[4]) + m_c[3]
            xc = xc + m_c[5] * moe(hc, router_w, router_b, moe_w_gate[l], moe_w_up[l], moe_w_down[l])
    return rmsnorm_2(xl, final_norm_g)


def setup_inputs(seed=0):
    out = dict(first_inputs(seed))
    for name, value in second_inputs(seed + 1).items():
        if name != "x":
            out[name + "_2"] = value
    return out


def reference(
    x, p, positions, norm_mix, pool_w, pool_scale, norm_kv, w_kv, cmp_pos_k, cmp_w1_k, cmp_w2_k,
    cmp_pos_v, cmp_w1_v, cmp_w2_v, w_in_b, w_out_b, norm_ffn, ffn_up, ffn_conv, ffn_conv_b,
    ffn_down, norm_ple, ple_gate, ple_proj, norm_final, c_2, ctx_2, c_ctx_2, mod_w_2, mod_b_2,
    norm_mix_g_2, norm_ffn_g_2, router_w_2, router_b_2, moe_w_gate_2, moe_w_up_2, moe_w_down_2,
    ab_w_in_2, ssd_conv_w_2, ssd_conv_b_2, ssd_dt_bias_2, ssd_a_log_2, ssd_d_2, ssd_norm_g_2,
    cf_dw_w_2, cf_dw_b_2, cf_ln_g_2, cf_ln_b_2, ab_w_out_2, hg_w_in_2, hg_lb_2, hg_norm_g_2,
    hg_w_out_2, final_norm_g_2,
):
    x = first_block(
        x, p, positions, norm_mix, pool_w, pool_scale, norm_kv, w_kv, cmp_pos_k, cmp_w1_k,
        cmp_w2_k, cmp_pos_v, cmp_w1_v, cmp_w2_v, w_in_b, w_out_b, norm_ffn, ffn_up, ffn_conv,
        ffn_conv_b, ffn_down, norm_ple, ple_gate, ple_proj, norm_final,
    )
    return second_block(
        x, c_2, ctx_2, c_ctx_2, mod_w_2, mod_b_2, norm_mix_g_2, norm_ffn_g_2, router_w_2,
        router_b_2, moe_w_gate_2, moe_w_up_2, moe_w_down_2, ab_w_in_2, ssd_conv_w_2,
        ssd_conv_b_2, ssd_dt_bias_2, ssd_a_log_2, ssd_d_2, ssd_norm_g_2, cf_dw_w_2, cf_dw_b_2,
        cf_ln_g_2, cf_ln_b_2, ab_w_out_2, hg_w_in_2, hg_lb_2, hg_norm_g_2, hg_w_out_2,
        final_norm_g_2,
    )


_drawn_inputs = setup_inputs


def setup_inputs(seed=0):
    import zlib

    import numpy as np

    out = dict(_drawn_inputs(seed))
    spreads = {}
    factors = {'cmp_pos_k': 4.206,
     'cf_dw_b_2': 3.074,
     'cf_ln_b_2': 3.688,
     'hg_lb_2': 19.452,
     'norm_kv': 2.987,
     'ssd_conv_b_2': 3.086}
    for name, (base, spread) in spreads.items():
        noise = np.random.default_rng([zlib.crc32(name.encode()), seed]).standard_normal(out[name].shape)
        drawn = base * np.exp(spread * noise) if base else spread * noise
        out[name] = jnp.asarray(drawn.astype(out[name].dtype))
    for name, factor in factors.items():
        out[name] = (out[name] * factor).astype(out[name].dtype)
    return out
```

```python
from contextlib import ExitStack, contextmanager

import numpy as np

import concourse.bass as bass
from concourse import mybir

F32 = mybir.dt.float32
I32 = mybir.dt.int32
U8 = mybir.dt.uint8
ALU = mybir.AluOpType
ACT = mybir.ActivationFunctionType
AX = mybir.AxisListType

P = 128
D = 1024
KD = D // P
T = 256
T2 = 2 * T
EPS = 1e-6
NEG = -1e30

RING = 12
TILES = 8

WINDOWS = (2, 4, 8, 16)
MAXWIN = max(WINDOWS)
HEADS, HD, GROUPS = 16, 64, 4
HPG = HEADS // GROUPS
ROT = HD // 4
CMP_STRIDE, CMP_LEN = 16, 32
NCMP = T // CMP_STRIDE - 1
DFF = 2816
KF = DFF // P
PLE = 256
PAIRS_PER_ROUND = RING // 2


@contextmanager
def stage_semaphores(nc, stage, *names):
    sems = [nc.alloc_semaphore(f"{stage}_{n}") for n in names]
    yield sems
    nc.clear_and_free_semaphores(sems)
    nc.all_engine_barrier(sem_only=True)


class Kit:

    def __init__(self, nc, ctx, weights, n_slots):
        self.nc, self.ctx = nc, ctx
        self.weights, self.n_slots = weights, n_slots
        self.next_slot = 0
        self.ring = self.sb("ring", [P, RING, TILES, P])
        self.ps = ctx.enter_context(nc.psum_tensor("ps", [P, 8, 512], F32))
        self.landed = [ctx.enter_context(nc.semaphore(f"slot_landed{i}")) for i in range(RING)]

    def sb(self, name, shape, dtype=F32):
        return self.ctx.enter_context(self.nc.sbuf_tensor(name, shape, dtype))

    def take(self, n):
        first = self.next_slot
        self.next_slot += n
        return first

    def prefill(self, sp):
        for n in range(RING):
            sp.dma_start(self.ring[:, n], self.weights[n]).then_inc(self.landed[n], 16)

    def refill(self, sp, first, count, used, per=1, mult=1, base=0):
        count = max(0, min(count, self.n_slots - RING - first))
        rounds = count // RING

        def one(s, i):
            n = first + s
            at = n % RING
            sp.wait_ge(used, i * (RING // per * mult) + base + (s // per + 1) * mult)
            sp.dma_start(self.ring[:, at], self.weights[n + RING + i * RING]).then_inc(self.landed[at], 16)

        if rounds > 1:
            with sp.Fori(0, rounds) as i:
                for s in range(RING):
                    one(s, i)
        else:
            rounds = 0
        for s in range(rounds * RING, count):
            one(s, 0)

    def slot(self, pe, n, i=0):
        at = n % RING
        pe.wait_ge(self.landed[at], 16 * (n // RING + 1) + i * 16)
        return self.ring[:, at]


def rounds_then_rest(engine, steps, per_round, body):
    whole = steps // per_round
    if whole > 1:
        with engine.Fori(0, whole) as i:
            for j in range(per_round):
                body(i * per_round + j, j, i)
    else:
        whole = 0
    for n in range(whole * per_round, steps):
        body(n, n, 0)


NORM_SEMS = ("squared", "summed", "rooted", "normed")
NORM_BANK = 7


def norm_scalar(k, act, sems, x, n):
    squared, summed, rooted, _ = sems
    for t in range(KD):
        act.activation(k.sq[:, t, 0:n], x[:, t, :], ACT.Square).then_inc(squared, 1)
    act.wait_ge(summed, 1)
    act.activation(k.root[:, 0:n], k.ps[:, NORM_BANK, 0:n], ACT.Sqrt, scale=1.0 / D, bias=k.eps[:, 0:1]).then_inc(rooted, 1)


def norm_tensor(k, pe, sems, n):
    squared, summed, _, _ = sems
    for t in range(KD):
        pe.wait_ge(squared, t + 1)
        mm = pe.matmul(k.ps[:, NORM_BANK, 0:n], k.ones[:, :], k.sq[:, t, 0:n], start=(t == 0), stop=(t == KD - 1))
    mm.then_inc(summed, 1)


def norm_vector(k, dve, sems, x, h, gain, n):
    _, _, rooted, normed = sems
    dve.wait_ge(rooted, 1)
    dve.reciprocal(k.rstd[:, 0:n], k.root[:, 0:n])
    dve.drain()
    for t in range(KD):
        dve.scalar_tensor_tensor(h[:, t, :], x[:, t, :], gain[:, t:t + 1], k.rstd[:, 0:n],
                                 ALU.mult, ALU.mult).then_inc(normed, 1)


def constants(k, loads):
    nc = k.nc
    k.ones = k.sb("ones", [P, P])
    k.ident = k.sb("ident", [P, P])
    k.eps = k.sb("eps", [P, 1])
    k.sq = k.sb("sq", [P, KD, T2])
    k.root = k.sb("root", [P, T2])
    k.rstd = k.sb("rstd", [P, T2])
    k.h = k.sb("h", [P, KD, T2])
    with stage_semaphores(nc, "constants", "loaded", "cleared") as (loaded, cleared), nc.Block(name="constants") as block:

        @block.sync
        def _(sp):
            for to, of in loads:
                sp.dma_start(to, of).then_inc(loaded, 16)
            k.prefill(sp)
            sp.wait_ge(loaded, 16 * len(loads))

        @block.gpsimd
        def _(pool):
            pool.memset(k.ones[:, :], 1.0)
            pool.memset(k.eps[:, :], EPS)
            pool.memset(k.ident[:, :], 0.0).then_inc(cleared, 1)
            pool.wait_ge(cleared, 1)
            pool.affine_select(out=k.ident[:, :], in_=k.ident[:, :], compare_op=ALU.not_equal, fill=1.0,
                               base=0, pattern=[[-1, P]], channel_multiplier=1)


def pool_mixer(k, x, gain, scale, rcount_in):
    nc = k.nc
    first = k.take(2)
    with ExitStack() as local:
        hp = local.enter_context(nc.sbuf_tensor("pool_h", [P, KD, MAXWIN + T], F32))
        wa = local.enter_context(nc.sbuf_tensor("pool_wa", [P, KD, MAXWIN + T], F32))
        wb = local.enter_context(nc.sbuf_tensor("pool_wb", [P, KD, MAXWIN + T], F32))
        u = local.enter_context(nc.sbuf_tensor("pool_u", [P, KD, T], F32))
        rcount = local.enter_context(nc.sbuf_tensor("pool_rcount", [P, len(WINDOWS), T], F32))
        with stage_semaphores(nc, "pool", *NORM_SEMS, "loaded", "u_ready", "mixed") as sems, \
                nc.Block(name="pool_mixer", no_gpsimd_drain=True) as block:
            norm, (loaded, u_ready, mixed) = sems[:4], sems[4:]

            @block.sync
            def _(sp):
                sp.dma_start(rcount[:, :, :], rcount_in).then_inc(loaded, 16)
                k.refill(sp, first, 2, mixed, mult=4)

            @block.scalar
            def _(act):
                norm_scalar(k, act, norm, x, T)

            @block.vector
            def _(dve):
                for b in (hp, wa, wb):
                    dve.memset(b[:, :, 0:MAXWIN], 0.0)
                norm_vector(k, dve, norm, x, hp[:, :, MAXWIN:], gain, T)
                dve.drain()
                dve.wait_ge(loaded, 16)
                src, gt = hp, KD // len(WINDOWS)
                for gi, w in enumerate(WINDOWS):
                    dst, t0 = (wa, wb)[gi % 2], gi * gt
                    dve.tensor_tensor(dst[:, t0:, MAXWIN:], src[:, t0:, MAXWIN:],
                                      src[:, t0:, MAXWIN - w // 2:MAXWIN - w // 2 + T], ALU.add)
                    dve.drain()
                    dve.tensor_tensor(u[:, t0:t0 + gt, :], dst[:, t0:t0 + gt, MAXWIN:],
                                      rcount[:, gi, :].unsqueeze(1).broadcast_to([P, gt, T]), ALU.mult)
                    dve.drain()
                    dve.tensor_tensor(u[:, t0:t0 + gt, :], u[:, t0:t0 + gt, :], hp[:, t0:t0 + gt, MAXWIN:],
                                      ALU.subtract).then_inc(u_ready, 1)
                    src = dst
                for m in range(KD):
                    dve.wait_ge(mixed, m + 1)
                    dve.scalar_tensor_tensor(x[:, m, :], k.ps[:, m, 0:T], scale[:, m:m + 1],
                                             x[:, m, :], ALU.mult, ALU.add)

            @block.tensor
            def _(pe):
                norm_tensor(k, pe, norm, T)
                for s in range(2):
                    w = k.slot(pe, first + s)
                    for gg in range(2):
                        pe.wait_ge(u_ready, 2 * s + gg + 1)
                        for m in range(2):
                            mt = 4 * s + 2 * gg + m
                            for c in range(2):
                                mm = pe.matmul(k.ps[:, mt, 0:T], w[:, 4 * gg + 2 * m + c, :],
                                               u[:, 4 * s + 2 * gg + c, :], start=(c == 0), stop=(c == 1))
                            mm.then_inc(mixed, 1)


def conv_ffn(k, x, gain, taps, name):
    nc = k.nc
    up, down = k.take(2 * KF), k.take(KF)
    YB = 2
    with ExitStack() as local:
        hid = local.enter_context(nc.sbuf_tensor(f"{name}_hid", [P, KF, T], F32))
        y = local.enter_context(nc.sbuf_tensor(f"{name}_y", [P, YB, 2, T], F32))
        with stage_semaphores(nc, name, *NORM_SEMS, "product", "based", "conved", "gated", "hidden", "slot_used",
                              "summed_down") as sems, nc.Block(name=name, no_gpsimd_drain=True) as block:
            norm, (product, based, conved, gated, hidden, slot_used, down_done) = sems[:4], sems[4:]

            @block.sync
            def _(sp):
                k.refill(sp, up, 2 * KF, product, per=2)
                k.refill(sp, down, KF - 1, slot_used)
                k.refill(sp, down + KF - 1, 1, down_done, mult=KD)

            @block.tensor
            def _(pe):
                norm_tensor(k, pe, norm, T)
                pe.wait_ge(normed := norm[3], KD)

                def pair(p, j, i):
                    pe.wait_ge(conved, p + 1)
                    for half in range(2):
                        w = k.slot(pe, up + 2 * j + half, i)
                        for t in range(KD):
                            mm = pe.matmul(k.ps[:, j % 2, half * T:(half + 1) * T], w[:, t, :], k.h[:, t, 0:T],
                                           start=(t == 0), stop=(t == KD - 1))
                    mm.then_inc(product, 1)

                rounds_then_rest(pe, KF, PAIRS_PER_ROUND, pair)
                pe.wait_ge(conved, KF + YB)
                for c in range(KF):
                    w = k.slot(pe, down + c)
                    pe.wait_ge(hidden, c + 1 + YB)
                    for m in range(KD):
                        mm = pe.matmul(k.ps[:, m, 0:T], w[:, m, :], hid[:, c, :], start=(c == 0), stop=(c == KF - 1))
                        if c == KF - 1:
                            mm.then_inc(down_done, 1)
                    if c < KF - 1:
                        mm.then_inc(slot_used, 1)

            @block.scalar
            def _(act):
                norm_scalar(k, act, norm, x, T)

                def pair(p, j, i):
                    act.wait_ge(product, p + 1)
                    act.wait_ge(hidden, p + 1)
                    for half in range(2):
                        act.activation(y[:, j % YB, half], k.ps[:, j % 2, half * T:(half + 1) * T], ACT.Identity,
                                       scale=taps[:, bass.ds(p + half * KF, 1), 2], bias=taps[:, bass.ds(p + half * KF, 1), 3]
                                       ).then_inc(based, 1)
                    act.wait_ge(conved, p + 1 + YB)
                    act.activation(y[:, j % YB, 1], y[:, j % YB, 1], ACT.Silu).then_inc(gated, 1)

                rounds_then_rest(act, KF, PAIRS_PER_ROUND, pair)

            @block.vector
            def _(dve):
                norm_vector(k, dve, norm, x, k.h[:, :, 0:T], gain, T)
                dve.sem_inc(conved, YB)
                dve.sem_inc(hidden, YB)

                def pair(p, j, i):
                    dve.wait_ge(based, 2 * p + 2)
                    for back in (1, 2):
                        for half in range(2):
                            st = dve.scalar_tensor_tensor(
                                y[:, j % YB, half, back:], k.ps[:, j % 2, half * T:(half + 1) * T - back],
                                taps[:, bass.ds(p + half * KF, 1), 2 - back], y[:, j % YB, half, back:], ALU.mult, ALU.add)
                        if back == 1:
                            dve.drain()
                    st.then_inc(conved, 1)
                    dve.wait_ge(gated, p + 1)
                    dve.tensor_tensor(hid[:, p], y[:, j % YB, 0], y[:, j % YB, 1], ALU.mult
                                      ).then_inc(hidden, 1)

                rounds_then_rest(dve, KF, PAIRS_PER_ROUND, pair)
                for m in range(KD):
                    dve.wait_ge(down_done, m + 1)
                    dve.tensor_tensor(x[:, m, :], k.ps[:, m, 0:T], x[:, m, :], ALU.add)


def ple(k, x, gain, p_in, name):
    nc = k.nc
    KP = PLE // P
    proj_slots, gate_slots = k.take(2), k.take(KD)
    with ExitStack() as local:
        pt = local.enter_context(nc.sbuf_tensor(f"{name}_p", [P, KP, T], F32))
        proj = local.enter_context(nc.sbuf_tensor(f"{name}_proj", [P, KD, T], F32))
        gate = local.enter_context(nc.sbuf_tensor(f"{name}_gate", [P, 2, T], F32))
        with stage_semaphores(nc, name, *NORM_SEMS, "loaded", "projected", "kept", "product", "gated", "applied") as sems, \
                nc.Block(name=name, no_gpsimd_drain=True) as block:
            norm, (loaded, projected, kept, product, gated, applied) = sems[:4], sems[4:]

            @block.sync
            def _(sp):
                sp.dma_start(pt[:, :, :], p_in).then_inc(loaded, 16)
                k.refill(sp, proj_slots, 2, projected, mult=4)
                k.refill(sp, gate_slots, KD, product)

            @block.tensor
            def _(pe):
                pe.wait_ge(loaded, 16)
                for m in range(KD):
                    w = k.slot(pe, proj_slots + m // 4)
                    for c in range(KP):
                        mm = pe.matmul(k.ps[:, m // 2, m % 2 * T:(m % 2 + 1) * T], w[:, m % 4 * 2 + c, :], pt[:, c, :],
                                       start=(c == 0), stop=(c == KP - 1))
                    mm.then_inc(projected, 1)
                norm_tensor(k, pe, norm, T)
                pe.wait_ge(norm[3], KD)
                for m in range(KD):
                    if m >= 2:
                        pe.wait_ge(gated, m - 1)
                    w = k.slot(pe, gate_slots + m)
                    for t in range(KD):
                        mm = pe.matmul(k.ps[:, 4 + m % 2, 0:T], w[:, t, :], k.h[:, t, 0:T], start=(t == 0), stop=(t == KD - 1))
                    mm.then_inc(product, 1)

            @block.scalar
            def _(act):
                norm_scalar(k, act, norm, x, T)
                act.wait_ge(projected, KD)
                for m in range(KD):
                    act.activation(proj[:, m, :], k.ps[:, m // 2, m % 2 * T:(m % 2 + 1) * T], ACT.Copy).then_inc(kept, 1)
                for m in range(KD):
                    act.wait_ge(product, m + 1)
                    if m >= 2:
                        act.wait_ge(applied, m - 1)
                    act.activation(gate[:, m % 2, :], k.ps[:, 4 + m % 2, 0:T], ACT.Sigmoid).then_inc(gated, 1)

            @block.vector
            def _(dve):
                norm_vector(k, dve, norm, x, k.h[:, :, 0:T], gain, T)
                for m in range(KD):
                    dve.wait_ge(gated, m + 1)
                    dve.wait_ge(kept, m + 1)
                    dve.tensor_tensor(proj[:, m, :], proj[:, m, :], gate[:, m % 2, :], ALU.mult).then_inc(applied, 1)
                    dve.drain()
                    dve.tensor_tensor(x[:, m, :], x[:, m, :], proj[:, m, :], ALU.add)


def nsa(k, x, gain_kv, gain_q, pos, inv_freq, turn, gate_w_in, cmp_w1_in, cmp_small_in, masks_in):
    nc = k.nc
    kv_slots, v_slots, q_slots, o_slots = k.take(8), k.take(4), k.take(8), k.take(8)
    QT = T // P
    local = ExitStack()
    with local:
        def sb(name, shape, dtype=F32):
            return local.enter_context(nc.sbuf_tensor(name, shape, dtype))

        hq = sb("hq", [P, KD, T])
        q = sb("q", [HD, HEADS, T])
        kt = sb("kt", [HD, 4, GROUPS, T])
        v = sb("v", [P, QT, 2, GROUPS, HD])
        gate_w = sb("gate_w", [P, KD, 3 * HEADS])
        gates = sb("gates", [P, QT, HEADS, 3])
        cs = sb("cs", [ROT, 2, T])
        kc = sb("kc", [HD, GROUPS, NCMP])
        vc = sb("vc", [NCMP, GROUPS, HD])
        attn = sb("attn", [P, KD, T])

        with ExitStack() as tmp:
            ang = tmp.enter_context(nc.sbuf_tensor("ang", [ROT, 4, T], F32))
            posf = tmp.enter_context(nc.sbuf_tensor("posi", [ROT, T], I32))
            with stage_semaphores(nc, "qkv", *NORM_SEMS, "loaded", "q_normed", "product", "kept", "angled", "v_used") as sems, \
                    nc.Block(name="qkv", no_gpsimd_drain=True) as block:
                norm, (loaded, q_normed, product, kept, angled, v_used) = sems[:4], sems[4:]
                NB = 4

                @block.sync
                def _(sp):
                    sp.dma_start(gate_w[:, :, :], gate_w_in).then_inc(loaded, 16)
                    sp.dma_start(posf[:, :], pos).then_inc(loaded, 16)
                    k.refill(sp, kv_slots, 8, product)
                    k.refill(sp, v_slots, 3, v_used)
                    k.refill(sp, v_slots + 3, 1, product, mult=QT, base=8)
                    k.refill(sp, q_slots, 8, product, base=8 + QT)

                @block.tensor
                def _(pe):
                    norm_tensor(k, pe, norm, T)
                    pe.wait_ge(norm[3], KD)
                    for m in range(8):
                        if m >= NB:
                            pe.wait_ge(kept, m - NB + 1)
                        w = k.slot(pe, kv_slots + m)
                        for t in range(KD):
                            mm = pe.matmul(k.ps[:, m % NB, 0:T], w[:, t, :], k.h[:, t, 0:T], start=(t == 0), stop=(t == KD - 1))
                        mm.then_inc(product, 1)
                    for s in range(4):
                        w = k.slot(pe, v_slots + s).rearrange("p (a b) c -> p a (b c)", a=2)
                        for a in range(2):
                            for tok in range(QT):
                                mm = pe.matmul(k.ps[:, 4 + tok, :], k.h[:, 2 * s + a, tok * P:(tok + 1) * P], w[:, a, :],
                                               start=(s + a == 0), stop=(s + a == 4))
                                if s + a == 4:
                                    mm.then_inc(product, 1)
                        if s < 3:
                            mm.then_inc(v_used, 1)
                    pe.wait_ge(q_normed, KD)
                    for m in range(8):
                        pe.wait_ge(kept, 8 - NB + m + 1)
                        w = k.slot(pe, q_slots + m)
                        for t in range(KD):
                            mm = pe.matmul(k.ps[:, m % NB, 0:T], w[:, t, :], hq[:, t, :], start=(t == 0), stop=(t == KD - 1))
                        mm.then_inc(product, 1)
                    pe.wait_ge(loaded, 32)
                    for tok in range(QT):
                        for t in range(KD):
                            mm = pe.matmul(k.ps[:, 6, tok * 64:tok * 64 + 3 * HEADS], hq[:, t, tok * P:(tok + 1) * P],
                                           gate_w[:, t, :], start=(t == 0), stop=(t == KD - 1))
                        mm.then_inc(product, 1)

                @block.scalar
                def _(act):
                    norm_scalar(k, act, norm, x, T)
                    for m in range(8):
                        act.wait_ge(product, m + 1)
                        for half in range(2):
                            cp = act.activation(kt[:, m // 2, m % 2 * 2 + half, :], k.ps[half * HD:(half + 1) * HD, m % NB, 0:T],
                                                ACT.Copy)
                        cp.then_inc(kept, 1)
                    act.wait_ge(product, 10)
                    for tok in range(QT):
                        act.activation(v[:, tok].rearrange("p a g d -> p (a g d)"), k.ps[:, 4 + tok, :], ACT.Copy)
                    for m in range(8):
                        act.wait_ge(product, 11 + m)
                        for half in range(2):
                            cp = act.activation(q[:, 2 * m + half, :], k.ps[half * HD:(half + 1) * HD, m % NB, 0:T], ACT.Copy)
                        cp.then_inc(kept, 1)
                    act.wait_ge(product, 20)
                    for tok in range(QT):
                        act.activation(gates[:, tok].rearrange("p h b -> p (h b)"), k.ps[:, 6, tok * 64:tok * 64 + 3 * HEADS],
                                       ACT.Sigmoid)
                    act.wait_ge(angled, 2)
                    act.activation(cs[:, :, :], ang[:, 0:2, :], ACT.Sin)

                @block.vector
                def _(dve):
                    norm_vector(k, dve, norm, x, k.h[:, :, 0:T], gain_kv, T)
                    for t in range(KD):
                        dve.scalar_tensor_tensor(hq[:, t, :], x[:, t, :], gain_q[:, t:t + 1], k.rstd[:, 0:T],
                                                 ALU.mult, ALU.mult).then_inc(q_normed, 1)
                    two_pi = 2.0 * np.pi
                    c1 = 6.28125
                    c2 = float(np.float32(np.floor((two_pi - c1) * 2.0 ** 20) / 2.0 ** 20))
                    c3 = two_pi - c1 - c2
                    magic = 1.5 * 2.0 ** 23
                    dve.wait_ge(loaded, 32)
                    dve.tensor_copy(ang[:, 2, :], posf[:, :])
                    dve.drain()
                    dve.tensor_scalar(ang[:, 2, :], ang[:, 2, :], inv_freq[0:ROT, 0:1], None, ALU.mult)
                    dve.drain()
                    for part, quarter in ((0, 0.25), (1, 0.0)):
                        turns, r = ang[:, 3, :], ang[:, part, :]
                        dve.tensor_scalar(turns, ang[:, 2, :], 1.0 / two_pi, quarter, ALU.mult, ALU.add)
                        dve.drain()
                        dve.tensor_scalar(turns, turns, magic, None, ALU.add)
                        dve.drain()
                        dve.tensor_scalar(turns, turns, magic, None, ALU.subtract)
                        dve.drain()
                        dve.scalar_tensor_tensor(r, turns, -c1, ang[:, 2, :], ALU.mult, ALU.add)
                        dve.drain()
                        for c in (c2, c3):
                            dve.scalar_tensor_tensor(r, turns, -c, r, ALU.mult, ALU.add)
                            dve.drain()
                        pi = 3.141592
                        dve.tensor_scalar(r, r, quarter * two_pi, pi, ALU.add, ALU.min)
                        dve.drain()
                        dve.tensor_scalar(r, r, -pi, None, ALU.max).then_inc(angled, 1)

        with ExitStack() as tmp:
            w1 = tmp.enter_context(nc.sbuf_tensor("cmp_w1", [HD, 2, CMP_LEN, P], F32))
            small = tmp.enter_context(nc.sbuf_tensor("cmp_small", [P, 2 * HD + 2 * CMP_LEN], F32))
            bias = tmp.enter_context(nc.sbuf_tensor("cmp_bias", [P, 2], F32))
            hidc = tmp.enter_context(nc.sbuf_tensor("cmp_hid", [P, 2, GROUPS * NCMP], F32))
            turned = tmp.enter_context(nc.sbuf_tensor("turned", [ROT, 2, 2, T], F32))
            NR = 12
            with stage_semaphores(nc, "rope", "loaded", "crossed", "turned", "biased", "bias_kept", "hidden", "activated",
                                  "kc_made", "vc_made", "kc_kept", "kc_crossed") as sems, \
                    nc.Block(name="rope_compress", no_gpsimd_drain=True) as block:
                loaded, crossed, turned_s, biased, bias_kept, hidden, activated, kc_made, vc_made, kc_kept, kc_crossed = sems

                def rot_rows(n):
                    if n < 8:
                        return q[0:ROT, 2 * n:2 * n + 2, :]
                    return kt[0:ROT, 2 + (n - 8) // 2, (n - 8) % 2 * 2:(n - 8) % 2 * 2 + 2, :]

                @block.sync
                def _(sp):
                    sp.dma_start(w1[:, :, :, :], cmp_w1_in).then_inc(loaded, 16)
                    sp.dma_start(small[:, :], cmp_small_in).then_inc(loaded, 16)

                @block.tensor
                def _(pe):
                    for n in range(NR):
                        if n >= 2:
                            pe.wait_ge(turned_s, n - 1)
                        pe.matmul(k.ps[0:ROT, n % 2, :], turn[0:ROT, 0:ROT], rot_rows(n), start=True, stop=True
                                  ).then_inc(crossed, 1)
                    pe.wait_ge(loaded, 32)
                    for a in range(2):
                        blocks = kt[:, a].rearrange("p g (c s) -> p g c s", s=CMP_STRIDE)
                        for l in range(CMP_LEN):
                            c0, s0 = l // CMP_STRIDE, l % CMP_STRIDE
                            mm = pe.matmul(k.ps[:, 2 + a, 0:GROUPS * NCMP], w1[:, a, l, :], blocks[:, :, c0:c0 + NCMP, s0],
                                           start=(l == 0), stop=(l == CMP_LEN - 1))
                        mm.then_inc(hidden, 1)
                        for l in range(CMP_LEN):
                            mm = pe.matmul(k.ps[:, 4 + a, 0:1], w1[:, a, l, :],
                                           small[0:HD, 2 * HD + a * CMP_LEN + l:2 * HD + a * CMP_LEN + l + 1],
                                           start=(l == 0), stop=(l == CMP_LEN - 1))
                        mm.then_inc(biased, 1)
                    pe.wait_ge(activated, 1)
                    pe.matmul(k.ps[0:HD, 6, 0:GROUPS * NCMP], small[:, 0:HD], hidc[:, 0, :], start=True, stop=True
                              ).then_inc(kc_made, 1)
                    pe.wait_ge(activated, 2)
                    for g in range(GROUPS):
                        mm = pe.matmul(k.ps[0:NCMP, 7, g * HD:(g + 1) * HD], hidc[:, 1, g * NCMP:(g + 1) * NCMP],
                                       small[:, HD:2 * HD], start=True, stop=True)
                    mm.then_inc(vc_made, 1)
                    pe.wait_ge(kc_kept, 1)
                    pe.matmul(k.ps[0:ROT, 5, 0:GROUPS * NCMP], turn[0:ROT, 0:ROT], kc[0:ROT].rearrange("p g c -> p (g c)"),
                              start=True, stop=True).then_inc(kc_crossed, 1)

                @block.scalar
                def _(act):
                    for a in range(2):
                        act.wait_ge(biased, a + 1)
                        act.wait_ge(hidden, a + 1)
                        act.activation(bias[:, a:a + 1], k.ps[:, 4 + a, 0:1], ACT.Copy).then_inc(bias_kept, 1)
                        act.drain()
                        act.activation(hidc[:, a, :], k.ps[:, 2 + a, 0:GROUPS * NCMP], ACT.Gelu_apprx_tanh,
                                       bias=bias[:, a:a + 1]).then_inc(activated, 1)
                    act.wait_ge(kc_made, 1)
                    act.activation(kc[:, :, :].rearrange("p g c -> p (g c)"), k.ps[0:HD, 6, 0:GROUPS * NCMP], ACT.Copy
                                   ).then_inc(kc_kept, 1)
                    act.wait_ge(vc_made, 1)
                    act.activation(vc[:, :, :].rearrange("p g d -> p (g d)"), k.ps[0:NCMP, 7, 0:GROUPS * HD], ACT.Copy)

                @block.vector
                def _(dve):
                    def turn_rows(rows, cross, cos, sin, keep):
                        a, b = keep
                        dve.drain()
                        dve.tensor_tensor(a, rows, cos, ALU.mult)
                        dve.tensor_tensor(b, cross, sin, ALU.mult)
                        dve.drain()
                        return dve.tensor_tensor(rows, a, b, ALU.add)

                    both = [cs[:, j].unsqueeze(1).broadcast_to([ROT, 2, T]) for j in range(2)]
                    for n in range(NR):
                        dve.wait_ge(crossed, n + 1)
                        turn_rows(rot_rows(n), k.ps[0:ROT, n % 2, :].rearrange("p (h t) -> p h t", h=2), both[0], both[1],
                                  (turned[:, 0], turned[:, 1])).then_inc(turned_s, 1)
                    dve.wait_ge(kc_crossed, 1)
                    ends = [cs[:, j].rearrange("p (c s) -> p c s", s=CMP_STRIDE)[:, 1:, CMP_STRIDE - 1]
                            .unsqueeze(1).broadcast_to([ROT, GROUPS, NCMP]) for j in range(2)]
                    keep = [turned[:, j, 0, 0:GROUPS * NCMP].rearrange("p (g c) -> p g c", g=GROUPS) for j in range(2)]
                    turn_rows(kc[0:ROT, :, :], k.ps[0:ROT, 5, 0:GROUPS * NCMP].rearrange("p (g c) -> p g c", g=GROUPS),
                              ends[0], ends[1], keep)

        with ExitStack() as tmp:
            def tb(name, shape, dtype=F32):
                return tmp.enter_context(nc.sbuf_tensor(name, shape, dtype))

            qg = tb("qg", [HD, HPG, T])
            vg = tb("vg", [P, 2, QT, HD])
            vcg = tb("vcg", [NCMP, HD])
            causal = tb("causal", [P, QT, T + 2 * NCMP])
            s = tb("s", [P, HPG, 2, T])
            sc = tb("sc", [P, HPG, NCMP])
            top = tb("top", [P, HPG, 3])
            total = tb("total", [P, HPG, 3])
            pt = tb("pt", [P, HPG, 2, QT, P])
            ptc = tb("ptc", [NCMP, HPG, P])
            scale = HD ** -0.5
            STEPS = QT
            with stage_semaphores(nc, "attn", "loaded", "grouped", "scored", "topped", "expd", "weighted", "turned", "turn_kept",
                                  "c_turned", "summed", "kept", "c_scored", "c_kept") as sems, \
                    nc.Block(name="attention", no_gpsimd_drain=True) as block:
                (loaded, grouped, scored, topped, expd, weighted, turned_s, turn_kept, c_turned, summed, kept, c_scored, c_kept) = sems

                @block.sync
                def _(sp):
                    sp.dma_start(causal[:, :, :], masks_in).then_inc(loaded, 16)

                @block.tensor
                def _(pe):
                    with pe.Fori(0, GROUPS) as g:
                        pe.wait_ge(grouped, g + 1)
                        for qt in range(QT):
                            n, nk = g * STEPS + qt, (qt + 1) * P
                            for hh in range(HPG):
                                mm = pe.matmul(k.ps[:, 4, hh * NCMP:(hh + 1) * NCMP], qg[:, hh, qt * P:(qt + 1) * P],
                                               kc[:, g, :], start=True, stop=True)
                            mm.then_inc(c_scored, 1)
                            for hh in range(HPG):
                                for br in range(2):
                                    mm = pe.matmul(k.ps[:, hh, br * T:br * T + nk], qg[:, hh, qt * P:(qt + 1) * P],
                                                   kt[:, 2 + br, g, 0:nk], start=True, stop=True)
                                mm.then_inc(scored, 1)
                            for hh in range(HPG):
                                pe.wait_ge(weighted, HPG * n + hh + 1)
                                for br in range(2):
                                    for c in range(qt + 1):
                                        mm = pe.transpose(k.ps[:, hh, (2 * br + c) * P:(2 * br + c + 1) * P],
                                                          s[:, hh, br, c * P:(c + 1) * P], k.ident[:, :])
                                mm.then_inc(turned_s, 1)
                            for hh in range(HPG):
                                mm = pe.transpose(k.ps[0:NCMP, 5, hh * P:(hh + 1) * P], sc[:, hh, :], k.ident[:, :])
                            mm.then_inc(c_turned, 1)
                            pe.wait_ge(c_kept, n + 1)
                            for hh in range(HPG):
                                pe.wait_ge(turn_kept, HPG * n + hh + 1)
                                at = k.ps[0:HD, 6 + qt, hh * P:(hh + 1) * P]
                                pe.matmul(at, vcg[:, :], ptc[:, hh, :], start=True, stop=False)
                                for br in range(2):
                                    for c in range(qt + 1):
                                        mm = pe.matmul(at, vg[:, br, c, :], pt[:, hh, br, c, :], start=False,
                                                       stop=(br == 1 and c == qt))
                            mm.then_inc(summed, 1)

                @block.scalar
                def _(act):
                    with act.Fori(0, GROUPS) as g:
                        for qt in range(QT):
                            n, nk = g * STEPS + qt, (qt + 1) * P
                            for hh in range(HPG):
                                act.wait_ge(topped, HPG * n + hh + 1)
                                for br in range(2):
                                    act.activation(s[:, hh, br, 0:nk], s[:, hh, br, 0:nk], ACT.Exp,
                                                   bias=top[:, hh, 1 + br:2 + br], accum_out=total[:, hh, 1 + br:2 + br])
                                act.activation(sc[:, hh, :], sc[:, hh, :], ACT.Exp, bias=top[:, hh, 0:1]).then_inc(expd, 1)
                            for hh in range(HPG):
                                act.wait_ge(turned_s, HPG * n + hh + 1)
                                for br in range(2):
                                    cp = act.activation(pt[:, hh, br, 0:qt + 1, :].rearrange("p c t -> p (c t)"),
                                                        k.ps[:, hh, 2 * br * P:(2 * br + qt + 1) * P], ACT.Copy)
                                cp.then_inc(turn_kept, 1)
                            act.wait_ge(c_turned, n + 1)
                            act.activation(ptc[:, :, :].rearrange("p h t -> p (h t)"), k.ps[0:NCMP, 5, :], ACT.Copy
                                           ).then_inc(c_kept, 1)
                            act.wait_ge(summed, n + 1)
                            for hh in range(HPG):
                                half = hh % 2
                                act.activation(attn[half * HD:(half + 1) * HD, g * (HPG // 2) + hh // 2, qt * P:(qt + 1) * P],
                                               k.ps[0:HD, 6 + qt, hh * P:(hh + 1) * P], ACT.Copy).then_inc(kept, 1)

                @block.vector
                def _(dve):
                    dve.wait_ge(loaded, 16)
                    dve.sem_inc(kept, QT * HPG)
                    with dve.Fori(0, GROUPS) as g:
                        dve.wait_ge(kept, QT * HPG * (g + 1))
                        dve.tensor_copy(qg[:, :, :], q[:, bass.ds(g * HPG, HPG), :])
                        for br in range(2):
                            dve.tensor_copy(vg[:, br], v[:, :, br, bass.ds(g, 1), :].rearrange("p a g d -> p a (g d)"))
                        dve.tensor_copy(vcg[:, :], vc[:, g, :]).then_inc(grouped, 1)
                        for qt in range(QT):
                            n, nk = g * STEPS + qt, (qt + 1) * P
                            dve.wait_ge(c_scored, n + 1)
                            dve.scalar_tensor_tensor(sc[:, :, :], k.ps[:, 4, 0:HPG * NCMP].rearrange("p (h c) -> p h c", h=HPG), scale,
                                                     causal[:, qt, T:T + NCMP].unsqueeze(1).broadcast_to([P, HPG, NCMP]),
                                                     ALU.mult, ALU.add)
                            for hh in range(HPG):
                                dve.wait_ge(scored, HPG * n + hh + 1)
                                dve.scalar_tensor_tensor(s[:, hh, :, 0:nk],
                                                         k.ps[:, hh, :].rearrange("p (b t) -> p b t", b=2)[:, :, 0:nk], scale,
                                                         causal[:, qt, 0:nk].unsqueeze(1).broadcast_to([P, 2, nk]),
                                                         ALU.mult, ALU.add)
                                dve.drain()
                                dve.tensor_reduce(top[:, hh, 1:3], s[:, hh, :, 0:nk], AX.X, ALU.max, negate=True)
                                dve.tensor_reduce(top[:, hh, 0:1], sc[:, hh, :], AX.X, ALU.max, negate=True).then_inc(topped, 1)
                            for hh in range(HPG):
                                dve.wait_ge(expd, HPG * n + hh + 1)
                                dve.tensor_tensor(sc[:, hh, :], sc[:, hh, :], causal[:, qt, T + NCMP:], ALU.mult)
                                dve.drain()
                                dve.tensor_reduce(total[:, hh, 0:1], sc[:, hh, :], AX.X, ALU.add)
                                dve.drain()
                                dve.tensor_scalar(total[:, hh, :], total[:, hh, :], 1e-30, None, ALU.max)
                                dve.drain()
                                dve.reciprocal(total[:, hh, :], total[:, hh, :])
                                dve.drain()
                                dve.tensor_tensor(total[:, hh, :].unsqueeze(1), total[:, hh, :].unsqueeze(1),
                                                  gates[:, qt, bass.ds(g * HPG + hh, 1), :], ALU.mult)
                                dve.drain()
                                for br in range(2):
                                    dve.tensor_scalar(s[:, hh, br, 0:nk], s[:, hh, br, 0:nk], total[:, hh, 1 + br:2 + br], None,
                                                      ALU.mult)
                                dve.tensor_scalar(sc[:, hh, :], sc[:, hh, :], total[:, hh, 0:1], None, ALU.mult
                                                  ).then_inc(weighted, 1)

        linear_residual(k, "attn_out", o_slots, attn, KD, T, x, x_cols=slice(0, T))


def linear_residual(k, name, first, inp, kt, n, x, x_cols):
    nc = k.nc
    per = kt // TILES
    with stage_semaphores(nc, name, "product", "added") as (product, added), \
            nc.Block(name=name, no_gpsimd_drain=True) as block:

        @block.sync
        def _(sp):
            k.refill(sp, first, KD * per, product, per=per)

        @block.tensor
        def _(pe):
            for m in range(KD):
                for c in range(per):
                    w = k.slot(pe, first + m * per + c)
                    for t in range(TILES):
                        mm = pe.matmul(k.ps[:, m, 0:n], w[:, t, :], inp[:, c * TILES + t, :],
                                       start=(c + t == 0), stop=(c == per - 1 and t == TILES - 1))
                mm.then_inc(product, 1)

        @block.vector
        def _(dve):
            for m in range(KD):
                dve.wait_ge(product, m + 1)
                dve.tensor_tensor(x[:, m, x_cols], k.ps[:, m, 0:n], x[:, m, x_cols], ALU.add)


def cols(a):
    a = np.asarray(a)
    return a.reshape(-1, P).T


def out_tiles(w):
    kk, m = w.shape
    return w.reshape(kk // P, P, m // P, P).transpose(2, 1, 0, 3).reshape(m // P, P, -1, TILES * P).transpose(0, 2, 1, 3).reshape(-1, P, TILES * P)


def first_block_stream(a):
    out = []
    pw = a["pool_w"][0].reshape(2, 2, 2, P, 2, P)
    out.append(pw.transpose(0, 3, 1, 4, 2, 5).reshape(2, P, TILES * P))

    def ffn(i):
        up = a["ffn_up"][i].reshape(KD, P, 2, KF, P).transpose(3, 2, 1, 0, 4).reshape(2 * KF, P, TILES * P)
        return [up, a["ffn_down"][i].reshape(KF, P, D)]

    def ple_w(i):
        pr = a["ple_proj"][i].reshape(2, P, 2, 4, P).transpose(2, 1, 3, 0, 4).reshape(2, P, TILES * P)
        return [pr, out_tiles(a["ple_gate"][i])]

    out += ffn(0) + ple_w(0)
    wkv = a["w_kv"].reshape(D, 6, GROUPS * HD)
    keys = np.concatenate([wkv[:, j] for j in (0, 1, 2, 4)], axis=1)
    vals = np.concatenate([wkv[:, j] for j in (3, 5)], axis=1)
    out.append(out_tiles(keys))
    out.append(vals.reshape(4, 2, P, 512).transpose(0, 2, 1, 3).reshape(4, P, TILES * P))
    out.append(out_tiles(a["w_in_b"][0][:, :HEADS * HD]))
    out.append(out_tiles(a["w_out_b"][0]))
    out += ffn(1) + ple_w(1)
    return out


def first_block_arrays(a):
    d = {}
    cl = []
    at = {}

    def put(name, arr):
        at[name] = (sum(c.shape[1] for c in cl), arr.shape[1])
        cl.append(arr)

    for i in range(2):
        put(f"norm_mix{i}", cols(a["norm_mix"][i]))
        put(f"norm_ffn{i}", cols(a["norm_ffn"][i]))
        put(f"norm_ple{i}", cols(a["norm_ple"][i]))
        taps = np.concatenate([a["ffn_conv"][i], a["ffn_conv_b"][i][None]], 0)
        put(f"taps{i}", taps.reshape(4, 2 * KF, P).transpose(2, 1, 0).reshape(P, -1))
    put("pool_scale", cols(a["pool_scale"][0]))
    put("norm_kv", cols(a["norm_kv"]))
    put("norm_final", cols(a["norm_final"]))
    d["x_in"] = a["x"][0].T.reshape(KD, P, T).transpose(1, 0, 2)
    d["p_in"] = a["p"][:, 0].transpose(0, 2, 1).reshape(2, 2, P, T).transpose(0, 2, 1, 3)
    d["pos_in"] = np.broadcast_to(a["positions"][0].astype(np.int32), (ROT, T))
    d["gate_w_in"] = a["w_in_b"][0][:, HEADS * HD:].reshape(KD, P, 3 * HEADS).transpose(1, 0, 2)
    w1 = np.stack([a["cmp_w1_k"], a["cmp_w1_v"]]).reshape(2, CMP_LEN, HD, P).transpose(2, 0, 1, 3)
    d["cmp_w1_in"] = w1
    posT = np.concatenate([a["cmp_pos_k"].T, a["cmp_pos_v"].T], 1)
    d["cmp_small_in"] = np.concatenate([a["cmp_w2_k"], a["cmp_w2_v"], np.concatenate([posT, np.zeros_like(posT)], 0)], 1)
    return d, cl, at


def first_block_shape_constants():
    d = {}
    t = np.arange(T)
    rc = np.stack([1.0 / np.minimum(t + 1, w) for w in WINDOWS]).astype(np.float32)
    d["rcount_in"] = np.broadcast_to(rc, (P, 4, T))
    inv = (np.float32(500000.0) ** (-np.arange(0, ROT, 2, dtype=np.float32) / np.float32(ROT))).astype(np.float32)
    rope = np.zeros((P, 1 + ROT), np.float32)
    rope[:ROT, 0] = np.concatenate([inv, inv])
    for m in range(ROT // 2):
        rope[m + ROT // 2, 1 + m] = -1.0
        rope[m, 1 + m + ROT // 2] = 1.0
    d["rope_in"] = rope
    q = np.arange(P)[:, None]
    m = np.zeros((P, 2, T + 2 * NCMP), np.float32)
    for qt in range(2):
        m[:, qt, :T] = np.where(np.arange(T)[None] <= q + qt * P, 0.0, NEG)
        ok = CMP_STRIDE * np.arange(NCMP)[None] + CMP_LEN - 1 <= q + qt * P
        m[:, qt, T:T + NCMP] = np.where(ok, 0.0, NEG)
        m[:, qt, T + NCMP:] = ok
    d["masks_in"] = m
    return d
N_MOD = 6
SEGS = 2
TT = T2 // P
SH, SP_, SG, SN = 16, 64, 4, 128
SREP = SH // SG
XBC = (SH * SP_ + 2 * SG * SN) // P
XS_TILES = SH * SP_ // P
SCONV, CFK = 5, 31
GRID = 64
ROWS = T // GRID
GH, GC = 8, 64
NCH = T // GC
EXPERTS, EGROUPS, EPG, TOPK = 16, 4, 4, 2
DEXP = 512
KE = DEXP // P


def halves(ap):
    return ap.rearrange("p (s t) -> p s t", s=SEGS)


def final_norm(k, x, gain, name):
    nc = k.nc
    with stage_semaphores(nc, name, *NORM_SEMS) as norm, nc.Block(name=name, no_gpsimd_drain=True) as block:

        @block.scalar
        def _(act):
            norm_scalar(k, act, norm, x, T)

        @block.tensor
        def _(pe):
            norm_tensor(k, pe, norm, T)

        @block.vector
        def _(dve):
            norm_vector(k, dve, norm, x, x, gain, T)


def modulation(k, cond, bias, mods):
    nc = k.nc
    NM = N_MOD * KD
    HALF = RING // 2
    for layer in range(2):
        first = k.take(NM)
        name = f"mod{layer}"
        with stage_semaphores(nc, name, "activated", "product", "kept") as (activated, product, kept), \
                nc.Block(name=name, no_gpsimd_drain=True) as block:

            @block.sync
            def _(sp):
                k.refill(sp, first, NM, product)

            @block.scalar
            def _(act):
                if layer == 0:
                    act.activation(cond, cond, ACT.Silu).then_inc(activated, 1)

            @block.tensor
            def _(pe):
                if layer == 0:
                    pe.wait_ge(activated, 1)

                def one(m, j, i):
                    if j % HALF == 0:
                        pe.wait_ge(kept, i * 2 + j // HALF + 1)
                    w = k.slot(pe, first + j, i)
                    for t in range(KD):
                        mm = pe.matmul(k.ps[:, j // HALF % 2, j % HALF * 2:j % HALF * 2 + 2], w[:, t, :], cond[:, t, :],
                                       start=(t == 0), stop=(t == KD - 1))
                    mm.then_inc(product, 1)

                rounds_then_rest(pe, NM, RING, one)

            @block.vector
            def _(dve):
                dve.sem_inc(kept, 2)

                def half(n, j, i):
                    dve.wait_ge(product, n * HALF + HALF)
                    dve.tensor_tensor(mods[:, layer, bass.ds(n * HALF, HALF), :],
                                      k.ps[:, j, 0:2 * HALF].rearrange("p (m s) -> p m s", s=2),
                                      bias[:, bass.ds(n * HALF + layer * NM, HALF)].unsqueeze(2).broadcast_to([P, HALF, 2]),
                                      ALU.add).then_inc(kept, 1)

                rounds_then_rest(dve, NM // HALF, 2, half)


def scaled_gains(k, mods, gains, out):
    nc = k.nc
    with nc.Block(name="scaled_gains", no_gpsimd_drain=True) as block:

        @block.vector
        def _(dve):
            for layer in range(2):
                for which, part in ((0, 1), (1, 4)):
                    o = out[:, layer, which]
                    m = mods[:, layer, part * KD:(part + 1) * KD, :]
                    dve.tensor_scalar(o, m, 1.0, None, ALU.add)
                    dve.drain()
                    dve.tensor_tensor(o, o, gains[which][:, layer * KD:(layer + 1) * KD].unsqueeze(2).broadcast_to([P, KD, 2]),
                                      ALU.mult)


def mod_norm_vector(k, dve, norm, x, segs, gain, n, made):
    dve.wait_ge(norm[2], 1)
    dve.reciprocal(k.rstd[:, 0:n], k.root[:, 0:n])
    dve.drain()
    for t in range(KD):
        for j, s in enumerate(segs):
            dve.scalar_tensor_tensor(k.h[:, t, j * T:(j + 1) * T], x[:, t, s * T:(s + 1) * T], gain[:, t, s:s + 1],
                                     k.rstd[:, j * T:(j + 1) * T], ALU.mult, ALU.mult).then_inc(made, 1)


def mod_norm_shift(k, act, segs, shift, made, ready, col_major=False):
    for t in range(KD):
        for j, s in enumerate(segs):
            act.wait_ge(made, t * len(segs) + j + 1)
            of = k.h[:, t, j * T:(j + 1) * T]
            to = of
            if col_major:
                to = k.sq[:, t, j * T:(j + 1) * T]
                if s == 1:
                    of = of.rearrange("p (r w) -> p r w", r=ROWS)
                    to = to.rearrange("p (w r) -> p r w", r=ROWS)
            act.activation(to, of, ACT.Identity, bias=shift[:, t, s:s + 1]).then_inc(ready, 1)


def even_in(k, x, col, gain, shift, zs, xbc, cf, dt):
    nc = k.nc
    cf_slots, z_slots, x_slots = k.take(16), k.take(8), k.take(XBC)
    NM = 40
    dt_w = col("dt_w").rearrange("p (t c) -> p t c", t=KD)
    ctaps = col("ssd_taps").rearrange("p (t j) -> p t j", j=SCONV + 1)
    ftaps = col("cf_taps").rearrange("p (t j) -> p t j", j=CFK + 1)
    with ExitStack() as local:
        u = local.enter_context(nc.sbuf_tensor("cf_u", [P, KD, T2], F32))
        keep = local.enter_context(nc.sbuf_tensor("cf_gate", [P, 2, T2], F32))
        raw = local.enter_context(nc.sbuf_tensor("dt_raw", [P, 2, TT * 32], F32))
        with stage_semaphores(nc, "even_in", *NORM_SEMS, "made", "ready", "product", "gated", "freed", "based", "conved",
                              "dt_product", "dt_abs", "dt_log") as sems, nc.Block(name="even_in", no_gpsimd_drain=True) as block:
            norm, (made, ready, product, gated, freed, based, conved, dt_product, dt_abs, dt_log) = sems[:4], sems[4:]
            BANKS = 4

            @block.sync
            def _(sp):
                k.refill(sp, cf_slots, NM, product)

            @block.tensor
            def _(pe):
                norm_tensor(k, pe, norm, T2)
                pe.wait_ge(ready, KD * SEGS)
                for tt in range(TT):
                    for t in range(KD):
                        mm = pe.matmul(k.ps[:, 6, tt * 32:(tt + 1) * 32], k.h[:, t, tt * P:(tt + 1) * P], dt_w[:, t, :],
                                       start=(t == 0), stop=(t == KD - 1))
                mm.then_inc(dt_product, 1)
                for n in range(NM):
                    if n >= BANKS:
                        pe.wait_ge(freed, n - BANKS + 1)
                    w = k.slot(pe, cf_slots + n)
                    for t in range(KD):
                        mm = pe.matmul(k.ps[:, n % BANKS, :], w[:, t, :], k.h[:, t, :], start=(t == 0), stop=(t == KD - 1))
                    mm.then_inc(product, 1)

            @block.scalar
            def _(act):
                norm_scalar(k, act, norm, x, T2)
                mod_norm_shift(k, act, (0, 1), shift, made, ready)
                for m in range(KD):
                    act.wait_ge(product, 2 * m + 2)
                    if m >= 2:
                        act.wait_ge(freed, 2 * m - 2)
                    act.activation(keep[:, m % 2, :], k.ps[:, (2 * m + 1) % BANKS, :], ACT.Sigmoid).then_inc(gated, 1)
                act.wait_ge(dt_abs, 1)
                act.activation(raw[:, 1, :], raw[:, 1, :], ACT.Exp, scale=-1.0)
                act.drain()
                act.activation(raw[:, 1, :], raw[:, 1, :], ACT.Ln, bias=k.ones[:, 0:1]).then_inc(dt_log, 1)
                for m in range(KD):
                    n = 16 + m
                    act.wait_ge(product, n + 1)
                    act.activation(zs[:, m, :], k.ps[:, n % BANKS, :], ACT.Silu).then_inc(based, 1)
                for m in range(XBC):
                    n = 24 + m
                    act.wait_ge(product, n + 1)
                    act.activation(xbc[:, m, :], k.ps[:, n % BANKS, :], ACT.Identity, scale=ctaps[:, m, SCONV // 2:SCONV // 2 + 1],
                                   bias=ctaps[:, m, SCONV:SCONV + 1]).then_inc(based, 1)
                    if m >= 1:
                        act.wait_ge(conved, m)
                        act.activation(xbc[:, m - 1, :], xbc[:, m - 1, :], ACT.Silu)
                act.wait_ge(conved, XBC)
                act.activation(xbc[:, XBC - 1, :], xbc[:, XBC - 1, :], ACT.Silu)

            @block.vector
            def _(dve):
                mod_norm_vector(k, dve, norm, x, (0, 1), gain, T2, made)
                dve.wait_ge(dt_product, 1)
                bias = col("dt_bias").unsqueeze(1).broadcast_to([P, TT, 32])
                three = raw[:, 0, :].rearrange("p (t c) -> p t c", t=TT)
                dve.tensor_tensor(three, k.ps[:, 6, 0:TT * 32].rearrange("p (t c) -> p t c", t=TT), bias, ALU.add)
                dve.drain()
                dve.scalar_tensor_tensor(raw[:, 1, :], raw[:, 0, :], -1.0, raw[:, 0, :], ALU.mult, ALU.max).then_inc(dt_abs, 1)
                for m in range(KD):
                    dve.wait_ge(gated, m + 1)
                    dve.tensor_tensor(u[:, m, :], k.ps[:, 2 * m % BANKS, :], keep[:, m % 2, :], ALU.mult).then_inc(freed, 2)
                dve.wait_ge(dt_log, 1)
                dve.scalar_tensor_tensor(dt[:, :, :].rearrange("p t c -> p (t c)"), raw[:, 0, :], 0.0, raw[:, 1, :],
                                         ALU.max, ALU.add)
                work = [(m, j) for m in range(0, KD, 2) for j in [CFK // 2] + [j for j in range(CFK) if j != CFK // 2]]

                def cf_tap(m0, j):
                    s = j - CFK // 2
                    for m in (m0, m0 + 1):
                        if s == 0:
                            dve.tensor_scalar(cf[:, m, :], u[:, m, :], ftaps[:, m, j:j + 1], ftaps[:, m, CFK:CFK + 1],
                                              ALU.mult, ALU.add)
                            continue
                        lo, hi = max(0, -s), max(0, s)
                        for rows in (1, ROWS):
                            w = T // rows
                            part = slice(0, T) if rows == 1 else slice(T, T2)
                            o = cf[:, m, part].rearrange("p (r w) -> p r w", r=rows)[:, :, lo:w - hi]
                            i = u[:, m, part].rearrange("p (r w) -> p r w", r=rows)[:, :, lo + s:w - hi + s]
                            dve.scalar_tensor_tensor(o, i, ftaps[:, m, j:j + 1], o, ALU.mult, ALU.add)
                    dve.drain()

                steps = 8 + XBC
                done = 0
                dve.drain()
                for n in range(steps):
                    dve.wait_ge(based, n + 1)
                    if n < 8:
                        dve.sem_inc(freed, 1)
                    else:
                        m, bank = n - 8, (16 + n) % BANKS
                        for j in (0, 1, 3, 4):
                            s = j - SCONV // 2
                            lo, hi = max(0, -s), max(0, s)
                            last = dve.scalar_tensor_tensor(
                                halves(xbc[:, m, :])[:, :, lo:T - hi], halves(k.ps[:, bank, :])[:, :, lo + s:T - hi + s],
                                ctaps[:, m, j:j + 1], halves(xbc[:, m, :])[:, :, lo:T - hi], ALU.mult, ALU.add)
                            if j < 4:
                                dve.drain()
                        last.then_inc(conved, 1)
                        dve.drain()
                        dve.sem_inc(freed, 1)
                    upto = len(work) * (n + 1) // steps
                    for m0, j in work[done:upto]:
                        cf_tap(m0, j)
                    done = upto


def ssd(k, col, tri, dt, zs, xbc):
    nc = k.nc
    xs_tok = k.h[:, :, :].rearrange("p a b -> p (a b)").rearrange("p (t f) -> p t f", t=TT)
    spare = k.sq[:, :, :].rearrange("p a b -> p (a b)")
    b_tok = spare[:, 0:TT * SG * SN].rearrange("p (t f) -> p t f", t=TT)
    states = spare[:, TT * SG * SN:].rearrange("p (d f) -> p d f", d=2)
    y = xbc[:, 0:XS_TILES, :].rearrange("p a b -> p (a b)").rearrange("p (t f) -> p t f", t=TT)
    bf, cf_ = xbc[:, XS_TILES:XS_TILES + SG, :], xbc[:, XS_TILES + SG:, :]
    GW = SREP * SP_
    with ExitStack() as local:
        def sb(name, shape):
            return local.enter_context(nc.sbuf_tensor(name, shape, F32))

        la = sb("la", [P, TT, 2, SH])
        aneg = sb("aneg", [P, 2 * SH])
        acum = sb("acum", [P, TT, 2, SH])
        to_end = sb("to_end", [P, TT, 2, SH])
        eacum = sb("eacum", [P, TT, 2, SH])
        cdec = sb("cdec", [P, TT, 2, SH])
        dt4 = dt[:, :, :].rearrange("p t (d h) -> p t d h", d=2)
        with stage_semaphores(nc, "ssd_prep", "a_ready", "la_ready", "turned", "kept", "summed", "ended", "skipped") as sems, \
                nc.Block(name="ssd_prep", no_gpsimd_drain=True) as block:
            a_ready, la_ready, turned, kept, summed, ended, skipped = sems
            NT = 12

            @block.tensor
            def _(pe):
                for tt in range(TT):
                    for b in range(3):
                        n = tt * 3 + b
                        if n >= 6:
                            pe.wait_ge(kept, n - 5)
                        for j in range(4):
                            mm = pe.transpose(k.ps[:, n % 6, j * P:(j + 1) * P], xbc[:, b * 4 + j, tt * P:(tt + 1) * P], k.ident[:, :])
                        mm.then_inc(turned, 1)
                pe.wait_ge(la_ready, 1)
                for c in range(TT):
                    for d in range(2):
                        at = (c * 2 + d) * SH
                        pe.matmul(k.ps[:, 6, at:at + SH], tri[:, d, :], la[:, c, d, :], start=True, stop=True)
                        mm = pe.matmul(k.ps[:, 7, at:at + SH], k.ones[:, :], la[:, c, d, :], start=True, stop=True)
                mm.then_inc(summed, 1)

            @block.scalar
            def _(act):
                act.activation(aneg[:, :], col("a_log"), ACT.Exp).then_inc(a_ready, 1)
                for n in range(TT * 3):
                    act.wait_ge(turned, n + 1)
                    tt, b = divmod(n, 3)
                    to = xs_tok[:, tt, b * 512:(b + 1) * 512] if b < 2 else b_tok[:, tt, :]
                    act.activation(to, k.ps[:, n % 6, :], ACT.Copy).then_inc(kept, 1)
                act.wait_ge(ended, 1)
                for a in (to_end, eacum, cdec):
                    act.activation(a[:, :, :, :], a[:, :, :, :], ACT.Exp)

            @block.vector
            def _(dve):
                dve.memset(states, 0.0)
                dve.wait_ge(a_ready, 1)
                dve.tensor_scalar(aneg[:, :], aneg[:, :], -1.0, None, ALU.mult)
                dve.drain()
                dve.tensor_tensor(la[:, :, :, :].rearrange("p t d h -> p t (d h)"), dt[:, :, :],
                                  aneg[:, :].unsqueeze(1).broadcast_to([P, TT, 2 * SH]), ALU.mult).then_inc(la_ready, 1)
                dve.wait_ge(summed, 1)
                flat = [a[:, :, :, :].rearrange("p t d h -> p (t d h)") for a in (acum, to_end, eacum, cdec)]
                dve.tensor_copy(flat[0], k.ps[:, 6, 0:TT * 2 * SH])
                dve.tensor_copy(flat[3], k.ps[:, 7, 0:TT * 2 * SH])
                dve.drain()
                dve.tensor_copy(flat[2], flat[0])
                dve.tensor_tensor(flat[1], flat[3], flat[0], ALU.subtract).then_inc(ended, 1)
                dve.wait_ge(kept, TT * 3)
                for tt in range(TT):
                    dve.tensor_tensor(y[:, tt, :].rearrange("p (h d) -> p h d", h=SH),
                                      xs_tok[:, tt, :].rearrange("p (h d) -> p h d", h=SH),
                                      col("ssd_d").unsqueeze(2).broadcast_to([P, SH, SP_]), ALU.mult)

        xdt = sb("xdt", [P, 2, SH * SP_])
        xw = sb("xw", [P, 2, SH * SP_])
        seg = sb("seg", [P, 2, SREP, P])
        cbm = sb("cbm", [P, 2, P])
        yo = sb("yo", [P, GW])
        units = [(s, d, (s if d == 0 else s ^ 1), g) for s in range(TT) for d in range(2) for g in range(SG)]
        with stage_semaphores(nc, "ssd", "rows", "segs", "exps", "mixed", "summed", "added", "scaled") as sems, \
                nc.Block(name="ssd_scan", no_gpsimd_drain=True) as block:
            rows, segs, exps, mixed, summed, added, scaled = sems

            @block.tensor
            def _(pe):
                def front(u):
                    s, d, c, g = units[u]
                    if u >= 2:
                        pe.wait_ge(segs, u - 1)
                    for h in range(SREP):
                        pe.matmul(k.ps[:, u % 2, h * P:(h + 1) * P],
                                  la[:, c, d, g * SREP + h:g * SREP + h + 1].broadcast_to([P, P]), tri[:, d, :],
                                  start=True, stop=True)
                    pe.matmul(k.ps[:, 2 + u % 2, 0:P], bf[:, g, c * P:(c + 1) * P], cf_[:, g, c * P:(c + 1) * P],
                              start=True, stop=True).then_inc(rows, 1)

                front(0)
                front(1)
                for u, (s, d, c, g) in enumerate(units):
                    pe.wait_ge(mixed, u + 1)
                    if u >= 2:
                        pe.wait_ge(added, u - 1)
                    for h in range(SREP):
                        hh = g * SREP + h
                        pe.matmul(k.ps[:, 4 + u % 2, h * SP_:(h + 1) * SP_], seg[:, u % 2, h, :],
                                  xdt[:, (u // SG) % 2, hh * SP_:(hh + 1) * SP_], start=True, stop=True)
                    if s:
                        pe.wait_ge(added, u - 2 * SG + 1)
                    pe.matmul(k.ps[:, 4 + u % 2, GW:2 * GW], cf_[:, g, c * P:(c + 1) * P], states[:, d, g * GW:(g + 1) * GW],
                              start=True, stop=True)
                    pe.matmul(k.ps[:, 6 + u % 2, 0:GW], b_tok[:, c, g * SN:(g + 1) * SN],
                              xw[:, (u // SG) % 2, g * GW:(g + 1) * GW], start=True, stop=True).then_inc(summed, 1)
                    if u + 2 < len(units):
                        front(u + 2)

            @block.scalar
            def _(act):
                for u in range(len(units)):
                    act.wait_ge(segs, u + 1)
                    act.activation(seg[:, u % 2], seg[:, u % 2], ACT.Exp).then_inc(exps, 1)

            @block.vector
            def _(dve):
                def heads(ap):
                    return ap.rearrange("p (h e) -> p h e", e=SP_)

                def front(u):
                    s, d, c, g = units[u]
                    if g == 0:
                        v = (u // SG) % 2
                        if u >= 2 * SG:
                            dve.wait_ge(summed, u - SG)
                        dve.tensor_tensor(heads(xdt[:, v, :]), heads(xs_tok[:, c, :]),
                                          dt4[:, c, d, :].unsqueeze(2).broadcast_to([P, SH, SP_]), ALU.mult)
                        dve.drain()
                        dve.tensor_tensor(heads(xw[:, v, :]), heads(xdt[:, v, :]),
                                          to_end[:, c, d, :].unsqueeze(2).broadcast_to([P, SH, SP_]), ALU.mult)
                    dve.wait_ge(rows, u + 1)
                    if u >= 2:
                        dve.wait_ge(summed, u - 1)
                    a = acum[:, c, d, g * SREP:(g + 1) * SREP].unsqueeze(2).broadcast_to([P, SREP, P])
                    dve.tensor_tensor(cbm[:, u % 2, :], k.ps[:, 2 + u % 2, 0:P], tri[:, d, :], ALU.mult)
                    dve.tensor_tensor(seg[:, u % 2], k.ps[:, u % 2, :].rearrange("p (h l) -> p h l", h=SREP), a, ALU.min)
                    dve.drain()
                    dve.tensor_tensor(seg[:, u % 2], seg[:, u % 2], a, ALU.subtract).then_inc(segs, 1)

                def back(u):
                    s, d, c, g = units[u]
                    dve.wait_ge(summed, u + 1)
                    dve.tensor_tensor(heads(yo[:, :]), heads(k.ps[:, 4 + u % 2, GW:2 * GW]),
                                      eacum[:, c, d, g * SREP:(g + 1) * SREP].unsqueeze(2).broadcast_to([P, SREP, SP_]), ALU.mult)
                    yy = y[:, c, g * GW:(g + 1) * GW]
                    dve.tensor_tensor(yy, yy, k.ps[:, 4 + u % 2, 0:GW], ALU.add)
                    st = states[:, d, g * GW:(g + 1) * GW]
                    dve.tensor_tensor(heads(st), heads(st),
                                      cdec[:, c, d, g * SREP:(g + 1) * SREP].unsqueeze(2).broadcast_to([P, SREP, SP_]), ALU.mult)
                    dve.drain()
                    dve.tensor_tensor(yy, yy, yo[:, :], ALU.add)
                    dve.tensor_tensor(st, st, k.ps[:, 6 + u % 2, 0:GW], ALU.add).then_inc(added, 1)
                    dve.drain()

                front(0)
                for u in range(len(units)):
                    if u + 1 < len(units):
                        front(u + 1)
                    dve.wait_ge(exps, u + 1)
                    dve.tensor_tensor(seg[:, u % 2], seg[:, u % 2], cbm[:, u % 2, :].unsqueeze(1).broadcast_to([P, SREP, P]),
                                      ALU.mult).then_inc(mixed, 1)
                    if u:
                        back(u - 1)
                back(len(units) - 1)

    with stage_semaphores(nc, "ssd_out", *NORM_SEMS, "turned", "gated") as sems, \
            nc.Block(name="ssd_readout", no_gpsimd_drain=True) as block:
        norm, (turned, gated) = sems[:4], sems[4:]

        @block.tensor
        def _(pe):
            for m in range(KD):
                if m >= 4:
                    pe.wait_ge(gated, m - 3)
                for tt in range(TT):
                    mm = pe.transpose(k.ps[:, m % 4, tt * P:(tt + 1) * P], y[:, tt, m * P:(m + 1) * P], k.ident[:, :])
                mm.then_inc(turned, 1)
            norm_tensor(k, pe, norm, T2)

        @block.scalar
        def _(act):
            for m in range(KD):
                act.wait_ge(gated, m + 1)
                act.activation(k.sq[:, m, :], zs[:, m, :], ACT.Square).then_inc(norm[0], 1)
            act.wait_ge(norm[1], 1)
            act.activation(k.root[:, :], k.ps[:, NORM_BANK, :], ACT.Sqrt, scale=1.0 / D, bias=k.eps[:, 0:1]).then_inc(norm[2], 1)

        @block.vector
        def _(dve):
            for m in range(KD):
                dve.wait_ge(turned, m + 1)
                dve.tensor_tensor(zs[:, m, :], k.ps[:, m % 4, :], zs[:, m, :], ALU.mult).then_inc(gated, 1)
            norm_vector(k, dve, norm, zs, zs, col("ssd_norm_g"), T2)


def conformer_norm(k, cf, gain, bias):
    nc = k.nc
    with stage_semaphores(nc, "cf_norm", *NORM_SEMS, "mean_done", "centred") as sems, \
            nc.Block(name="conformer_norm", no_gpsimd_drain=True) as block:
        norm, (mean_done, centred) = sems[:4], sems[4:]

        @block.tensor
        def _(pe):
            for t in range(KD):
                mm = pe.matmul(k.ps[:, 0, :], k.ones[:, :], cf[:, t, :], start=(t == 0), stop=(t == KD - 1))
            mm.then_inc(mean_done, 1)
            norm_tensor(k, pe, norm, T2)

        @block.vector
        def _(dve):
            dve.wait_ge(mean_done, 1)
            for t in range(KD):
                dve.scalar_tensor_tensor(cf[:, t, :], k.ps[:, 0, :], -1.0 / D, cf[:, t, :], ALU.mult, ALU.add).then_inc(centred, 1)
            dve.wait_ge(norm[2], 1)
            dve.reciprocal(k.rstd[:, :], k.root[:, :])
            dve.drain()
            for t in range(KD):
                dve.tensor_tensor(cf[:, t, :], cf[:, t, :], k.rstd[:, :], ALU.mult).then_inc(norm[3], 1)

        @block.scalar
        def _(act):
            for t in range(KD):
                act.wait_ge(centred, t + 1)
                act.activation(k.sq[:, t, :], cf[:, t, :], ACT.Square).then_inc(norm[0], 1)
            act.wait_ge(norm[1], 1)
            act.activation(k.root[:, :], k.ps[:, NORM_BANK, :], ACT.Sqrt, scale=1.0 / D, bias=k.eps[:, 0:1]).then_inc(norm[2], 1)
            for t in range(KD):
                act.wait_ge(norm[3], t + 1)
                act.activation(cf[:, t, :], cf[:, t, :], ACT.Silu, scale=gain[:, t:t + 1], bias=bias[:, t:t + 1])


def even_out(k, x, zs, cf, gate):
    nc = k.nc
    per = 2
    first = k.take(KD * per)
    with stage_semaphores(nc, "even_out", "product") as (product,), nc.Block(name="even_out", no_gpsimd_drain=True) as block:

        @block.sync
        def _(sp):
            k.refill(sp, first, KD * per, product, per=per)

        @block.tensor
        def _(pe):
            for m in range(KD):
                for c, inp in enumerate((zs, cf)):
                    w = k.slot(pe, first + m * per + c)
                    for t in range(TILES):
                        mm = pe.matmul(k.ps[:, m, :], w[:, t, :], inp[:, t, :], start=(c + t == 0), stop=(c == 1 and t == TILES - 1))
                mm.then_inc(product, 1)

        @block.vector
        def _(dve):
            for m in range(KD):
                dve.wait_ge(product, m + 1)
                for s in range(SEGS):
                    xs = x[:, m, s * T:(s + 1) * T]
                    dve.scalar_tensor_tensor(xs, k.ps[:, m, s * T:(s + 1) * T], gate[:, m, s:s + 1], xs, ALU.mult, ALU.add)


def moe(k, x, segs, gain, shift, gate, router_w, router_b, slot_number, name):
    nc = k.nc
    n = len(segs) * T
    x0 = segs[0] * T
    tt_n = n // P
    first = k.take(EXPERTS * RING)
    with ExitStack() as local:
        def sb(nm, shape, dtype=F32):
            return local.enter_context(nc.sbuf_tensor(f"{name}_{nm}", shape, dtype))

        comb = sb("comb", [P, tt_n, EXPERTS])
        place = sb("place", [P, tt_n, EXPERTS])
        late = sb("late", [P, tt_n, EXPERTS])
        most = sb("most", [P, 1], I32)
        with nc.sbuf_tensor(f"{name}_token_rows", [P, tt_n, D], F32) as rows:
            moe_route(k, x, segs, gain, shift, router_w, router_b, name, n, tt_n, comb, place, late, most, rows)
            moe_experts(k, x, segs, gate, name, n, tt_n, first, comb, place, rows, slot_number)
        fullest = nc.values_load(most[0:1, 0:1], min_val=0, max_val=n,
                                 skip_runtime_bounds_check_because="a count of n tokens")
        moe_late(k, x, segs, gate, name + "_late", n, tt_n, first, late, fullest)


def moe_route(k, x, segs, gain, shift, router_w, router_b, name, n, tt_n, comb, place, late, most, rows):
    nc = k.nc
    x0 = segs[0] * T
    xin = x[:, :, x0:x0 + n]
    with ExitStack() as local:
        def sb(nm, shape, dtype=F32):
            return local.enter_context(nc.sbuf_tensor(f"{name}_{nm}", shape, dtype))

        score = sb("score", [P, tt_n, EGROUPS, EPG])
        sel = sb("sel", [P, tt_n, EGROUPS, EPG])
        chosen = sb("chosen", [P, tt_n, EXPERTS])
        w3 = sb("w3", [P, 8, tt_n * EGROUPS])
        rank = sb("rank", [P, tt_n, EGROUPS, EPG])
        top = sb("top", [P, 4, tt_n])
        with stage_semaphores(nc, f"{name}_route", *NORM_SEMS, "made", "ready", "routed", "scored", "picked", "placed",
                              "turned", "kept") as sems, nc.Block(name=f"{name}_route", no_gpsimd_drain=True) as block:
            norm, (made, ready, routed, scored, picked, placed, turned, kept) = sems[:4], sems[4:]
            UNITS, BANKS = 2 * tt_n, 4

            @block.tensor
            def _(pe):
                norm_tensor(k, pe, norm, n)
                pe.wait_ge(ready, KD * len(segs))
                for tt in range(tt_n):
                    for t in range(KD):
                        mm = pe.matmul(k.ps[:, 6, tt * EXPERTS:(tt + 1) * EXPERTS], k.h[:, t, tt * P:(tt + 1) * P],
                                       router_w[:, t, :], start=(t == 0), stop=(t == KD - 1))
                mm.then_inc(routed, 1)
                for u in range(UNITS):
                    if u >= BANKS:
                        pe.wait_ge(kept, u - BANKS + 1)
                    for j in range(4):
                        mm = pe.transpose(k.ps[:, u % BANKS, j * P:(j + 1) * P],
                                          k.h[:, u % 2 * 4 + j, u // 2 * P:(u // 2 + 1) * P], k.ident[:, :])
                    mm.then_inc(turned, 1)
                pe.wait_ge(picked, 1)
                for tt in range(tt_n):
                    for s in range(tt + 1):
                        pe.matmul(k.ps[:, NORM_BANK, tt * EXPERTS:(tt + 1) * EXPERTS], k.upto[:, :] if s == tt else k.ones[:, :],
                                  chosen[:, s, :], start=(s == 0), stop=(s == tt))
                for s in range(tt_n):
                    mm = pe.matmul(k.ps[:, NORM_BANK, tt_n * EXPERTS:(tt_n + 1) * EXPERTS], k.ones[:, :], chosen[:, s, :],
                                   start=(s == 0), stop=(s == tt_n - 1))
                mm.then_inc(placed, 1)

            @block.scalar
            def _(act):
                norm_scalar(k, act, norm, xin, n)
                mod_norm_shift(k, act, segs, shift, made, ready)
                act.wait_ge(routed, 1)
                act.activation(score[:, :, :, :].rearrange("p t g e -> p (t g e)"), k.ps[:, 6, 0:tt_n * EXPERTS], ACT.Sigmoid
                               ).then_inc(scored, 1)
                for u in range(UNITS):
                    act.wait_ge(turned, u + 1)
                    act.copy(rows[:, u // 2, u % 2 * 512:(u % 2 + 1) * 512], k.ps[:, u % BANKS, :]).then_inc(kept, 1)

            @block.vector
            def _(dve):
                mod_norm_vector(k, dve, norm, x, segs, gain, n, made)
                dve.wait_ge(scored, 1)
                G = tt_n * EGROUPS
                s4 = score[:, :, :, :].rearrange("p t g e -> p (t g) e")
                v4 = sel[:, :, :, :].rearrange("p t g e -> p (t g) e")
                r4 = rank[:, :, :, :].rearrange("p t g e -> p (t g) e")
                wk = [w3[:, i, :] for i in range(8)]

                def tt_(o, a, b, op):
                    dve.tensor_tensor(o, a, b, op)
                    dve.drain()

                tt_(sel[:, :, :, :].rearrange("p t g e -> p t (g e)"), score[:, :, :, :].rearrange("p t g e -> p t (g e)"),
                    router_b.unsqueeze(1).broadcast_to([P, tt_n, EXPERTS]), ALU.add)
                e = [v4[:, :, i] for i in range(EPG)]
                tt_(wk[0], e[0], e[1], ALU.max)
                tt_(wk[1], e[0], e[1], ALU.min)
                tt_(wk[2], e[2], e[3], ALU.max)
                tt_(wk[3], e[2], e[3], ALU.min)
                tt_(wk[4], wk[0], wk[2], ALU.max)
                tt_(wk[5], wk[0], wk[2], ALU.min)
                tt_(wk[6], wk[1], wk[3], ALU.max)
                tt_(wk[5], wk[5], wk[6], ALU.max)
                tt_(wk[4], wk[4], wk[5], ALU.add)
                gs = wk[4].rearrange("p (t g) -> p t g", g=EGROUPS)
                isg = wk[5].rearrange("p (t g) -> p t g", g=EGROUPS)
                dve.tensor_reduce(top[:, 0, :], gs, AX.X, ALU.max)
                dve.drain()
                tt_(isg, gs, top[:, 0, :].unsqueeze(2).broadcast_to([P, tt_n, EGROUPS]), ALU.is_equal)
                dve.memset(top[:, 1, :], 1.0)
                dve.drain()
                for g in range(EGROUPS):
                    tt_(isg[:, :, g], isg[:, :, g], top[:, 1, :], ALU.mult)
                    tt_(top[:, 1, :], top[:, 1, :], isg[:, :, g], ALU.subtract)
                dve.memset(rank[:, :, :, :], 0.0)
                dve.drain()
                for i in range(EPG):
                    for j in range(i + 1, EPG):
                        tt_(wk[0], e[j], e[i], ALU.is_gt)
                        tt_(r4[:, :, i], r4[:, :, i], wk[0], ALU.add)
                        dve.tensor_scalar(wk[1], wk[0], -1.0, 1.0, ALU.mult, ALU.add)
                        dve.drain()
                        tt_(r4[:, :, j], r4[:, :, j], wk[1], ALU.add)
                dve.tensor_scalar(rank[:, :, :, :], rank[:, :, :, :], TOPK - 0.5, None, ALU.is_lt)
                dve.drain()
                c4 = chosen[:, :, :].rearrange("p t (g e) -> p (t g) e", g=EGROUPS)
                tt_(c4, r4, wk[5].unsqueeze(2).broadcast_to([P, G, EPG]), ALU.mult)
                dve.sem_inc(picked, 1)
                tt_(r4, c4, s4, ALU.mult)
                dve.tensor_reduce(top[:, 2, :], rank[:, :, :, :].rearrange("p t g e -> p t (g e)"), AX.X, ALU.add)
                dve.drain()
                dve.reciprocal(top[:, 3, :], top[:, 2, :])
                dve.drain()
                tt_(comb[:, :, :], rank[:, :, :, :].rearrange("p t g e -> p t (g e)"),
                    top[:, 3, :].unsqueeze(2).broadcast_to([P, tt_n, EXPERTS]), ALU.mult)
                dve.wait_ge(placed, 1)
                upto = k.ps[:, NORM_BANK, 0:tt_n * EXPERTS].rearrange("p (t e) -> p t e", e=EXPERTS)
                tt_(place[:, :, :], upto, chosen[:, :, :], ALU.mult)
                dve.tensor_scalar(late[:, :, :], place[:, :, :], P + 0.5, None, ALU.is_gt)
                dve.tensor_scalar(place[:, :, :], place[:, :, :], -1.0, None, ALU.add)
                dve.tensor_reduce(top[:, 0, 0:1], k.ps[:, NORM_BANK, tt_n * EXPERTS:(tt_n + 1) * EXPERTS], AX.X, ALU.max)
                dve.drain()
                dve.tensor_copy(most[:, :], top[:, 0, 0:1])
                tt_(late[:, :, :], late[:, :, :], comb[:, :, :], ALU.mult)


def moe_experts(k, x, segs, gate, name, n, tt_n, first, comb, place, rows, slot_number):
    nc = k.nc
    with ExitStack() as local:
        def sb(nm, shape, dtype=F32):
            return local.enter_context(nc.sbuf_tensor(f"{name}_{nm}", shape, dtype))

        onehot = sb("onehot", [P, 2, tt_n, P])
        turned_hot = sb("turned_hot", [P, n])
        own = sb("own", [P, KD, P])
        act_g = sb("act_g", [P, 2, P])
        hid = sb("hid", [P, KE, P])
        slot_w = sb("slot_w", [P, 1])
        y = sb("y", [P, D])
        GATHER, DOWN, SCATTER = 2, 4, 6
        PRE = 2
        with stage_semaphores(nc, f"{name}_experts", "selected", "gathered", "own_made", "product", "gated", "hidden", "turned",
                              "turned_kept", "weighed", "weight_kept", "down", "scaled", "scattered", "added"
                              ) as sems, nc.Block(name=f"{name}_experts", no_gpsimd_drain=True) as block:
            (selected, gathered, own_made, product, gated, hidden, turned, turned_kept, weighed, weight_kept, down, scaled,
             scattered, added) = sems

            def rounds(engine, expert):
                for s in range(2):
                    expert(s, s, s == 0, False)
                with engine.Fori(1, EXPERTS // 2 - 1) as i:
                    for s in range(2):
                        expert(i * 2 + s, s, False, False)
                for s in range(2):
                    expert(EXPERTS - 2 + s, s, False, s == 1)

            @block.sync
            def _(sp):
                count = EXPERTS if first + EXPERTS * RING + RING <= k.n_slots else EXPERTS - 1

                def one(s, e):
                    if s < 2 * KE:
                        sp.wait_ge(product, e * KE + s // 2 + 1)
                    else:
                        sp.wait_ge(down, e * KE + s - 2 * KE + 1)
                    at = (first + s) % RING
                    sp.dma_start(k.ring[:, at], k.weights[first + s + RING + e * RING]).then_inc(k.landed[at], 16)

                with sp.Fori(0, count) as e:
                    for s in range(RING):
                        one(s, e)
                if count < EXPERTS:
                    for s in range(k.n_slots - first - EXPERTS * RING):
                        one(s, EXPERTS - 1)

            @block.tensor
            def _(pe):
                def gather(e, s, first_one=False):
                    pe.wait_ge(selected, e + 1)
                    for half in range(2):
                        if not first_one:
                            pe.wait_ge(own_made, e * 2 + half - 1)
                        for f in range(4):
                            t = half * 4 + f
                            for tt in range(tt_n):
                                mm = pe.matmul(k.ps[:, GATHER + half, f * P:(f + 1) * P], rows[:, tt, t * P:(t + 1) * P],
                                               onehot[:, s, tt, :], start=(tt == 0), stop=(tt == tt_n - 1))
                        mm.then_inc(gathered, 1)

                def scatter(e):
                    pe.wait_ge(scaled, e * 2 + 2)
                    pe.wait_ge(turned_kept, e + 1)
                    for m in range(KD):
                        pe.wait_ge(added, e * KD + m + 1)
                        pe.matmul(k.ps[:, SCATTER + m % 2, 0:n], y[:, m * P:(m + 1) * P], turned_hot[:, :],
                                  start=True, stop=True).then_inc(scattered, 1)

                def expert(e, s, start, end):
                    pe.wait_ge(own_made, e * 2 + 2)
                    for m in range(KE):
                        pe.wait_ge(hidden, e * KE + m + 1)
                        if not start and m == 0:
                            pe.wait_ge(turned_kept, e)
                        if not start and m == 1:
                            pe.wait_ge(weight_kept, e)
                        for half in range(2):
                            w = k.slot(pe, first + 2 * m + half, e)
                            for t in range(KD):
                                mm = pe.matmul(k.ps[:, m % 2, half * P:(half + 1) * P], w[:, t, :], own[:, t, :],
                                               start=(t == 0), stop=(t == KD - 1))
                        mm.then_inc(product, 1)
                    if not start:
                        scatter(e - 1)
                    pe.wait_ge(hidden, e * KE + KE - 1 + PRE)
                    for tt in range(tt_n):
                        mm = pe.transpose(k.ps[:, 0, tt * P:(tt + 1) * P], onehot[:, s, tt, :], k.ident[:, :])
                    mm.then_inc(turned, 1)
                    pe.wait_ge(hidden, e * KE + KE + PRE)
                    for tt in range(tt_n):
                        mm = pe.matmul(k.ps[:, 1, 0:1], onehot[:, s, tt, :], comb[:, tt, bass.ds(e, 1)],
                                       start=(tt == 0), stop=(tt == tt_n - 1))
                    mm.then_inc(weighed, 1)
                    if not end:
                        gather(e + 1, 1 - s)
                    if not start:
                        pe.wait_ge(scaled, e * 2)
                    for t in range(KE):
                        w = k.slot(pe, first + 2 * KE + t, e)
                        for half in range(2):
                            mm = pe.matmul(k.ps[:, DOWN + half, :], hid[:, t, :],
                                           w[:, half * 4:(half + 1) * 4, :].rearrange("p a f -> p (a f)"),
                                           start=(t == 0), stop=(t == KE - 1))
                        mm.then_inc(down, 1)

                gather(0, 0, True)
                rounds(pe, expert)
                scatter(EXPERTS - 1)

            @block.scalar
            def _(act):
                def keep_own(e):
                    for half in range(2):
                        act.wait_ge(gathered, e * 2 + half + 1)
                        act.copy(own[:, half * 4:(half + 1) * 4, :].rearrange("p a f -> p (a f)"), k.ps[:, GATHER + half, :]
                                 ).then_inc(own_made, 1)

                def expert(e, s, start, end):
                    for m in range(KE):
                        act.wait_ge(product, e * KE + m + 1)
                        act.wait_ge(hidden, e * KE + m + 1)
                        act.activation(act_g[:, m % 2, :], k.ps[:, m % 2, 0:P], ACT.Silu).then_inc(gated, 1)
                    act.wait_ge(turned, e + 1)
                    act.copy(turned_hot[:, :], k.ps[:, 0, 0:n]).then_inc(turned_kept, 1)
                    act.wait_ge(weighed, e + 1)
                    act.copy(slot_w[:, :], k.ps[:, 1, 0:1]).then_inc(weight_kept, 1)
                    if not end:
                        keep_own(e + 1)
                    act.wait_ge(weight_kept, e + 1)
                    act.wait_ge(down, e * KE + KE)
                    for half in range(2):
                        act.mul(y[:, half * 512:(half + 1) * 512], k.ps[:, DOWN + half, :], slot_w[:, 0:1]).then_inc(scaled, 1)

                keep_own(0)
                rounds(act, expert)

            @block.vector
            def _(dve):
                def select(e, s):
                    for tt in range(tt_n):
                        ts = dve.tensor_scalar(onehot[:, s, tt, :], slot_number, place[:, tt, bass.ds(e, 1)], None, ALU.is_equal)
                    ts.then_inc(selected, 1)

                def add(e):
                    for m in range(KD):
                        dve.wait_ge(scattered, e * KD + m + 1)
                        for j, s in enumerate(segs):
                            xs = x[:, m, s * T:(s + 1) * T]
                            ad = dve.scalar_tensor_tensor(xs, k.ps[:, SCATTER + m % 2, j * T:(j + 1) * T], gate[:, m, s:s + 1], xs,
                                                          ALU.mult, ALU.add)
                        ad.then_inc(added, 1)

                def expert(e, s, start, end):
                    if not end:
                        if not start:
                            dve.wait_ge(weighed, e)
                        select(e + 1, 1 - s)
                    for m in range(KE):
                        dve.wait_ge(gated, e * KE + m + 1)
                        dve.tensor_tensor(hid[:, m, :], act_g[:, m % 2, :], k.ps[:, m % 2, P:2 * P], ALU.mult).then_inc(hidden, 1)
                    if not start:
                        add(e - 1)

                dve.sem_inc(hidden, PRE)
                dve.sem_inc(added, PRE)
                select(0, 0)
                rounds(dve, expert)
                add(EXPERTS - 1)


def moe_late(k, x, segs, gate, name, n, tt_n, first, late, fullest):
    nc = k.nc
    with ExitStack() as local:
        def sb(nm, shape):
            return local.enter_context(nc.sbuf_tensor(f"{name}_{nm}", shape, F32))

        own_w = sb("weights", [P, RING, TILES, P])
        diag = sb("diag", [P, tt_n, P])
        hid = sb("hid", [P, KE, n])
        act_g = sb("act_g", [P, 2, n])
        with stage_semaphores(nc, name, "read", "spread", "diag_made", "product", "gated", "hidden", "down", "added"
                              ) as sems, nc.Block(name=name, no_gpsimd_drain=True) as block:
            read, spread, diag_made, product, gated, hidden, down, added = sems
            PRE = 2

            @block.sync
            def _(sp):
                with sp.If(fullest > P):
                    sp.sem_inc(down, KD)
                    with sp.Fori(0, EXPERTS) as e:
                        sp.wait_ge(down, e * KD + KD)
                        for s in range(RING):
                            sp.dma_start(own_w[:, s], k.weights[first + s + e * RING]).then_inc(read, 16)

            @block.tensor
            def _(pe):
                with pe.If(fullest > P):
                    with pe.Fori(0, EXPERTS) as e:
                        pe.wait_ge(read, e * (16 * RING) + 16 * RING)
                        for m in range(KE):
                            pe.wait_ge(hidden, e * KE + m + 1)
                            for half in range(2):
                                for t in range(KD):
                                    mm = pe.matmul(k.ps[:, m % 2 + 2 * half, 0:n], own_w[:, 2 * m + half, t, :], k.h[:, t, 0:n],
                                                   start=(t == 0), stop=(t == KD - 1))
                            mm.then_inc(product, 1)
                            if m == 0:
                                pe.wait_ge(diag_made, e + 1)
                                for tt in range(tt_n):
                                    mm = pe.matmul(k.ps[:, 6, tt * P:(tt + 1) * P], k.ones[:, :], diag[:, tt, :], start=True, stop=True)
                                mm.then_inc(spread, 1)
                        pe.wait_ge(hidden, e * KE + KE + PRE)
                        for m in range(KD):
                            pe.wait_ge(added, e * KD + m + 1)
                            for t in range(KE):
                                mm = pe.matmul(k.ps[:, 4 + m % 2, 0:n], own_w[:, 2 * KE + t, m, :], hid[:, t, :],
                                               start=(t == 0), stop=(t == KE - 1))
                            mm.then_inc(down, 1)

            @block.scalar
            def _(act):
                with act.If(fullest > P):
                    with act.Fori(0, EXPERTS) as e:
                        for m in range(KE):
                            act.wait_ge(product, e * KE + m + 1)
                            act.wait_ge(hidden, e * KE + m + 1)
                            act.activation(act_g[:, m % 2, :], k.ps[:, m % 2, 0:n], ACT.Silu).then_inc(gated, 1)

            @block.vector
            def _(dve):
                with dve.If(fullest > P):
                    dve.sem_inc(hidden, PRE)
                    dve.sem_inc(added, PRE)
                    with dve.Fori(0, EXPERTS) as ex:
                        for tt in range(tt_n):
                            dg = dve.tensor_scalar(diag[:, tt, :], k.ident[:, :], late[:, tt, bass.ds(ex, 1)], None, ALU.mult)
                        dg.then_inc(diag_made, 1)
                        for m in range(KE):
                            dve.wait_ge(gated, ex * KE + m + 1)
                            dve.tensor_tensor(act_g[:, m % 2, :], act_g[:, m % 2, :], k.ps[:, m % 2 + 2, 0:n], ALU.mult)
                            dve.drain()
                            if m == 0:
                                dve.wait_ge(spread, ex + 1)
                            dve.tensor_tensor(hid[:, m, :], act_g[:, m % 2, :], k.ps[:, 6, 0:n], ALU.mult).then_inc(hidden, 1)
                        for m in range(KD):
                            dve.wait_ge(down, ex * KD + m + 1 + KD)
                            for j, s in enumerate(segs):
                                xs = x[:, m, s * T:(s + 1) * T]
                                ad = dve.scalar_tensor_tensor(xs, k.ps[:, 4 + m % 2, j * T:(j + 1) * T], gate[:, m, s:s + 1], xs,
                                                              ALU.mult, ALU.add)
                            ad.then_inc(added, 1)


def odd_mixer(k, x, col, gain, shift, gate, hmask, reset):
    nc = k.nc
    q_slots, g_slots, v_slots, f_slots, o_slots = k.take(8), k.take(8), k.take(8), k.take(16), k.take(8)
    H = k.sq
    outer = ExitStack()
    with outer:
        def sb(name, shape):
            return outer.enter_context(nc.sbuf_tensor(name, shape, F32))

        q = sb("hg_q", [P, GH, T])
        sg = sb("hg_g", [P, GH, T])
        v = sb("hg_v", [P, TT, GH * P])
        f = sb("hg_f", [P, 2, GH, T2])
        lb = sb("hg_lbs", [P, 3, GH])
        o = q
        lb_in = col("hg_lb")
        with stage_semaphores(nc, "odd_in", *NORM_SEMS, "made", "ready", "product", "kept", "v_used", "v_kept", "lb1", "lb2",
                              "lb_done", "forgot") as sems, nc.Block(name="odd_in", no_gpsimd_drain=True) as block:
            norm, (made, ready, product, kept, v_used, v_kept, lb1, lb2, lb_done, forgot) = sems[:4], sems[4:]

            @block.sync
            def _(sp):
                k.refill(sp, q_slots, 16, product)
                k.refill(sp, v_slots, 7, v_used)
                k.refill(sp, v_slots + 7, 1, product, mult=8, base=16)
                k.refill(sp, f_slots, 16, product, base=24)

            @block.tensor
            def _(pe):
                norm_tensor(k, pe, norm, T2)
                pe.wait_ge(ready, KD * SEGS)
                for m in range(16):
                    if m >= 4:
                        pe.wait_ge(kept, m - 3)
                    w = k.slot(pe, q_slots + m)
                    for t in range(KD):
                        mm = pe.matmul(k.ps[:, m % 4, 0:T], w[:, t, :], H[:, t, T:T2], start=(t == 0), stop=(t == KD - 1))
                    mm.then_inc(product, 1)
                pe.wait_ge(kept, 16)
                for t in range(KD):
                    w = k.slot(pe, v_slots + t).rearrange("p (a b) c -> p a (b c)", a=2)
                    for tt in range(TT):
                        for half in range(2):
                            mm = pe.matmul(k.ps[:, tt * 2 + half, :], H[:, t, tt * P:(tt + 1) * P], w[:, half, :],
                                           start=(t == 0), stop=(t == KD - 1))
                            if t == KD - 1:
                                mm.then_inc(product, 1)
                    if t < KD - 1:
                        mm.then_inc(v_used, 1)
                for m in range(16):
                    if m < 4:
                        pe.wait_ge(kept, 16 + m + 1)
                    else:
                        pe.wait_ge(kept, 24 + m - 3)
                    w = k.slot(pe, f_slots + m)
                    for t in range(KD):
                        mm = pe.matmul(k.ps[:, m % 4, :], w[:, t, :], H[:, t, :], start=(t == 0), stop=(t == KD - 1))
                    mm.then_inc(product, 1)

            @block.scalar
            def _(act):
                norm_scalar(k, act, norm, x, T2)
                act.wait_ge(norm[1], 1)
                mod_norm_shift(k, act, (0, 1), shift, made, ready, col_major=True)
                act.wait_ge(lb1, 1)
                act.activation(lb[:, 0:2, :], lb[:, 0:2, :], ACT.Exp).then_inc(lb2, 1)
                for m in range(16):
                    act.wait_ge(product, m + 1)
                    act.activation((q if m < 8 else sg)[:, m % 8, :], k.ps[:, m % 4, 0:T], ACT.Silu).then_inc(kept, 1)
                for n in range(8):
                    act.wait_ge(product, 16 + n + 1)
                    act.activation(v[:, n // 2, n % 2 * 512:(n % 2 + 1) * 512], k.ps[:, n, :], ACT.Copy).then_inc(kept, 1)
                for m in range(16):
                    act.wait_ge(product, 24 + m + 1)
                    act.activation(f[:, m // 8, m % 8, :], k.ps[:, m % 4, :], ACT.Sigmoid).then_inc(kept, 1)

            @block.vector
            def _(dve):
                dve.tensor_tensor(lb[:, 2, :], lb_in[:, 0:GH], lb_in[:, GH:], ALU.max)
                dve.drain()
                for i in range(2):
                    lw = dve.tensor_tensor(lb[:, i, :], lb_in[:, i * GH:(i + 1) * GH], lb[:, 2, :], ALU.subtract)
                lw.then_inc(lb1, 1)
                mod_norm_vector(k, dve, norm, x, (0, 1), gain, T2, made)
                dve.wait_ge(lb2, 1)
                dve.tensor_tensor(lb[:, 2, :], lb[:, 0, :], lb[:, 1, :], ALU.add)
                dve.drain()
                dve.reciprocal(lb[:, 2, :], lb[:, 2, :])
                dve.drain()
                dve.tensor_tensor(lb[:, 0, :], lb[:, 1, :], lb[:, 2, :], ALU.mult)
                dve.drain()
                dve.tensor_scalar(lb[:, 1, :], lb[:, 0, :], -1.0, 1.0, ALU.mult, ALU.add)
                dve.drain()
                for m in range(16):
                    dve.wait_ge(kept, 24 + m + 1)
                    ff = f[:, m // 8, m % 8, :]
                    dve.tensor_scalar(ff, ff, lb[:, 1, m % 8:m % 8 + 1], lb[:, 0, m % 8:m % 8 + 1], ALU.mult, ALU.add)

        lf = (k.h, k.sq)
        with nc.Block(name="log_forget", no_gpsimd_drain=True) as block:

            @block.scalar
            def _(act):
                for d in range(2):
                    act.activation(lf[d][:, :, :], f[:, d], ACT.Ln)

        with ExitStack() as local:
            def tb(name, shape):
                return local.enter_context(nc.sbuf_tensor(name, shape, F32))

            vh = x[:, 0:2, 0:T].rearrange("p a (b v) -> p a b v", b=2)
            g = tb("g_cum", [P, 2, T2])
            ke = tb("k_end", [P, 2, T2])
            kx = (k.root, k.rstd)
            rel = tb("rel", [P, 2, 5, T])
            QM, KM, QB, KB, QS = range(5)
            HC = GC // 2
            dec = tb("dec", [P, 2, 2 * NCH])
            ket = tb("k_end_tok", [P, 2, TT, P])
            att = tb("att", [P, 2, 2, P])
            sin = tb("s_in", [P, 2, NCH + 1, P])
            with stage_semaphores(nc, "hgrn", "cleared", "cum", "exps", "rels", "kends", "turned", "turn_kept", "atts",
                                  "att_kept", "states", "chained", "summed", "kept") as sems, \
                    nc.Block(name="hgrn_scan", no_gpsimd_drain=True) as block:
                cleared, cum, exps, rels, kends, turned, turn_kept, atts, att_kept, states, chained, summed, kept = sems

                def order(d):
                    ctx_ch = list(range(NCH))
                    lat_ch = list(range(NCH, 2 * NCH))
                    return (ctx_ch + lat_ch) if d == 0 else (ctx_ch[::-1] + lat_ch[::-1])

                @block.vector
                def _(dve):
                    dve.memset(att[:, :, :, :], 0.0)
                    dve.memset(sin[:, :, :, :], 0.0)
                    dve.sem_inc(turned, 2)
                    dve.sem_inc(summed, 1)
                    with dve.Fori(0, GH) as h:
                        dve.drain()
                        dve.wait_ge(summed, h * 2 + 1)
                        dve.tensor_copy(vh, v[:, :, bass.ds(h * P, P)].rearrange("p (a b) v -> p a b v", b=2))
                        for d in range(2):
                            u = h * 2 + d
                            gg, L = g[:, d, :], lf[d][:, bass.ds(h, 1), :].rearrange("p a t -> p (a t)")
                            F = f[:, d, bass.ds(h, 1), :].rearrange("p a t -> p (a t)")
                            dve.tensor_tensor_scan(gg, reset, L, 0.0, ALU.mult, ALU.add)
                            dve.tensor_scalar(kx[d][:, :], F, -1.0, 1.0, ALU.mult, ALU.add)
                            dve.drain()
                            chunks = gg.rearrange("p (c t) -> p c t", t=GC)
                            dve.tensor_copy(dec[:, d, :], chunks[:, :, GC - 1])
                            dve.drain()
                            end = dec[:, d, :].unsqueeze(2).broadcast_to([P, 2 * NCH, GC])
                            if d == 0:
                                dve.tensor_tensor(ke[:, d, :].rearrange("p (c t) -> p c t", t=GC), end, chunks, ALU.subtract)
                                mid, edge = HC // 2 - 1, HC - 1
                            else:
                                dve.tensor_tensor(ke[:, d, :], gg, L, ALU.subtract)
                                dve.drain()
                                dve.tensor_tensor(chunks, end, ke[:, d, :].rearrange("p (c t) -> p c t", t=GC), ALU.subtract)
                                dve.drain()
                                mid, edge = HC // 2, HC
                            lat = gg[:, T:].rearrange("p (c t) -> p c t", t=GC)
                            for q_at, k_at, size, ref in ((QM, KM, HC, mid), (QB, KB, GC, edge)):
                                own = gg[:, T:].rearrange("p (c t) -> p c t", t=size)
                                refs = own[:, :, ref:ref + 1].broadcast_to([P, T // size, size])
                                rq, rk = [rel[:, d, i, :].rearrange("p (c t) -> p c t", t=size) for i in (q_at, k_at)]
                                dve.tensor_tensor(rq, own, refs, ALU.subtract)
                                dve.tensor_tensor(rk, refs, own, ALU.subtract)
                            dve.drain()
                            dve.tensor_scalar(rel[:, d, QB:KB + 1, :], rel[:, d, QB:KB + 1, :], 0.0, None, ALU.min)
                            dve.tensor_copy(rel[:, d, QS, :], gg[:, T:]).then_inc(cum, 1)
                        for d in range(2):
                            u = h * 2 + d
                            dve.wait_ge(exps, u + 1)
                            dve.tensor_tensor(ke[:, d, :], ke[:, d, :], kx[d][:, :], ALU.mult).then_inc(kends, 1)
                            qh = q[:, bass.ds(h, 1), :].rearrange("p a t -> p (a t)")
                            for i, by in ((QM, qh), (QB, qh), (QS, qh), (KM, kx[d][:, T:]), (KB, kx[d][:, T:])):
                                last = dve.tensor_tensor(rel[:, d, i, :], rel[:, d, i, :], by, ALU.mult)
                            last.then_inc(rels, 1)
                        for d in range(2):
                            u = h * 2 + d
                            dve.wait_ge(states, u + 1)
                            od = order(d)
                            for i, c in enumerate(od[:-1]):
                                if i == 1:
                                    for j in range(2):
                                        if j:
                                            dve.drain()
                                        cp = dve.copy_predicated(
                                            att[:, d], hmask[:, 2 * j + d, :].bitcast(I32).unsqueeze(1).broadcast_to([P, 2, P]),
                                            k.ps[:, 1, 2 * j * P:2 * (j + 1) * P].rearrange("p (a l) -> p a l", a=2))
                                    cp.then_inc(att_kept, 1)
                                if i:
                                    dve.drain()
                                src = sin[:, d, 0, :] if i < NCH else sin[:, d, 1 + i - NCH, :]
                                dst = sin[:, d, 0, :] if i < NCH - 1 else sin[:, d, 1 + i + 1 - NCH, :]
                                cs_ = k.ps[:, 2 + c % 2, c // 2 * P:(c // 2 + 1) * P]
                                if i == 0:
                                    ch = dve.tensor_copy(dst, cs_)
                                else:
                                    ch = dve.scalar_tensor_tensor(dst, src, dec[:, d, c:c + 1], cs_, ALU.mult, ALU.add)
                            ch.then_inc(chained, 1)

                @block.scalar
                def _(act):
                    with act.Fori(0, GH) as h:
                        for d in range(2):
                            u = h * 2 + d
                            act.wait_ge(cum, u + 1)
                            act.activation(ke[:, d, :], ke[:, d, :], ACT.Exp)
                            act.activation(dec[:, d, :], dec[:, d, :], ACT.Exp)
                            act.activation(rel[:, d].rearrange("p i t -> p (i t)"), rel[:, d].rearrange("p i t -> p (i t)"),
                                           ACT.Exp).then_inc(exps, 1)
                        for d in range(2):
                            u = h * 2 + d
                            act.wait_ge(turned, u + 3)
                            act.activation(ket[:, d].rearrange("p a k -> p (a k)"), k.ps[:, 0, :], ACT.Copy).then_inc(turn_kept, 1)
                        act.wait_ge(summed, h * 2 + 3)
                        act.activation(o[:, bass.ds(h, 1), :].rearrange("p a t -> p (a t)"), k.ps[:, 6, 0:T], ACT.Copy
                                       ).then_inc(kept, 1)

                @block.tensor
                def _(pe):
                    with pe.Fori(0, GH) as h:
                        for d in range(2):
                            u = h * 2 + d
                            pe.wait_ge(kends, u + 1)
                            if d:
                                pe.wait_ge(turn_kept, u)
                            for a in range(TT):
                                mm = pe.transpose(k.ps[:, 0, a * P:(a + 1) * P], ke[:, d, a * P:(a + 1) * P], k.ident[:, :])
                            mm.then_inc(turned, 1)
                            pe.wait_ge(rels, u + 1)
                            if d:
                                pe.wait_ge(chained, u)
                            for j, (q_at, k_at) in enumerate(((QM, KM), (QB, KB))):
                                for a in range(2):
                                    mm = pe.matmul(k.ps[:, 1, (2 * j + a) * P:(2 * j + a + 1) * P],
                                                   rel[:, d, k_at, a * P:(a + 1) * P], rel[:, d, q_at, a * P:(a + 1) * P],
                                                   start=True, stop=True)
                            mm.then_inc(atts, 1)
                            pe.wait_ge(turn_kept, u + 1)
                            for i, c in enumerate(order(d)[:-1]):
                                a, r = c // 2, c % 2 * GC
                                mm = pe.matmul(k.ps[:, 2 + c % 2, c // 2 * P:(c // 2 + 1) * P], ket[r:r + GC, d, a, :],
                                               vh[r:r + GC, a // 2, a % 2, :], start=True, stop=True)
                            mm.then_inc(states, 1)
                            pe.wait_ge(att_kept, u + 1)
                            for a in range(2):
                                pe.matmul(k.ps[:, 6, a * P:(a + 1) * P], vh[:, 1, a, :], att[:, d, a, :],
                                          start=(d == 0 and a == 0), stop=False, skip_group_check=True)
                            pe.wait_ge(chained, u + 1)
                            for i, c in enumerate(order(d)[NCH:]):
                                cc = c - NCH
                                mm = pe.matmul(k.ps[:, 6, cc * GC:(cc + 1) * GC], sin[:, d, 1 + i, :],
                                               rel[:, d, QS, cc * GC:(cc + 1) * GC], start=False, stop=(d == 1 and i == NCH - 1),
                                               skip_group_check=True)
                            mm.then_inc(summed, 1)

        with stage_semaphores(nc, "hg_out", "squared", "summed", "rooted", "normed", "product") as sems, \
                nc.Block(name="hgrn_readout", no_gpsimd_drain=True) as block:
            squared, summed, rooted, normed, product = sems
            oo = o[:, :, :].rearrange("p (a b) t -> p a (b t)", b=2)
            gg = sg[:, :, :].rearrange("p (a b) t -> p a (b t)", b=2)

            @block.sync
            def _(sp):
                k.refill(sp, o_slots, 8, product)

            @block.scalar
            def _(act):
                for a in range(4):
                    act.activation(k.sq[:, a, :], oo[:, a, :], ACT.Square).then_inc(squared, 1)
                for a in range(4):
                    act.wait_ge(summed, a + 1)
                    act.activation(k.sq[:, 4 + a, :], k.ps[:, a, :], ACT.Sqrt, scale=1.0 / P, bias=k.eps[:, 0:1]).then_inc(rooted, 1)

            @block.tensor
            def _(pe):
                for a in range(4):
                    pe.wait_ge(squared, a + 1)
                    pe.matmul(k.ps[:, a, :], k.ones[:, :], k.sq[:, a, :], start=True, stop=True).then_inc(summed, 1)
                pe.wait_ge(normed, 4)
                for m in range(KD):
                    w = k.slot(pe, o_slots + m)
                    for t in range(KD):
                        mm = pe.matmul(k.ps[:, m, 0:T], w[:, t, :], o[:, t, :], start=(t == 0), stop=(t == KD - 1))
                    mm.then_inc(product, 1)

            @block.vector
            def _(dve):
                for a in range(4):
                    dve.wait_ge(rooted, a + 1)
                    dve.reciprocal(k.sq[:, 4 + a, :], k.sq[:, 4 + a, :])
                    dve.drain()
                    dve.scalar_tensor_tensor(oo[:, a, :], oo[:, a, :], col("hg_norm_g"), k.sq[:, 4 + a, :], ALU.mult, ALU.mult)
                    dve.drain()
                    dve.tensor_tensor(oo[:, a, :], oo[:, a, :], gg[:, a, :], ALU.mult).then_inc(normed, 1)
                for m in range(KD):
                    dve.wait_ge(product, m + 1)
                    xs = x[:, m, T:T2].rearrange("p (r w) -> p r w", r=ROWS)
                    dve.scalar_tensor_tensor(xs, k.ps[:, m, 0:T].rearrange("p (w r) -> p r w", r=ROWS), gate[:, m, 1:2], xs,
                                             ALU.mult, ALU.add)


def second_block_stream(a):
    out = [out_tiles(a["mod_w_2"][i]) for i in range(2)]
    w = a["ab_w_in_2"][0]
    xbc0, dt0 = SH * SP_, SH * SP_ + XBC * P
    cf0 = dt0 + 2 * SH
    tiles = out_tiles(np.concatenate([w[:, :dt0], w[:, cf0:]], axis=1))
    v0, g0 = 8 + XBC, 8 + XBC + 8
    order = [i for m in range(8) for i in (v0 + m, g0 + m)] + list(range(8 + XBC))
    out.append(tiles[order])
    out.append(out_tiles(a["ab_w_out_2"][0]))

    def experts(i):
        g = a["moe_w_gate_2"][i].reshape(EXPERTS, KD, P, KE, P)
        u = a["moe_w_up_2"][i].reshape(EXPERTS, KD, P, KE, P)
        gu = np.stack([g, u], axis=4)
        gu = gu.transpose(0, 3, 4, 2, 1, 5).reshape(EXPERTS, 2 * KE, P, TILES * P)
        dn = a["moe_w_down_2"][i].reshape(EXPERTS, KE, P, TILES * P)
        return np.concatenate([gu, dn], axis=1).reshape(-1, P, TILES * P)

    out.append(experts(0))
    w = a["hg_w_in_2"][0]
    kd = GH * P
    out.append(out_tiles(w[:, :2 * kd]))
    out.append(w[:, 2 * kd:3 * kd].reshape(KD, P, kd))
    out.append(out_tiles(w[:, 3 * kd:]))
    out.append(out_tiles(a["hg_w_out_2"][0]))
    out.append(experts(1))
    return out


def second_block_cols(a, cl, at):
    def put(name, arr):
        at[name] = (sum(c.shape[1] for c in cl), arr.shape[1])
        cl.append(arr)

    def spread(row):
        return np.broadcast_to(np.asarray(row).reshape(1, -1), (P, np.asarray(row).size))

    put("cond", np.stack([a["c_ctx_2"], a["c_2"][0]], -1).reshape(KD, P, 2).transpose(1, 0, 2).reshape(P, -1))
    put("mod_b", np.concatenate([cols(a["mod_b_2"][i]) for i in range(2)], 1))
    put("mix_g", np.concatenate([cols(a["norm_mix_g_2"][i]) for i in range(2)], 1))
    put("ffn_g", np.concatenate([cols(a["norm_ffn_g_2"][i]) for i in range(2)], 1))
    put("router_w", a["router_w_2"].reshape(KD, P, EXPERTS).transpose(1, 0, 2).reshape(P, -1))
    put("router_b", spread(a["router_b_2"]))
    taps = np.concatenate([a["ssd_conv_w_2"][0], a["ssd_conv_b_2"]], 0)
    put("ssd_taps", taps.reshape(SCONV + 1, XBC, P).transpose(2, 1, 0).reshape(P, -1))
    taps = np.concatenate([a["cf_dw_w_2"][0], a["cf_dw_b_2"]], 0)
    put("cf_taps", taps.reshape(CFK + 1, KD, P).transpose(2, 1, 0).reshape(P, -1))
    dt0 = SH * SP_ + XBC * P
    put("dt_w", a["ab_w_in_2"][0][:, dt0:dt0 + 2 * SH].reshape(KD, P, 2 * SH).transpose(1, 0, 2).reshape(P, -1))
    put("dt_bias", spread(a["ssd_dt_bias_2"][0]))
    put("a_log", spread(a["ssd_a_log_2"][0]))
    put("ssd_d", spread(a["ssd_d_2"][0]))
    put("ssd_norm_g", cols(a["ssd_norm_g_2"][0]))
    put("ln_g", cols(a["cf_ln_g_2"][0]))
    put("ln_b", cols(a["cf_ln_b_2"][0]))
    put("hg_lb", np.concatenate([cols(a["hg_lb_2"][i]) for i in range(2)], 1))
    put("hg_norm_g", cols(a["hg_norm_g_2"][0]))
    put("final_g", cols(a["final_norm_g_2"]))


def second_block_shape_constants():
    i = np.arange(P)
    tri0 = (i[:, None] <= i[None]).astype(np.float32)
    half = i // (GC // 2)
    near = half[:, None] == half[None]
    same = (i[:, None] // GC == i[None] // GC) & ~near
    reset = (np.arange(T2) % GC != 0).astype(np.float32)
    return np.concatenate([tri0, tri0.T, tri0 * near, tri0.T * near, tri0 * same, tri0.T * same, np.broadcast_to(reset, (P, T2)),
                           np.broadcast_to(i.astype(np.float32), (P, P))], 1)


def second_block(k, x, col, tri, hmask, reset, slot_number, stop=None):
    k.upto = tri[:, 0, :]
    mods = k.sb("mods", [P, 2, N_MOD * KD, 2])
    gains = k.sb("gains", [P, 2, 2, KD, 2])
    modulation(k, col("cond").rearrange("p (t s) -> p t s", s=2), col("mod_b"), mods)
    scaled_gains(k, mods, (col("mix_g"), col("ffn_g")), gains)

    def part(layer, i):
        return mods[:, layer, i * KD:(i + 1) * KD, :]

    router_w = col("router_w").rearrange("p (t e) -> p t e", t=KD)
    with ExitStack() as local:
        def sb(name, shape):
            return local.enter_context(k.nc.sbuf_tensor(name, shape, F32))

        zs = sb("zs", [P, KD, T2])
        cf = sb("cf", [P, KD, T2])
        dt = sb("dt", [P, TT, 2 * SH])
        with k.nc.sbuf_tensor("xbc", [P, XBC, T2], F32) as xbc:
            even_in(k, x, col, gains[:, 0, 0], part(0, 0), zs, xbc, cf, dt)
            ssd(k, col, tri, dt, zs, xbc)
        conformer_norm(k, cf, col("ln_g"), col("ln_b"))
        even_out(k, x, zs, cf, part(0, 2))
    if stop == "mix0":
        return
    moe(k, x, (0, 1), gains[:, 0, 1], part(0, 3), part(0, 5), router_w, col("router_b"), slot_number, "moe0")
    if stop == "moe0":
        return
    odd_mixer(k, x, col, gains[:, 1, 0], part(1, 0), part(1, 2), hmask, reset)
    if stop == "mix1":
        return
    moe(k, x, (1,), gains[:, 1, 1], part(1, 3), part(1, 5), router_w, col("router_b"), slot_number, "moe1")


def build_program(nc, ins, out, n_slots, col_at):
    with ExitStack() as ctx:
        k = Kit(nc, ctx, ins["weights"], n_slots)
        stored = ctx.enter_context(nc.semaphore("stored"))
        both = k.sb("both", [P, KD, T2])
        small = k.sb("cols", [P, ins["cols"].shape[1]])
        masks = k.sb("masks", [P, 7 * P + T2])
        rope = k.sb("rope", [P, 1 + ROT])
        x = both[:, :, T:T2]
        tri = masks[:, 0:2 * P].rearrange("p (d l) -> p d l", d=2)
        hmask = masks[:, 2 * P:6 * P].rearrange("p (d l) -> p d l", d=4)
        reset = masks[:, 6 * P:6 * P + T2]
        slot_number = masks[:, 6 * P + T2:]

        def col(name):
            at, n = col_at[name]
            return small[:, at:at + n]

        def taps(i):
            return col(f"taps{i}").rearrange("p (t f) -> p t f", f=4)

        constants(k, [(x, ins["x"]), (both[:, :, 0:T], ins["context"]), (small[:, :], ins["cols"]),
                      (masks[:, :], ins["masks"]), (rope[:, :], ins["rope"])])
        pool_mixer(k, x, col("norm_mix0"), col("pool_scale"), ins["rcount"])
        conv_ffn(k, x, col("norm_ffn0"), taps(0), "ffn0")
        ple(k, x, col("norm_ple0"), ins["ple_in"][0], "ple0")
        nsa(k, x, col("norm_kv"), col("norm_mix1"), ins["positions"], rope[:, 0:1], rope[:, 1:], ins["gate_w"],
            ins["cmp_w1"], ins["cmp_small"], ins["attn_masks"])
        conv_ffn(k, x, col("norm_ffn1"), taps(1), "ffn1")
        ple(k, x, col("norm_ple1"), ins["ple_in"][1], "ple1")
        final_norm(k, x, col("norm_final"), "norm_first")
        second_block(k, both, col, tri, hmask, reset, slot_number)
        final_norm(k, x, col("final_g"), "norm_second")
        with nc.Block(name="store") as block:

            @block.sync
            def _(sp):
                sp.dma_start(out, x).then_inc(stored, 16)
                sp.wait_ge(stored, 16)


def lay_out(a):
    first, parts, at = first_block_arrays(a)
    second_block_cols(a, parts, at)
    first.update(first_block_shape_constants())
    d = {
        "weights": np.concatenate(first_block_stream(a) + second_block_stream(a)),
        "cols": np.concatenate(parts, 1),
        "masks": second_block_shape_constants(),
        "x": first["x_in"], "context": a["ctx_2"][0].T.reshape(KD, P, T).transpose(1, 0, 2),
        "ple_in": first["p_in"], "positions": first["pos_in"], "gate_w": first["gate_w_in"],
        "cmp_w1": first["cmp_w1_in"], "cmp_small": first["cmp_small_in"], "rcount": first["rcount_in"],
        "rope": first["rope_in"], "attn_masks": first["masks_in"],
    }
    return {n: np.ascontiguousarray(v) for n, v in d.items()}, at


def kernel(**inputs):
    import concourse.bacc as bacc
    from concourse.bass_utils import run_bass_kernel_spmd

    arrays, at = lay_out({n: np.asarray(v) for n, v in inputs.items()})
    nc = bacc.Bacc("TRN2", target_bir_lowering=False, num_devices=1)
    ins = {n: nc.dram_tensor(f"in_{n}", v.shape, mybir.dt.from_np(v.dtype), kind="ExternalInput").ap()
           for n, v in arrays.items()}
    out = nc.dram_tensor("out", (P, KD, T), F32, kind="ExternalOutput").ap()
    build_program(nc, ins, out, arrays["weights"].shape[0], at)
    got = run_bass_kernel_spmd(nc, [{f"in_{n}": v for n, v in arrays.items()}], core_ids=[0])
    y = got.results[0]["out"]
    return y.transpose(1, 0, 2).reshape(D, T).T.reshape(1, T, D)
```

```python
from contextlib import ExitStack, contextmanager

import numpy as np

import concourse.bass as bass
from concourse import mybir

F32 = mybir.dt.float32
F32R = mybir.dt.float32r
I32 = mybir.dt.int32
U8 = mybir.dt.uint8
ALU = mybir.AluOpType
ACT = mybir.ActivationFunctionType
AX = mybir.AxisListType

P = 128
D = 1024
KD = D // P
T = 256
T2 = 2 * T
EPS = 1e-6
NEG = -1e30

RING = 12
TILES = 8

WINDOWS = (2, 4, 8, 16)
MAXWIN = max(WINDOWS)
HEADS, HD, GROUPS = 16, 64, 4
HPG = HEADS // GROUPS
ROT = HD // 4
CMP_STRIDE, CMP_LEN = 16, 32
NCMP = T // CMP_STRIDE - 1
DFF = 2816
KF = DFF // P
PLE = 256
PAIRS_PER_ROUND = RING // 2


@contextmanager
def stage_semaphores(nc, stage, *names):
    sems = [nc.alloc_semaphore(f"{stage}_{n}") for n in names]
    yield sems
    nc.clear_and_free_semaphores(sems)
    nc.all_engine_barrier(sem_only=True)


class Kit:

    def __init__(self, nc, ctx, weights, n_slots):
        self.nc, self.ctx = nc, ctx
        self.weights, self.n_slots = weights, n_slots
        self.next_slot = 0
        self.ring = self.sb("ring", [P, RING, TILES, P])
        self.ps = ctx.enter_context(nc.psum_tensor("ps", [P, 8, 512], F32))
        self.landed = [ctx.enter_context(nc.semaphore(f"slot_landed{i}")) for i in range(RING)]

    def sb(self, name, shape, dtype=F32):
        return self.ctx.enter_context(self.nc.sbuf_tensor(name, shape, dtype))

    def take(self, n):
        first = self.next_slot
        self.next_slot += n
        return first

    def prefill(self, sp):
        for n in range(RING):
            sp.dma_start(self.ring[:, n], self.weights[n]).then_inc(self.landed[n], 16)

    def refill(self, sp, first, count, used, per=1, mult=1, base=0):
        count = max(0, min(count, self.n_slots - RING - first))
        rounds = count // RING

        def one(s, i):
            n = first + s
            at = n % RING
            sp.wait_ge(used, i * (RING // per * mult) + base + (s // per + 1) * mult)
            sp.dma_start(self.ring[:, at], self.weights[n + RING + i * RING]).then_inc(self.landed[at], 16)

        if rounds > 1:
            with sp.Fori(0, rounds) as i:
                for s in range(RING):
                    one(s, i)
        else:
            rounds = 0
        for s in range(rounds * RING, count):
            one(s, 0)

    def slot(self, pe, n, i=0):
        at = n % RING
        pe.wait_ge(self.landed[at], 16 * (n // RING + 1) + i * 16)
        return self.ring[:, at]


def rounds_then_rest(engine, steps, per_round, body):
    whole = steps // per_round
    if whole > 1:
        with engine.Fori(0, whole) as i:
            for j in range(per_round):
                body(i * per_round + j, j, i)
    else:
        whole = 0
    for n in range(whole * per_round, steps):
        body(n, n, 0)


NORM_SEMS = ("squared", "summed", "rooted", "normed")
NORM_BANK = 7


def norm_scalar(k, act, sems, x, n):
    squared, summed, rooted, _ = sems
    for t in range(KD):
        act.activation(k.sq[:, t, 0:n], x[:, t, :], ACT.Square).then_inc(squared, 1)
    act.wait_ge(summed, 1)
    act.activation(k.root[:, 0:n], k.ps[:, NORM_BANK, 0:n], ACT.Sqrt, scale=1.0 / D, bias=k.eps[:, 0:1]).then_inc(rooted, 1)


def norm_tensor(k, pe, sems, n):
    squared, summed, _, _ = sems
    for t in range(KD):
        pe.wait_ge(squared, t + 1)
        mm = pe.matmul(k.ps[:, NORM_BANK, 0:n], k.ones[:, :], k.sq[:, t, 0:n], start=(t == 0), stop=(t == KD - 1))
    mm.then_inc(summed, 1)


def norm_vector(k, dve, sems, x, h, gain, n):
    _, _, rooted, normed = sems
    dve.wait_ge(rooted, 1)
    dve.reciprocal(k.rstd[:, 0:n], k.root[:, 0:n])
    dve.drain()
    for t in range(KD):
        dve.scalar_tensor_tensor(h[:, t, :], x[:, t, :], gain[:, t:t + 1], k.rstd[:, 0:n],
                                 ALU.mult, ALU.mult).then_inc(normed, 1)


def constants(k, loads):
    nc = k.nc
    k.ones = k.sb("ones", [P, P])
    k.ident = k.sb("ident", [P, P])
    k.eps = k.sb("eps", [P, 1])
    k.sq = k.sb("sq", [P, KD, T2])
    k.root = k.sb("root", [P, T2])
    k.rstd = k.sb("rstd", [P, T2])
    k.h = k.sb("h", [P, KD, T2])
    with stage_semaphores(nc, "constants", "loaded", "cleared") as (loaded, cleared), nc.Block(name="constants") as block:

        @block.sync
        def _(sp):
            for to, of in loads:
                sp.dma_start(to, of).then_inc(loaded, 16)
            k.prefill(sp)
            sp.wait_ge(loaded, 16 * len(loads))

        @block.gpsimd
        def _(pool):
            pool.memset(k.ones[:, :], 1.0)
            pool.memset(k.eps[:, :], EPS)
            pool.memset(k.ident[:, :], 0.0).then_inc(cleared, 1)
            pool.wait_ge(cleared, 1)
            pool.affine_select(out=k.ident[:, :], in_=k.ident[:, :], compare_op=ALU.not_equal, fill=1.0,
                               base=0, pattern=[[-1, P]], channel_multiplier=1)


def pool_mixer(k, x, gain, scale, rcount_in):
    nc = k.nc
    first = k.take(2)
    with ExitStack() as local:
        hp = local.enter_context(nc.sbuf_tensor("pool_h", [P, KD, MAXWIN + T], F32))
        wa = local.enter_context(nc.sbuf_tensor("pool_wa", [P, KD, MAXWIN + T], F32))
        wb = local.enter_context(nc.sbuf_tensor("pool_wb", [P, KD, MAXWIN + T], F32))
        u = local.enter_context(nc.sbuf_tensor("pool_u", [P, KD, T], F32))
        rcount = local.enter_context(nc.sbuf_tensor("pool_rcount", [P, len(WINDOWS), T], F32))
        with stage_semaphores(nc, "pool", *NORM_SEMS, "loaded", "u_ready", "mixed") as sems, \
                nc.Block(name="pool_mixer", no_gpsimd_drain=True) as block:
            norm, (loaded, u_ready, mixed) = sems[:4], sems[4:]

            @block.sync
            def _(sp):
                sp.dma_start(rcount[:, :, :], rcount_in).then_inc(loaded, 16)
                k.refill(sp, first, 2, mixed, mult=4)

            @block.scalar
            def _(act):
                norm_scalar(k, act, norm, x, T)

            @block.vector
            def _(dve):
                for b in (hp, wa, wb):
                    dve.memset(b[:, :, 0:MAXWIN], 0.0)
                norm_vector(k, dve, norm, x, hp[:, :, MAXWIN:], gain, T)
                dve.drain()
                dve.wait_ge(loaded, 16)
                src, gt = hp, KD // len(WINDOWS)
                for gi, w in enumerate(WINDOWS):
                    dst, t0 = (wa, wb)[gi % 2], gi * gt
                    dve.tensor_tensor(dst[:, t0:, MAXWIN:], src[:, t0:, MAXWIN:],
                                      src[:, t0:, MAXWIN - w // 2:MAXWIN - w // 2 + T], ALU.add)
                    dve.drain()
                    dve.tensor_tensor(u[:, t0:t0 + gt, :], dst[:, t0:t0 + gt, MAXWIN:],
                                      rcount[:, gi, :].unsqueeze(1).broadcast_to([P, gt, T]), ALU.mult)
                    dve.drain()
                    dve.tensor_tensor(u[:, t0:t0 + gt, :], u[:, t0:t0 + gt, :], hp[:, t0:t0 + gt, MAXWIN:],
                                      ALU.subtract).then_inc(u_ready, 1)
                    src = dst
                for m in range(KD):
                    dve.wait_ge(mixed, m + 1)
                    dve.scalar_tensor_tensor(x[:, m, :], k.ps[:, m, 0:T], scale[:, m:m + 1],
                                             x[:, m, :], ALU.mult, ALU.add)

            @block.tensor
            def _(pe):
                norm_tensor(k, pe, norm, T)
                for s in range(2):
                    w = k.slot(pe, first + s)
                    for gg in range(2):
                        pe.wait_ge(u_ready, 2 * s + gg + 1)
                        for m in range(2):
                            mt = 4 * s + 2 * gg + m
                            for c in range(2):
                                mm = pe.matmul(k.ps[:, mt, 0:T], w[:, 4 * gg + 2 * m + c, :],
                                               u[:, 4 * s + 2 * gg + c, :], start=(c == 0), stop=(c == 1))
                            mm.then_inc(mixed, 1)


def product_of_parts(pe, out, w, x, start, stop):
    (w_hi, w_lo), (x_hi, x_lo) = w, x
    pe.matmul(out, w_hi, x_hi, start=start, stop=False)
    pe.matmul(out, w_hi, x_lo, start=False, stop=False)
    return pe.matmul(out, w_lo, x_hi, start=False, stop=stop)


def conv_ffn(k, x, gain, taps, name):
    nc = k.nc
    DOWN_PAIRS = KF // 2
    first = k.take(2 * (KF + DOWN_PAIRS))
    YB = 2
    WB = 2
    with ExitStack() as local:
        def sb(nm, shape, dtype=F32):
            return local.enter_context(nc.sbuf_tensor(f"{name}_{nm}", shape, dtype))

        h_hi = sb("h_hi", [P, KD, T], F32R)
        h_lo = sb("h_lo", [P, KD, T], F32R)
        hid = sb("hid", [P, 2, KF, T], F32R)
        y = k.h[:, 0:2 * YB, T:T2].rearrange("p (b h) t -> p b h t", h=2)
        w_hi = sb("w_hi", [P, WB, 2, TILES, P], F32R)
        w_lo = sb("w_lo", [P, WB, 2, TILES, P], F32R)
        with stage_semaphores(nc, name, *NORM_SEMS, "rounded", "h_split", "used", "w_rounded", "w_split", "based", "conved", "gated",
                              "made", "hid_rounded", "hidden", "summed_down") as sems, \
                nc.Block(name=name, no_gpsimd_drain=True) as block:
            norm, (rounded, h_split, used, w_rounded, w_split, based, conved, gated, made, hid_rounded, hidden, down_done) \
                = sems[:4], sems[4:]

            @block.sync
            def _(sp):
                k.refill(sp, first, 2 * (KF + DOWN_PAIRS), w_split, per=2)

            def matmul(pe, out, q, half, t, xt, start, stop):
                w = (w_hi[:, q % WB, half, t, :], w_lo[:, q % WB, half, t, :])
                return product_of_parts(pe, out, w, xt, start, stop)

            @block.tensor
            def _(pe):
                pe.sem_inc(used, WB)
                norm_tensor(k, pe, norm, T)
                pe.wait_ge(h_split, KD)

                def pair(p, j, i):
                    pe.wait_ge(conved, p + 1)
                    pe.wait_ge(w_split, p + 1)
                    for half in range(2):
                        for t in range(KD):
                            mm = matmul(pe, k.ps[:, j % 2, half * T:(half + 1) * T], j, half, t, (h_hi[:, t, :], h_lo[:, t, :]),
                                        t == 0, t == KD - 1)
                    mm.then_inc(used, 1)

                rounds_then_rest(pe, KF, PAIRS_PER_ROUND, pair)
                pe.wait_ge(conved, KF + YB)
                for q in range(DOWN_PAIRS):
                    pe.wait_ge(w_split, KF + q + 1)
                    for half in range(2):
                        c = 2 * q + half
                        pe.wait_ge(hidden, c + 1 + YB)
                        for m in range(KD):
                            mm = matmul(pe, k.ps[:, m, 0:T], q + KF, half, m, (hid[:, 0, c, :], hid[:, 1, c, :]),
                                        c == 0, c == KF - 1)
                            if c == KF - 1:
                                mm.then_inc(down_done, 1)
                    if q < DOWN_PAIRS - 1:
                        mm.then_inc(used, 1)

            @block.scalar
            def _(act):
                def split(q, j, i, ring_rounds):
                    act.wait_ge(used, q + 1)
                    for half in range(2):
                        w = k.slot(act, first + 2 * j + half, ring_rounds)
                        act.copy(w_hi[:, j % WB, half], w).then_inc(w_rounded, 1)

                split(0, 0, 0, 0)
                norm_scalar(k, act, norm, x, T)
                split(1, 1, 0, 0)
                for t in range(KD):
                    act.wait_ge(norm[3], t + 1)
                    act.copy(h_hi[:, t, :], k.h[:, t, 0:T]).then_inc(rounded, 1)

                def pair(p, j, i):
                    act.wait_ge(used, p + 1 + WB)
                    act.wait_ge(hidden, p + 1)
                    for half in range(2):
                        act.activation(y[:, j % YB, half], k.ps[:, j % 2, half * T:(half + 1) * T], ACT.Identity,
                                       scale=taps[:, bass.ds(p + half * KF, 1), 2], bias=taps[:, bass.ds(p + half * KF, 1), 3]
                                       ).then_inc(based, 1)
                    split(p + WB, j + WB, i, i)
                    act.wait_ge(conved, p + 1 + YB)
                    act.activation(y[:, j % YB, 1], y[:, j % YB, 1], ACT.Silu).then_inc(gated, 1)
                    act.wait_ge(made, p + 1)
                    act.copy(hid[:, 0, p], y[:, j % YB, 0]).then_inc(hid_rounded, 1)

                rounds_then_rest(act, KF, PAIRS_PER_ROUND, pair)
                for q in range(KF + WB, KF + DOWN_PAIRS):
                    split(q, q, 0, 0)

            @block.vector
            def _(dve):
                def split(q, j, i, ring_rounds):
                    for half in range(2):
                        dve.wait_ge(w_rounded, 2 * q + half + 1)
                        tt = dve.tensor_tensor(w_lo[:, j % WB, half], k.ring[:, (first + 2 * j + half) % RING], w_hi[:, j % WB, half],
                                               ALU.subtract)
                    tt.then_inc(w_split, 1)

                split(0, 0, 0, 0)
                norm_vector(k, dve, norm, x, k.h[:, :, 0:T], gain, T)
                dve.sem_inc(conved, YB)
                dve.sem_inc(hidden, YB)
                for t in range(KD):
                    dve.wait_ge(rounded, t + 1)
                    dve.tensor_tensor(h_lo[:, t, :], k.h[:, t, 0:T], h_hi[:, t, :], ALU.subtract).then_inc(h_split, 1)
                split(1, 1, 0, 0)

                def pair(p, j, i):
                    dve.wait_ge(based, 2 * p + 2)
                    for back in (1, 2):
                        for half in range(2):
                            st = dve.scalar_tensor_tensor(
                                y[:, j % YB, half, back:], k.ps[:, j % 2, half * T:(half + 1) * T - back],
                                taps[:, bass.ds(p + half * KF, 1), 2 - back], y[:, j % YB, half, back:], ALU.mult, ALU.add)
                        if back == 1:
                            dve.drain()
                    st.then_inc(conved, 1)
                    split(p + WB, j + WB, i, i)
                    dve.wait_ge(gated, p + 1)
                    dve.tensor_tensor(y[:, j % YB, 0], y[:, j % YB, 0], y[:, j % YB, 1], ALU.mult).then_inc(made, 1)
                    dve.wait_ge(hid_rounded, p + 1)
                    dve.tensor_tensor(hid[:, 1, p], y[:, j % YB, 0], hid[:, 0, p], ALU.subtract).then_inc(hidden, 1)

                rounds_then_rest(dve, KF, PAIRS_PER_ROUND, pair)
                for q in range(KF + WB, KF + DOWN_PAIRS):
                    split(q, q, 0, 0)
                for m in range(KD):
                    dve.wait_ge(down_done, m + 1)
                    dve.tensor_tensor(x[:, m, :], k.ps[:, m, 0:T], x[:, m, :], ALU.add)


def ple(k, x, gain, p_in, name):
    nc = k.nc
    KP = PLE // P
    proj_slots, gate_slots = k.take(2), k.take(KD)
    with ExitStack() as local:
        pt = local.enter_context(nc.sbuf_tensor(f"{name}_p", [P, KP, T], F32))
        proj = local.enter_context(nc.sbuf_tensor(f"{name}_proj", [P, KD, T], F32))
        gate = local.enter_context(nc.sbuf_tensor(f"{name}_gate", [P, 2, T], F32))
        with stage_semaphores(nc, name, *NORM_SEMS, "loaded", "projected", "kept", "product", "gated", "applied") as sems, \
                nc.Block(name=name, no_gpsimd_drain=True) as block:
            norm, (loaded, projected, kept, product, gated, applied) = sems[:4], sems[4:]

            @block.sync
            def _(sp):
                sp.dma_start(pt[:, :, :], p_in).then_inc(loaded, 16)
                k.refill(sp, proj_slots, 2, projected, mult=4)
                k.refill(sp, gate_slots, KD, product)

            @block.tensor
            def _(pe):
                pe.wait_ge(loaded, 16)
                for m in range(KD):
                    w = k.slot(pe, proj_slots + m // 4)
                    for c in range(KP):
                        mm = pe.matmul(k.ps[:, m // 2, m % 2 * T:(m % 2 + 1) * T], w[:, m % 4 * 2 + c, :], pt[:, c, :],
                                       start=(c == 0), stop=(c == KP - 1))
                    mm.then_inc(projected, 1)
                norm_tensor(k, pe, norm, T)
                pe.wait_ge(norm[3], KD)
                for m in range(KD):
                    if m >= 2:
                        pe.wait_ge(gated, m - 1)
                    w = k.slot(pe, gate_slots + m)
                    for t in range(KD):
                        mm = pe.matmul(k.ps[:, 4 + m % 2, 0:T], w[:, t, :], k.h[:, t, 0:T], start=(t == 0), stop=(t == KD - 1))
                    mm.then_inc(product, 1)

            @block.scalar
            def _(act):
                norm_scalar(k, act, norm, x, T)
                act.wait_ge(projected, KD)
                for m in range(KD):
                    act.activation(proj[:, m, :], k.ps[:, m // 2, m % 2 * T:(m % 2 + 1) * T], ACT.Copy).then_inc(kept, 1)
                for m in range(KD):
                    act.wait_ge(product, m + 1)
                    if m >= 2:
                        act.wait_ge(applied, m - 1)
                    act.activation(gate[:, m % 2, :], k.ps[:, 4 + m % 2, 0:T], ACT.Sigmoid).then_inc(gated, 1)

            @block.vector
            def _(dve):
                norm_vector(k, dve, norm, x, k.h[:, :, 0:T], gain, T)
                for m in range(KD):
                    dve.wait_ge(gated, m + 1)
                    dve.wait_ge(kept, m + 1)
                    dve.tensor_tensor(proj[:, m, :], proj[:, m, :], gate[:, m % 2, :], ALU.mult).then_inc(applied, 1)
                    dve.drain()
                    dve.tensor_tensor(x[:, m, :], x[:, m, :], proj[:, m, :], ALU.add)


def nsa(k, x, gain_kv, gain_q, pos, inv_freq, turn, gate_w_in, cmp_w1_in, cmp_small_in, masks_in):
    nc = k.nc
    kv_slots, v_slots, q_slots, o_slots = k.take(8), k.take(4), k.take(8), k.take(8)
    QT = T // P
    local = ExitStack()
    with local:
        def sb(name, shape, dtype=F32):
            return local.enter_context(nc.sbuf_tensor(name, shape, dtype))

        hq = sb("hq", [P, KD, T])
        q = sb("q", [HD, HEADS, T])
        kt = sb("kt", [HD, 4, GROUPS, T])
        v = sb("v", [P, QT, 2, GROUPS, HD])
        gate_w = sb("gate_w", [P, KD, 3 * HEADS])
        gates = sb("gates", [P, QT, HEADS, 3])
        cs = sb("cs", [ROT, 2, T])
        kc = sb("kc", [HD, GROUPS, NCMP])
        vc = sb("vc", [NCMP, GROUPS, HD])
        attn = sb("attn", [P, KD, T])

        with ExitStack() as tmp:
            ang = tmp.enter_context(nc.sbuf_tensor("ang", [ROT, 4, T], F32))
            posf = tmp.enter_context(nc.sbuf_tensor("posi", [ROT, T], I32))
            with stage_semaphores(nc, "qkv", *NORM_SEMS, "loaded", "q_normed", "product", "kept", "angled", "v_used") as sems, \
                    nc.Block(name="qkv", no_gpsimd_drain=True) as block:
                norm, (loaded, q_normed, product, kept, angled, v_used) = sems[:4], sems[4:]
                NB = 4

                @block.sync
                def _(sp):
                    sp.dma_start(gate_w[:, :, :], gate_w_in).then_inc(loaded, 16)
                    sp.dma_start(posf[:, :], pos).then_inc(loaded, 16)
                    k.refill(sp, kv_slots, 8, product)
                    k.refill(sp, v_slots, 3, v_used)
                    k.refill(sp, v_slots + 3, 1, product, mult=QT, base=8)
                    k.refill(sp, q_slots, 8, product, base=8 + QT)

                @block.tensor
                def _(pe):
                    norm_tensor(k, pe, norm, T)
                    pe.wait_ge(norm[3], KD)
                    for m in range(8):
                        if m >= NB:
                            pe.wait_ge(kept, m - NB + 1)
                        w = k.slot(pe, kv_slots + m)
                        for t in range(KD):
                            mm = pe.matmul(k.ps[:, m % NB, 0:T], w[:, t, :], k.h[:, t, 0:T], start=(t == 0), stop=(t == KD - 1))
                        mm.then_inc(product, 1)
                    for s in range(4):
                        w = k.slot(pe, v_slots + s).rearrange("p (a b) c -> p a (b c)", a=2)
                        for a in range(2):
                            for tok in range(QT):
                                mm = pe.matmul(k.ps[:, 4 + tok, :], k.h[:, 2 * s + a, tok * P:(tok + 1) * P], w[:, a, :],
                                               start=(s + a == 0), stop=(s + a == 4))
                                if s + a == 4:
                                    mm.then_inc(product, 1)
                        if s < 3:
                            mm.then_inc(v_used, 1)
                    pe.wait_ge(q_normed, KD)
                    for m in range(8):
                        pe.wait_ge(kept, 8 - NB + m + 1)
                        w = k.slot(pe, q_slots + m)
                        for t in range(KD):
                            mm = pe.matmul(k.ps[:, m % NB, 0:T], w[:, t, :], hq[:, t, :], start=(t == 0), stop=(t == KD - 1))
                        mm.then_inc(product, 1)
                    pe.wait_ge(loaded, 32)
                    for tok in range(QT):
                        for t in range(KD):
                            mm = pe.matmul(k.ps[:, 6, tok * 64:tok * 64 + 3 * HEADS], hq[:, t, tok * P:(tok + 1) * P],
                                           gate_w[:, t, :], start=(t == 0), stop=(t == KD - 1))
                        mm.then_inc(product, 1)

                @block.scalar
                def _(act):
                    norm_scalar(k, act, norm, x, T)
                    for m in range(8):
                        act.wait_ge(product, m + 1)
                        for half in range(2):
                            cp = act.activation(kt[:, m // 2, m % 2 * 2 + half, :], k.ps[half * HD:(half + 1) * HD, m % NB, 0:T],
                                                ACT.Copy)
                        cp.then_inc(kept, 1)
                    act.wait_ge(product, 10)
                    for tok in range(QT):
                        act.activation(v[:, tok].rearrange("p a g d -> p (a g d)"), k.ps[:, 4 + tok, :], ACT.Copy)
                    for m in range(8):
                        act.wait_ge(product, 11 + m)
                        for half in range(2):
                            cp = act.activation(q[:, 2 * m + half, :], k.ps[half * HD:(half + 1) * HD, m % NB, 0:T], ACT.Copy)
                        cp.then_inc(kept, 1)
                    act.wait_ge(product, 20)
                    for tok in range(QT):
                        act.activation(gates[:, tok].rearrange("p h b -> p (h b)"), k.ps[:, 6, tok * 64:tok * 64 + 3 * HEADS],
                                       ACT.Sigmoid)
                    act.wait_ge(angled, 2)
                    act.activation(cs[:, :, :], ang[:, 0:2, :], ACT.Sin)

                @block.vector
                def _(dve):
                    norm_vector(k, dve, norm, x, k.h[:, :, 0:T], gain_kv, T)
                    for t in range(KD):
                        dve.scalar_tensor_tensor(hq[:, t, :], x[:, t, :], gain_q[:, t:t + 1], k.rstd[:, 0:T],
                                                 ALU.mult, ALU.mult).then_inc(q_normed, 1)
                    two_pi = 2.0 * np.pi
                    c1 = 6.28125
                    c2 = float(np.float32(np.floor((two_pi - c1) * 2.0 ** 20) / 2.0 ** 20))
                    c3 = two_pi - c1 - c2
                    magic = 1.5 * 2.0 ** 23
                    dve.wait_ge(loaded, 32)
                    dve.tensor_copy(ang[:, 2, :], posf[:, :])
                    dve.drain()
                    dve.tensor_scalar(ang[:, 2, :], ang[:, 2, :], inv_freq[0:ROT, 0:1], None, ALU.mult)
                    dve.drain()
                    for part, quarter in ((0, 0.25), (1, 0.0)):
                        turns, r = ang[:, 3, :], ang[:, part, :]
                        dve.tensor_scalar(turns, ang[:, 2, :], 1.0 / two_pi, quarter, ALU.mult, ALU.add)
                        dve.drain()
                        dve.tensor_scalar(turns, turns, magic, None, ALU.add)
                        dve.drain()
                        dve.tensor_scalar(turns, turns, magic, None, ALU.subtract)
                        dve.drain()
                        dve.scalar_tensor_tensor(r, turns, -c1, ang[:, 2, :], ALU.mult, ALU.add)
                        dve.drain()
                        for c in (c2, c3):
                            dve.scalar_tensor_tensor(r, turns, -c, r, ALU.mult, ALU.add)
                            dve.drain()
                        pi = 3.141592
                        dve.tensor_scalar(r, r, quarter * two_pi, pi, ALU.add, ALU.min)
                        dve.drain()
                        dve.tensor_scalar(r, r, -pi, None, ALU.max).then_inc(angled, 1)

        with ExitStack() as tmp:
            w1 = tmp.enter_context(nc.sbuf_tensor("cmp_w1", [HD, 2, CMP_LEN, P], F32))
            small = tmp.enter_context(nc.sbuf_tensor("cmp_small", [P, 2 * HD + 2 * CMP_LEN], F32))
            bias = tmp.enter_context(nc.sbuf_tensor("cmp_bias", [P, 2], F32))
            hidc = tmp.enter_context(nc.sbuf_tensor("cmp_hid", [P, 2, GROUPS * NCMP], F32))
            turned = tmp.enter_context(nc.sbuf_tensor("turned", [ROT, 2, 2, T], F32))
            NR = 12
            with stage_semaphores(nc, "rope", "loaded", "crossed", "turned", "biased", "bias_kept", "hidden", "activated",
                                  "kc_made", "vc_made", "kc_kept", "kc_crossed") as sems, \
                    nc.Block(name="rope_compress", no_gpsimd_drain=True) as block:
                loaded, crossed, turned_s, biased, bias_kept, hidden, activated, kc_made, vc_made, kc_kept, kc_crossed = sems

                def rot_rows(n):
                    if n < 8:
                        return q[0:ROT, 2 * n:2 * n + 2, :]
                    return kt[0:ROT, 2 + (n - 8) // 2, (n - 8) % 2 * 2:(n - 8) % 2 * 2 + 2, :]

                @block.sync
                def _(sp):
                    sp.dma_start(w1[:, :, :, :], cmp_w1_in).then_inc(loaded, 16)
                    sp.dma_start(small[:, :], cmp_small_in).then_inc(loaded, 16)

                @block.tensor
                def _(pe):
                    for n in range(NR):
                        if n >= 2:
                            pe.wait_ge(turned_s, n - 1)
                        pe.matmul(k.ps[0:ROT, n % 2, :], turn[0:ROT, 0:ROT], rot_rows(n), start=True, stop=True
                                  ).then_inc(crossed, 1)
                    pe.wait_ge(loaded, 32)
                    for a in range(2):
                        blocks = kt[:, a].rearrange("p g (c s) -> p g c s", s=CMP_STRIDE)
                        for l in range(CMP_LEN):
                            c0, s0 = l // CMP_STRIDE, l % CMP_STRIDE
                            mm = pe.matmul(k.ps[:, 2 + a, 0:GROUPS * NCMP], w1[:, a, l, :], blocks[:, :, c0:c0 + NCMP, s0],
                                           start=(l == 0), stop=(l == CMP_LEN - 1))
                        mm.then_inc(hidden, 1)
                        for l in range(CMP_LEN):
                            mm = pe.matmul(k.ps[:, 4 + a, 0:1], w1[:, a, l, :],
                                           small[0:HD, 2 * HD + a * CMP_LEN + l:2 * HD + a * CMP_LEN + l + 1],
                                           start=(l == 0), stop=(l == CMP_LEN - 1))
                        mm.then_inc(biased, 1)
                    pe.wait_ge(activated, 1)
                    pe.matmul(k.ps[0:HD, 6, 0:GROUPS * NCMP], small[:, 0:HD], hidc[:, 0, :], start=True, stop=True
                              ).then_inc(kc_made, 1)
                    pe.wait_ge(activated, 2)
                    for g in range(GROUPS):
                        mm = pe.matmul(k.ps[0:NCMP, 7, g * HD:(g + 1) * HD], hidc[:, 1, g * NCMP:(g + 1) * NCMP],
                                       small[:, HD:2 * HD], start=True, stop=True)
                    mm.then_inc(vc_made, 1)
                    pe.wait_ge(kc_kept, 1)
                    pe.matmul(k.ps[0:ROT, 5, 0:GROUPS * NCMP], turn[0:ROT, 0:ROT], kc[0:ROT].rearrange("p g c -> p (g c)"),
                              start=True, stop=True).then_inc(kc_crossed, 1)

                @block.scalar
                def _(act):
                    for a in range(2):
                        act.wait_ge(biased, a + 1)
                        act.wait_ge(hidden, a + 1)
                        act.activation(bias[:, a:a + 1], k.ps[:, 4 + a, 0:1], ACT.Copy).then_inc(bias_kept, 1)
                        act.drain()
                        act.activation(hidc[:, a, :], k.ps[:, 2 + a, 0:GROUPS * NCMP], ACT.Gelu_apprx_tanh,
                                       bias=bias[:, a:a + 1]).then_inc(activated, 1)
                    act.wait_ge(kc_made, 1)
                    act.activation(kc[:, :, :].rearrange("p g c -> p (g c)"), k.ps[0:HD, 6, 0:GROUPS * NCMP], ACT.Copy
                                   ).then_inc(kc_kept, 1)
                    act.wait_ge(vc_made, 1)
                    act.activation(vc[:, :, :].rearrange("p g d -> p (g d)"), k.ps[0:NCMP, 7, 0:GROUPS * HD], ACT.Copy)

                @block.vector
                def _(dve):
                    def turn_rows(rows, cross, cos, sin, keep):
                        a, b = keep
                        dve.drain()
                        dve.tensor_tensor(a, rows, cos, ALU.mult)
                        dve.tensor_tensor(b, cross, sin, ALU.mult)
                        dve.drain()
                        return dve.tensor_tensor(rows, a, b, ALU.add)

                    both = [cs[:, j].unsqueeze(1).broadcast_to([ROT, 2, T]) for j in range(2)]
                    for n in range(NR):
                        dve.wait_ge(crossed, n + 1)
                        turn_rows(rot_rows(n), k.ps[0:ROT, n % 2, :].rearrange("p (h t) -> p h t", h=2), both[0], both[1],
                                  (turned[:, 0], turned[:, 1])).then_inc(turned_s, 1)
                    dve.wait_ge(kc_crossed, 1)
                    ends = [cs[:, j].rearrange("p (c s) -> p c s", s=CMP_STRIDE)[:, 1:, CMP_STRIDE - 1]
                            .unsqueeze(1).broadcast_to([ROT, GROUPS, NCMP]) for j in range(2)]
                    keep = [turned[:, j, 0, 0:GROUPS * NCMP].rearrange("p (g c) -> p g c", g=GROUPS) for j in range(2)]
                    turn_rows(kc[0:ROT, :, :], k.ps[0:ROT, 5, 0:GROUPS * NCMP].rearrange("p (g c) -> p g c", g=GROUPS),
                              ends[0], ends[1], keep)

        with ExitStack() as tmp:
            def tb(name, shape, dtype=F32):
                return tmp.enter_context(nc.sbuf_tensor(name, shape, dtype))

            qg = tb("qg", [HD, HPG, T])
            vg = tb("vg", [P, 2, QT, HD])
            vcg = tb("vcg", [NCMP, HD])
            causal = tb("causal", [P, QT, T + 2 * NCMP])
            s = tb("s", [P, HPG, 2, T])
            sc = tb("sc", [P, HPG, NCMP])
            top = tb("top", [P, HPG, 3])
            total = tb("total", [P, HPG, 3])
            pt = tb("pt", [P, HPG, 2, QT, P])
            ptc = tb("ptc", [NCMP, HPG, P])
            scale = HD ** -0.5
            STEPS = QT
            with stage_semaphores(nc, "attn", "loaded", "grouped", "scored", "topped", "expd", "weighted", "turned", "turn_kept",
                                  "c_turned", "summed", "kept", "c_scored", "c_kept") as sems, \
                    nc.Block(name="attention", no_gpsimd_drain=True) as block:
                (loaded, grouped, scored, topped, expd, weighted, turned_s, turn_kept, c_turned, summed, kept, c_scored, c_kept) = sems

                @block.sync
                def _(sp):
                    sp.dma_start(causal[:, :, :], masks_in).then_inc(loaded, 16)

                @block.tensor
                def _(pe):
                    with pe.Fori(0, GROUPS) as g:
                        pe.wait_ge(grouped, g + 1)
                        for qt in range(QT):
                            n, nk = g * STEPS + qt, (qt + 1) * P
                            for hh in range(HPG):
                                mm = pe.matmul(k.ps[:, 4, hh * NCMP:(hh + 1) * NCMP], qg[:, hh, qt * P:(qt + 1) * P],
                                               kc[:, g, :], start=True, stop=True)
                            mm.then_inc(c_scored, 1)
                            for hh in range(HPG):
                                for br in range(2):
                                    mm = pe.matmul(k.ps[:, hh, br * T:br * T + nk], qg[:, hh, qt * P:(qt + 1) * P],
                                                   kt[:, 2 + br, g, 0:nk], start=True, stop=True)
                                mm.then_inc(scored, 1)
                            for hh in range(HPG):
                                pe.wait_ge(weighted, HPG * n + hh + 1)
                                for br in range(2):
                                    for c in range(qt + 1):
                                        mm = pe.transpose(k.ps[:, hh, (2 * br + c) * P:(2 * br + c + 1) * P],
                                                          s[:, hh, br, c * P:(c + 1) * P], k.ident[:, :])
                                mm.then_inc(turned_s, 1)
                            for hh in range(HPG):
                                mm = pe.transpose(k.ps[0:NCMP, 5, hh * P:(hh + 1) * P], sc[:, hh, :], k.ident[:, :])
                            mm.then_inc(c_turned, 1)
                            pe.wait_ge(c_kept, n + 1)
                            for hh in range(HPG):
                                pe.wait_ge(turn_kept, HPG * n + hh + 1)
                                at = k.ps[0:HD, 6 + qt, hh * P:(hh + 1) * P]
                                pe.matmul(at, vcg[:, :], ptc[:, hh, :], start=True, stop=False)
                                for br in range(2):
                                    for c in range(qt + 1):
                                        mm = pe.matmul(at, vg[:, br, c, :], pt[:, hh, br, c, :], start=False,
                                                       stop=(br == 1 and c == qt))
                            mm.then_inc(summed, 1)

                @block.scalar
                def _(act):
                    with act.Fori(0, GROUPS) as g:
                        for qt in range(QT):
                            n, nk = g * STEPS + qt, (qt + 1) * P
                            for hh in range(HPG):
                                act.wait_ge(topped, HPG * n + hh + 1)
                                for br in range(2):
                                    act.activation(s[:, hh, br, 0:nk], s[:, hh, br, 0:nk], ACT.Exp,
                                                   bias=top[:, hh, 1 + br:2 + br], accum_out=total[:, hh, 1 + br:2 + br])
                                act.activation(sc[:, hh, :], sc[:, hh, :], ACT.Exp, bias=top[:, hh, 0:1]).then_inc(expd, 1)
                            for hh in range(HPG):
                                act.wait_ge(turned_s, HPG * n + hh + 1)
                                for br in range(2):
                                    cp = act.activation(pt[:, hh, br, 0:qt + 1, :].rearrange("p c t -> p (c t)"),
                                                        k.ps[:, hh, 2 * br * P:(2 * br + qt + 1) * P], ACT.Copy)
                                cp.then_inc(turn_kept, 1)
                            act.wait_ge(c_turned, n + 1)
                            act.activation(ptc[:, :, :].rearrange("p h t -> p (h t)"), k.ps[0:NCMP, 5, :], ACT.Copy
                                           ).then_inc(c_kept, 1)
                            act.wait_ge(summed, n + 1)
                            for hh in range(HPG):
                                half = hh % 2
                                act.activation(attn[half * HD:(half + 1) * HD, g * (HPG // 2) + hh // 2, qt * P:(qt + 1) * P],
                                               k.ps[0:HD, 6 + qt, hh * P:(hh + 1) * P], ACT.Copy).then_inc(kept, 1)

                @block.vector
                def _(dve):
                    dve.wait_ge(loaded, 16)
                    dve.sem_inc(kept, QT * HPG)
                    with dve.Fori(0, GROUPS) as g:
                        dve.wait_ge(kept, QT * HPG * (g + 1))
                        dve.tensor_copy(qg[:, :, :], q[:, bass.ds(g * HPG, HPG), :])
                        for br in range(2):
                            dve.tensor_copy(vg[:, br], v[:, :, br, bass.ds(g, 1), :].rearrange("p a g d -> p a (g d)"))
                        dve.tensor_copy(vcg[:, :], vc[:, g, :]).then_inc(grouped, 1)
                        for qt in range(QT):
                            n, nk = g * STEPS + qt, (qt + 1) * P
                            dve.wait_ge(c_scored, n + 1)
                            dve.scalar_tensor_tensor(sc[:, :, :], k.ps[:, 4, 0:HPG * NCMP].rearrange("p (h c) -> p h c", h=HPG), scale,
                                                     causal[:, qt, T:T + NCMP].unsqueeze(1).broadcast_to([P, HPG, NCMP]),
                                                     ALU.mult, ALU.add)
                            for hh in range(HPG):
                                dve.wait_ge(scored, HPG * n + hh + 1)
                                dve.scalar_tensor_tensor(s[:, hh, :, 0:nk],
                                                         k.ps[:, hh, :].rearrange("p (b t) -> p b t", b=2)[:, :, 0:nk], scale,
                                                         causal[:, qt, 0:nk].unsqueeze(1).broadcast_to([P, 2, nk]),
                                                         ALU.mult, ALU.add)
                                dve.drain()
                                dve.tensor_reduce(top[:, hh, 1:3], s[:, hh, :, 0:nk], AX.X, ALU.max, negate=True)
                                dve.tensor_reduce(top[:, hh, 0:1], sc[:, hh, :], AX.X, ALU.max, negate=True).then_inc(topped, 1)
                            for hh in range(HPG):
                                dve.wait_ge(expd, HPG * n + hh + 1)
                                dve.tensor_tensor(sc[:, hh, :], sc[:, hh, :], causal[:, qt, T + NCMP:], ALU.mult)
                                dve.drain()
                                dve.tensor_reduce(total[:, hh, 0:1], sc[:, hh, :], AX.X, ALU.add)
                                dve.drain()
                                dve.tensor_scalar(total[:, hh, :], total[:, hh, :], 1e-30, None, ALU.max)
                                dve.drain()
                                dve.reciprocal(total[:, hh, :], total[:, hh, :])
                                dve.drain()
                                dve.tensor_tensor(total[:, hh, :].unsqueeze(1), total[:, hh, :].unsqueeze(1),
                                                  gates[:, qt, bass.ds(g * HPG + hh, 1), :], ALU.mult)
                                dve.drain()
                                for br in range(2):
                                    dve.tensor_scalar(s[:, hh, br, 0:nk], s[:, hh, br, 0:nk], total[:, hh, 1 + br:2 + br], None,
                                                      ALU.mult)
                                dve.tensor_scalar(sc[:, hh, :], sc[:, hh, :], total[:, hh, 0:1], None, ALU.mult
                                                  ).then_inc(weighted, 1)

        linear_residual(k, "attn_out", o_slots, attn, KD, T, x, x_cols=slice(0, T))


def linear_residual(k, name, first, inp, kt, n, x, x_cols):
    nc = k.nc
    per = kt // TILES
    with stage_semaphores(nc, name, "product", "added") as (product, added), \
            nc.Block(name=name, no_gpsimd_drain=True) as block:

        @block.sync
        def _(sp):
            k.refill(sp, first, KD * per, product, per=per)

        @block.tensor
        def _(pe):
            for m in range(KD):
                for c in range(per):
                    w = k.slot(pe, first + m * per + c)
                    for t in range(TILES):
                        mm = pe.matmul(k.ps[:, m, 0:n], w[:, t, :], inp[:, c * TILES + t, :],
                                       start=(c + t == 0), stop=(c == per - 1 and t == TILES - 1))
                mm.then_inc(product, 1)

        @block.vector
        def _(dve):
            for m in range(KD):
                dve.wait_ge(product, m + 1)
                dve.tensor_tensor(x[:, m, x_cols], k.ps[:, m, 0:n], x[:, m, x_cols], ALU.add)


def cols(a):
    a = np.asarray(a)
    return a.reshape(-1, P).T


def out_tiles(w):
    kk, m = w.shape
    return w.reshape(kk // P, P, m // P, P).transpose(2, 1, 0, 3).reshape(m // P, P, -1, TILES * P).transpose(0, 2, 1, 3).reshape(-1, P, TILES * P)


def first_block_stream(a):
    out = []
    pw = a["pool_w"][0].reshape(2, 2, 2, P, 2, P)
    out.append(pw.transpose(0, 3, 1, 4, 2, 5).reshape(2, P, TILES * P))

    def ffn(i):
        up = a["ffn_up"][i].reshape(KD, P, 2, KF, P).transpose(3, 2, 1, 0, 4).reshape(2 * KF, P, TILES * P)
        return [up, a["ffn_down"][i].reshape(KF, P, D)]

    def ple_w(i):
        pr = a["ple_proj"][i].reshape(2, P, 2, 4, P).transpose(2, 1, 3, 0, 4).reshape(2, P, TILES * P)
        return [pr, out_tiles(a["ple_gate"][i])]

    out += ffn(0) + ple_w(0)
    wkv = a["w_kv"].reshape(D, 6, GROUPS * HD)
    keys = np.concatenate([wkv[:, j] for j in (0, 1, 2, 4)], axis=1)
    vals = np.concatenate([wkv[:, j] for j in (3, 5)], axis=1)
    out.append(out_tiles(keys))
    out.append(vals.reshape(4, 2, P, 512).transpose(0, 2, 1, 3).reshape(4, P, TILES * P))
    out.append(out_tiles(a["w_in_b"][0][:, :HEADS * HD]))
    out.append(out_tiles(a["w_out_b"][0]))
    out += ffn(1) + ple_w(1)
    return out


def first_block_arrays(a):
    d = {}
    cl = []
    at = {}

    def put(name, arr):
        at[name] = (sum(c.shape[1] for c in cl), arr.shape[1])
        cl.append(arr)

    for i in range(2):
        put(f"norm_mix{i}", cols(a["norm_mix"][i]))
        put(f"norm_ffn{i}", cols(a["norm_ffn"][i]))
        put(f"norm_ple{i}", cols(a["norm_ple"][i]))
        taps = np.concatenate([a["ffn_conv"][i], a["ffn_conv_b"][i][None]], 0)
        put(f"taps{i}", taps.reshape(4, 2 * KF, P).transpose(2, 1, 0).reshape(P, -1))
    put("pool_scale", cols(a["pool_scale"][0]))
    put("norm_kv", cols(a["norm_kv"]))
    put("norm_final", cols(a["norm_final"]))
    d["x_in"] = a["x"][0].T.reshape(KD, P, T).transpose(1, 0, 2)
    d["p_in"] = a["p"][:, 0].transpose(0, 2, 1).reshape(2, 2, P, T).transpose(0, 2, 1, 3)
    d["pos_in"] = np.broadcast_to(a["positions"][0].astype(np.int32), (ROT, T))
    d["gate_w_in"] = a["w_in_b"][0][:, HEADS * HD:].reshape(KD, P, 3 * HEADS).transpose(1, 0, 2)
    w1 = np.stack([a["cmp_w1_k"], a["cmp_w1_v"]]).reshape(2, CMP_LEN, HD, P).transpose(2, 0, 1, 3)
    d["cmp_w1_in"] = w1
    posT = np.concatenate([a["cmp_pos_k"].T, a["cmp_pos_v"].T], 1)
    d["cmp_small_in"] = np.concatenate([a["cmp_w2_k"], a["cmp_w2_v"], np.concatenate([posT, np.zeros_like(posT)], 0)], 1)
    return d, cl, at


def first_block_shape_constants():
    d = {}
    t = np.arange(T)
    rc = np.stack([1.0 / np.minimum(t + 1, w) for w in WINDOWS]).astype(np.float32)
    d["rcount_in"] = np.broadcast_to(rc, (P, 4, T))
    inv = (np.float32(500000.0) ** (-np.arange(0, ROT, 2, dtype=np.float32) / np.float32(ROT))).astype(np.float32)
    rope = np.zeros((P, 1 + ROT), np.float32)
    rope[:ROT, 0] = np.concatenate([inv, inv])
    for m in range(ROT // 2):
        rope[m + ROT // 2, 1 + m] = -1.0
        rope[m, 1 + m + ROT // 2] = 1.0
    d["rope_in"] = rope
    q = np.arange(P)[:, None]
    m = np.zeros((P, 2, T + 2 * NCMP), np.float32)
    for qt in range(2):
        m[:, qt, :T] = np.where(np.arange(T)[None] <= q + qt * P, 0.0, NEG)
        ok = CMP_STRIDE * np.arange(NCMP)[None] + CMP_LEN - 1 <= q + qt * P
        m[:, qt, T:T + NCMP] = np.where(ok, 0.0, NEG)
        m[:, qt, T + NCMP:] = ok
    d["masks_in"] = m
    return d
N_MOD = 6
SEGS = 2
TT = T2 // P
SH, SP_, SG, SN = 16, 64, 4, 128
SREP = SH // SG
XBC = (SH * SP_ + 2 * SG * SN) // P
XS_TILES = SH * SP_ // P
SCONV, CFK = 5, 31
GRID = 64
ROWS = T // GRID
GH, GC = 8, 64
NCH = T // GC
EXPERTS, EGROUPS, EPG, TOPK = 16, 4, 4, 2
DEXP = 512
POOL_TILES = 2
KE = DEXP // P


def halves(ap):
    return ap.rearrange("p (s t) -> p s t", s=SEGS)


def final_norm(k, x, gain, name):
    nc = k.nc
    with stage_semaphores(nc, name, *NORM_SEMS) as norm, nc.Block(name=name, no_gpsimd_drain=True) as block:

        @block.scalar
        def _(act):
            norm_scalar(k, act, norm, x, T)

        @block.tensor
        def _(pe):
            norm_tensor(k, pe, norm, T)

        @block.vector
        def _(dve):
            norm_vector(k, dve, norm, x, x, gain, T)


def modulation(k, cond, bias, mods):
    nc = k.nc
    CG, RUN = 32, 512
    PER = P // CG * RUN // D
    BANKS = N_MOD * D * CG // (RUN * P)
    with nc.sbuf_tensor("mod_cond", [P, KD, CG], F32) as padded, nc.sbuf_tensor("mod_rows", [P, 2, RUN], F32) as rows, \
            stage_semaphores(nc, "mod", "activated", "product", "taken", "turned", "kept") as sems, \
            nc.Block(name="modulation", no_gpsimd_drain=True) as block:
        activated, product, taken, turned, kept = sems
        first = k.take(2 * BANKS * KD * PER)

        @block.sync
        def _(sp):
            k.refill(sp, first, 2 * BANKS * KD * PER, product, per=PER)

        @block.scalar
        def _(act):
            act.activation(padded[:, :, 0:2], cond, ACT.Silu).then_inc(activated, 1)
            for n in range(2 * BANKS):
                act.wait_ge(product, (n + 1) * KD)
                if n >= 2:
                    act.wait_ge(turned, n - 1)
                act.copy(rows[:, n % 2, :], k.ps[:, n % 2, :]).then_inc(taken, 1)

        @block.tensor
        def _(pe):
            def turn(n):
                pe.wait_ge(taken, n + 1)
                if n >= 2:
                    pe.wait_ge(kept, n - 1)
                for q in range(RUN // P):
                    mm = pe.transpose(k.ps[:, 2 + n % 2, q * P:(q + 1) * P], rows[:, n % 2, q * P:(q + 1) * P], k.ident[:, :])
                mm.then_inc(turned, 1)

            pe.wait_ge(activated, 2)
            for n in range(2 * BANKS):
                if n >= 2:
                    pe.wait_ge(taken, n - 1)
                for t in range(KD):
                    for j in range(P // CG):
                        at = j * RUN
                        if at % D == 0:
                            w = k.slot(pe, first + (n * KD + t) * PER + at // D)[:, :, :].rearrange("p a f -> p (a f)")
                        mm = pe.matmul(k.ps[j * CG:(j + 1) * CG, n % 2, :], padded[:, t, :], w[:, at % D:at % D + RUN],
                                       start=(t == 0), stop=(t == KD - 1))
                    mm.then_inc(product, 1)
                if n:
                    turn(n - 1)
            turn(2 * BANKS - 1)

        @block.vector
        def _(dve):
            dve.memset(padded[:, :, 2:], 0.0).then_inc(activated, 1)
            for n in range(2 * BANKS):
                layer, part = divmod(n, BANKS)
                dve.wait_ge(turned, n + 1)
                for q in range(RUN // P):
                    tiles = slice(part * 16 + q, (part + 1) * 16, 4)
                    out = mods[:, layer, tiles, :]
                    of = k.ps[:, 2 + n % 2, q * P:(q + 1) * P].rearrange("p (j r) -> p j r", r=CG)[:, :, 0:2]
                    b = bias[:, layer * N_MOD * KD:(layer + 1) * N_MOD * KD][:, tiles].unsqueeze(2).broadcast_to([P, P // CG, 2])
                    tt = dve.tensor_tensor(out, of, b, ALU.add)
                tt.then_inc(kept, 1)


def scaled_gains(k, mods, gains, out):
    nc = k.nc
    with nc.Block(name="scaled_gains", no_gpsimd_drain=True) as block:

        @block.vector
        def _(dve):
            for layer in range(2):
                for which, part in ((0, 1), (1, 4)):
                    o = out[:, layer, which]
                    m = mods[:, layer, part * KD:(part + 1) * KD, :]
                    dve.tensor_scalar(o, m, 1.0, None, ALU.add)
                    dve.drain()
                    dve.tensor_tensor(o, o, gains[which][:, layer * KD:(layer + 1) * KD].unsqueeze(2).broadcast_to([P, KD, 2]),
                                      ALU.mult)


def mod_norm_vector(k, dve, norm, x, segs, gain, n, made):
    dve.wait_ge(norm[2], 1)
    dve.reciprocal(k.rstd[:, 0:n], k.root[:, 0:n])
    dve.drain()
    for t in range(KD):
        for j, s in enumerate(segs):
            dve.scalar_tensor_tensor(k.h[:, t, j * T:(j + 1) * T], x[:, t, s * T:(s + 1) * T], gain[:, t, s:s + 1],
                                     k.rstd[:, j * T:(j + 1) * T], ALU.mult, ALU.mult).then_inc(made, 1)


def mod_norm_shift(k, act, segs, shift, made, ready, col_major=False):
    for t in range(KD):
        for j, s in enumerate(segs):
            act.wait_ge(made, t * len(segs) + j + 1)
            of = k.h[:, t, j * T:(j + 1) * T]
            to = of
            if col_major:
                to = k.sq[:, t, j * T:(j + 1) * T]
                if s == 1:
                    of = of.rearrange("p (r w) -> p r w", r=ROWS)
                    to = to.rearrange("p (w r) -> p r w", r=ROWS)
            act.activation(to, of, ACT.Identity, bias=shift[:, t, s:s + 1]).then_inc(ready, 1)


def even_in(k, x, col, gain, shift, zs, xbc, dt):
    nc = k.nc
    cf_slots, z_slots, x_slots = k.take(16), k.take(8), k.take(XBC)
    NM = 40
    HALF = TILES // 2
    dt_w = col("dt_w").rearrange("p (t c) -> p t c", t=KD)
    ctaps = col("ssd_taps").rearrange("p (t j) -> p t j", j=SCONV + 1)
    ftaps = col("cf_taps").rearrange("p (t j) -> p t j", j=CFK + 1)
    u, cf = k.sq, k.h
    keep = zs[:, 0:2, :]
    with ExitStack() as local:
        def sb(name, shape, dtype=F32):
            return local.enter_context(nc.sbuf_tensor(f"even_{name}", shape, dtype))

        WB = 3
        h_hi = sb("h_hi", [P, KD, T2], F32R)
        h_lo = sb("h_lo", [P, KD, T2], F32R)
        w_hi = sb("w_hi", [P, WB, HALF, P], F32R)
        w_lo = sb("w_lo", [P, WB, HALF, P], F32R)
        raw = sb("dt_raw", [P, 2, TT * 32])
        scaled = (k.root, k.rstd)
        with stage_semaphores(nc, "even_in", *NORM_SEMS, "made", "ready", "rounded", "h_split", "used", "w_rounded", "w_split",
                              "gated", "freed", "based", "conved", "u_made", "dt_product", "dt_abs", "dt_log"
                              ) as sems, nc.Block(name="even_in", no_gpsimd_drain=True) as block:
            norm, (made, ready, rounded, h_split, used, w_rounded, w_split, gated, freed, based, conved, u_made, dt_product,
                   dt_abs, dt_log) = sems[:4], sems[4:]
            BANKS = 4

            def done(n):
                return WB + 2 * n + 2

            @block.sync
            def _(sp):
                k.refill(sp, cf_slots, NM, w_split, mult=2)

            @block.tensor
            def _(pe):
                pe.sem_inc(used, WB)
                norm_tensor(k, pe, norm, T2)
                pe.wait_ge(ready, KD * SEGS)
                for tt in range(TT):
                    for t in range(KD):
                        mm = pe.matmul(k.ps[:, 6, tt * 32:(tt + 1) * 32], k.h[:, t, tt * P:(tt + 1) * P], dt_w[:, t, :],
                                       start=(t == 0), stop=(t == KD - 1))
                mm.then_inc(dt_product, 1)
                pe.wait_ge(h_split, KD)
                for n in range(NM):
                    if n >= BANKS:
                        pe.wait_ge(freed, n - BANKS + 1)
                    for half in range(2):
                        g = 2 * n + half
                        pe.wait_ge(w_split, g + 1)
                        for j in range(HALF):
                            t = half * HALF + j
                            mm = product_of_parts(pe, k.ps[:, n % BANKS, :], (w_hi[:, g % WB, j, :], w_lo[:, g % WB, j, :]),
                                                  (h_hi[:, t, :], h_lo[:, t, :]), t == 0, t == KD - 1)
                        mm.then_inc(used, 1)

            @block.scalar
            def _(act):
                def split(g):
                    if g < 2 * NM:
                        n, half = divmod(g, 2)
                        act.wait_ge(used, g + 1)
                        act.copy(w_hi[:, g % WB].rearrange("p a f -> p (a f)"),
                                 k.slot(act, cf_slots + n)[:, half * HALF:(half + 1) * HALF, :].rearrange("p a f -> p (a f)")
                                 ).then_inc(w_rounded, 1)

                def next_splits(n):
                    split(2 * n + WB)
                    split(2 * n + WB + 1)

                norm_scalar(k, act, norm, x, T2)
                for g in range(WB):
                    split(g)
                mod_norm_shift(k, act, (0, 1), shift, made, ready)
                act.drain()
                for t in range(KD):
                    act.copy(h_hi[:, t, :], k.h[:, t, :]).then_inc(rounded, 1)
                for m in range(KD):
                    next_splits(2 * m)
                    next_splits(2 * m + 1)
                    act.wait_ge(used, done(2 * m + 1))
                    if m >= 2:
                        act.wait_ge(freed, 2 * m - 2)
                    act.activation(keep[:, m % 2, :], k.ps[:, (2 * m + 1) % BANKS, :], ACT.Sigmoid).then_inc(gated, 1)
                act.wait_ge(dt_abs, 1)
                act.activation(raw[:, 1, :], raw[:, 1, :], ACT.Exp, scale=-1.0)
                act.drain()
                act.activation(raw[:, 1, :], raw[:, 1, :], ACT.Ln, bias=k.ones[:, 0:1]).then_inc(dt_log, 1)
                act.wait_ge(freed, 16)
                for m in range(KD):
                    n = 16 + m
                    next_splits(n)
                    act.wait_ge(used, done(n))
                    act.activation(zs[:, m, :], k.ps[:, n % BANKS, :], ACT.Silu).then_inc(based, 1)
                for m in range(XBC):
                    n = 24 + m
                    next_splits(n)
                    act.wait_ge(used, done(n))
                    act.activation(xbc[:, m, :], k.ps[:, n % BANKS, :], ACT.Identity, scale=ctaps[:, m, SCONV // 2:SCONV // 2 + 1],
                                   bias=ctaps[:, m, SCONV:SCONV + 1]).then_inc(based, 1)
                    if m >= 1:
                        act.wait_ge(conved, m)
                        act.activation(xbc[:, m - 1, :], xbc[:, m - 1, :], ACT.Silu)
                act.wait_ge(conved, XBC)
                act.activation(xbc[:, XBC - 1, :], xbc[:, XBC - 1, :], ACT.Silu)

            def cf_taps(m0):
                return [(m0, j) for j in [CFK // 2] + [j for j in range(CFK) if j != CFK // 2]]

            def cf_tap(engine, m0, j):
                s = j - CFK // 2
                for m in (m0, m0 + 1):
                    if s == 0:
                        engine.tensor_scalar(cf[:, m, :], u[:, m, :], ftaps[:, m, j:j + 1], ftaps[:, m, CFK:CFK + 1],
                                             ALU.mult, ALU.add)
                        continue
                    lo, hi = max(0, -s), max(0, s)
                    for rows in (1, ROWS):
                        w = T // rows
                        part = slice(0, T) if rows == 1 else slice(T, T2)
                        o = cf[:, m, part].rearrange("p (r w) -> p r w", r=rows)[:, :, lo:w - hi]
                        i = u[:, m, part].rearrange("p (r w) -> p r w", r=rows)[:, :, lo + s:w - hi + s]
                        engine.scalar_tensor_tensor(o, i, ftaps[:, m, j:j + 1], o, ALU.mult, ALU.add)
                engine.drain()

            @block.gpsimd
            def _(pool):
                pool.wait_ge(dt_product, 1)
                pool.wait_ge(h_split, KD)
                pool.wait_ge(u_made, POOL_TILES)
                for m, j in cf_taps(0):
                    s = j - CFK // 2
                    for i in range(POOL_TILES):
                        if s == 0:
                            pool.tensor_scalar(cf[:, i, :], u[:, i, :], ftaps[:, i, j:j + 1], ftaps[:, i, CFK:CFK + 1],
                                               ALU.mult, ALU.add)
                        else:
                            pool.tensor_scalar(scaled[i][:, :], u[:, i, :], ftaps[:, i, j:j + 1], None, ALU.mult)
                    pool.drain()
                    if s:
                        lo, hi = max(0, -s), max(0, s)
                        for rows in (1, ROWS):
                            w = T // rows
                            part = slice(0, T) if rows == 1 else slice(T, T2)
                            for i in range(POOL_TILES):
                                o = cf[:, i, part].rearrange("p (r w) -> p r w", r=rows)[:, :, lo:w - hi]
                                of = scaled[i][:, part].rearrange("p (r w) -> p r w", r=rows)[:, :, lo + s:w - hi + s]
                                pool.tensor_tensor(o, of, o, ALU.add)
                        pool.drain()

            @block.vector
            def _(dve):
                def split(g):
                    if g < 2 * NM:
                        n, half = divmod(g, 2)
                        dve.wait_ge(w_rounded, g + 1)
                        dve.tensor_tensor(w_lo[:, g % WB], k.ring[:, (cf_slots + n) % RING, half * HALF:(half + 1) * HALF, :],
                                          w_hi[:, g % WB], ALU.subtract).then_inc(w_split, 1)

                def next_splits(n):
                    split(2 * n + WB)
                    split(2 * n + WB + 1)

                mod_norm_vector(k, dve, norm, x, (0, 1), gain, T2, made)
                for g in range(WB):
                    split(g)
                for t in range(KD):
                    dve.wait_ge(rounded, t + 1)
                    dve.tensor_tensor(h_lo[:, t, :], k.h[:, t, :], h_hi[:, t, :], ALU.subtract).then_inc(h_split, 1)
                dve.wait_ge(dt_product, 1)
                bias = col("dt_bias").unsqueeze(1).broadcast_to([P, TT, 32])
                three = raw[:, 0, :].rearrange("p (t c) -> p t c", t=TT)
                dve.tensor_tensor(three, k.ps[:, 6, 0:TT * 32].rearrange("p (t c) -> p t c", t=TT), bias, ALU.add)
                dve.drain()
                dve.scalar_tensor_tensor(raw[:, 1, :], raw[:, 0, :], -1.0, raw[:, 0, :], ALU.mult, ALU.max).then_inc(dt_abs, 1)
                for m in range(KD):
                    next_splits(2 * m)
                    next_splits(2 * m + 1)
                    dve.wait_ge(gated, m + 1)
                    dve.tensor_tensor(u[:, m, :], k.ps[:, 2 * m % BANKS, :], keep[:, m % 2, :], ALU.mult).then_inc(u_made, 1)
                    dve.drain()
                    dve.sem_inc(freed, 2)
                dve.wait_ge(dt_log, 1)
                dve.scalar_tensor_tensor(dt[:, :, :].rearrange("p t c -> p (t c)"), raw[:, 0, :], 0.0, raw[:, 1, :],
                                         ALU.max, ALU.add)
                work = [w for m0 in range(POOL_TILES, KD, 2) for w in cf_taps(m0)]
                steps = 8 + XBC
                taken = 0
                for n in range(steps):
                    next_splits(16 + n)
                    dve.wait_ge(based, n + 1)
                    if n < 8:
                        dve.sem_inc(freed, 1)
                    else:
                        m, bank = n - 8, (16 + n) % BANKS
                        for j in (0, 1, 3, 4):
                            s = j - SCONV // 2
                            lo, hi = max(0, -s), max(0, s)
                            last = dve.scalar_tensor_tensor(
                                halves(xbc[:, m, :])[:, :, lo:T - hi], halves(k.ps[:, bank, :])[:, :, lo + s:T - hi + s],
                                ctaps[:, m, j:j + 1], halves(xbc[:, m, :])[:, :, lo:T - hi], ALU.mult, ALU.add)
                            if j < 4:
                                dve.drain()
                        last.then_inc(conved, 1)
                        dve.drain()
                        dve.sem_inc(freed, 1)
                    upto = len(work) * (n + 1) // steps
                    for m0, j in work[taken:upto]:
                        cf_tap(dve, m0, j)
                    taken = upto


def ssd(k, col, tri, dt, zs, xbc):
    nc = k.nc
    spare = k.sq[:, :, :].rearrange("p a b -> p (a b)")
    b_tok = spare[:, 0:TT * SG * SN].rearrange("p (t f) -> p t f", t=TT)
    states = spare[:, TT * SG * SN:].rearrange("p (d f) -> p d f", d=2)
    y = xbc[:, 0:XS_TILES, :].rearrange("p a b -> p (a b)").rearrange("p (t f) -> p t f", t=TT)
    bf, cf_ = xbc[:, XS_TILES:XS_TILES + SG, :], xbc[:, XS_TILES + SG:, :]
    GW = SREP * SP_
    with ExitStack() as local:
        def sb(name, shape):
            return local.enter_context(nc.sbuf_tensor(name, shape, F32))

        xs_tok = sb("xs_tok", [P, TT, SH * SP_])
        la = sb("la", [P, TT, 2, SH])
        aneg = sb("aneg", [P, 2 * SH])
        acum = sb("acum", [P, TT, 2, SH])
        to_end = sb("to_end", [P, TT, 2, SH])
        eacum = sb("eacum", [P, TT, 2, SH])
        cdec = sb("cdec", [P, TT, 2, SH])
        dt4 = dt[:, :, :].rearrange("p t (d h) -> p t d h", d=2)
        with stage_semaphores(nc, "ssd_prep", "a_ready", "la_ready", "turned", "kept", "summed", "ended", "skipped") as sems, \
                nc.Block(name="ssd_prep", no_gpsimd_drain=True) as block:
            a_ready, la_ready, turned, kept, summed, ended, skipped = sems
            NT = 12

            @block.tensor
            def _(pe):
                for tt in range(TT):
                    for b in range(3):
                        n = tt * 3 + b
                        if n >= 6:
                            pe.wait_ge(kept, n - 5)
                        for j in range(4):
                            mm = pe.transpose(k.ps[:, n % 6, j * P:(j + 1) * P], xbc[:, b * 4 + j, tt * P:(tt + 1) * P], k.ident[:, :])
                        mm.then_inc(turned, 1)
                pe.wait_ge(la_ready, 1)
                for c in range(TT):
                    for d in range(2):
                        at = (c * 2 + d) * SH
                        pe.matmul(k.ps[:, 6, at:at + SH], tri[:, d, :], la[:, c, d, :], start=True, stop=True)
                        mm = pe.matmul(k.ps[:, 7, at:at + SH], k.ones[:, :], la[:, c, d, :], start=True, stop=True)
                mm.then_inc(summed, 1)

            @block.scalar
            def _(act):
                act.activation(aneg[:, :], col("a_log"), ACT.Exp).then_inc(a_ready, 1)
                for n in range(TT * 3):
                    act.wait_ge(turned, n + 1)
                    tt, b = divmod(n, 3)
                    to = xs_tok[:, tt, b * 512:(b + 1) * 512] if b < 2 else b_tok[:, tt, :]
                    act.activation(to, k.ps[:, n % 6, :], ACT.Copy).then_inc(kept, 1)
                act.wait_ge(ended, 1)
                for a in (to_end, eacum, cdec):
                    act.activation(a[:, :, :, :], a[:, :, :, :], ACT.Exp)

            @block.vector
            def _(dve):
                dve.memset(states, 0.0)
                dve.wait_ge(a_ready, 1)
                dve.tensor_scalar(aneg[:, :], aneg[:, :], -1.0, None, ALU.mult)
                dve.drain()
                dve.tensor_tensor(la[:, :, :, :].rearrange("p t d h -> p t (d h)"), dt[:, :, :],
                                  aneg[:, :].unsqueeze(1).broadcast_to([P, TT, 2 * SH]), ALU.mult).then_inc(la_ready, 1)
                dve.wait_ge(summed, 1)
                flat = [a[:, :, :, :].rearrange("p t d h -> p (t d h)") for a in (acum, to_end, eacum, cdec)]
                dve.tensor_copy(flat[0], k.ps[:, 6, 0:TT * 2 * SH])
                dve.tensor_copy(flat[3], k.ps[:, 7, 0:TT * 2 * SH])
                dve.drain()
                dve.tensor_copy(flat[2], flat[0])
                dve.tensor_tensor(flat[1], flat[3], flat[0], ALU.subtract).then_inc(ended, 1)
                dve.wait_ge(kept, TT * 3)
                for tt in range(TT):
                    dve.tensor_tensor(y[:, tt, :].rearrange("p (h d) -> p h d", h=SH),
                                      xs_tok[:, tt, :].rearrange("p (h d) -> p h d", h=SH),
                                      col("ssd_d").unsqueeze(2).broadcast_to([P, SH, SP_]), ALU.mult)

        xdt = sb("xdt", [P, 2, SH * SP_])
        xw = sb("xw", [P, 2, SH * SP_])
        seg = sb("seg", [P, 2, SREP, P])
        cbm = sb("cbm", [P, 2, P])
        yo = sb("yo", [P, GW])
        units = [(s, d, (s if d == 0 else s ^ 1), g) for s in range(TT) for d in range(2) for g in range(SG)]
        with stage_semaphores(nc, "ssd", "rows", "segs", "exps", "mixed", "summed", "added", "scaled") as sems, \
                nc.Block(name="ssd_scan", no_gpsimd_drain=True) as block:
            rows, segs, exps, mixed, summed, added, scaled = sems

            @block.tensor
            def _(pe):
                def front(u):
                    s, d, c, g = units[u]
                    if u >= 2:
                        pe.wait_ge(segs, u - 1)
                    for h in range(SREP):
                        pe.matmul(k.ps[:, u % 2, h * P:(h + 1) * P],
                                  la[:, c, d, g * SREP + h:g * SREP + h + 1].broadcast_to([P, P]), tri[:, d, :],
                                  start=True, stop=True)
                    pe.matmul(k.ps[:, 2 + u % 2, 0:P], bf[:, g, c * P:(c + 1) * P], cf_[:, g, c * P:(c + 1) * P],
                              start=True, stop=True).then_inc(rows, 1)

                front(0)
                front(1)
                for u, (s, d, c, g) in enumerate(units):
                    if u + 2 < len(units):
                        front(u + 2)
                    pe.wait_ge(mixed, u + 1)
                    if u >= 2:
                        pe.wait_ge(added, u - 1)
                    for h in range(SREP):
                        hh = g * SREP + h
                        pe.matmul(k.ps[:, 4 + u % 2, h * SP_:(h + 1) * SP_], seg[:, u % 2, h, :],
                                  xdt[:, (u // SG) % 2, hh * SP_:(hh + 1) * SP_], start=True, stop=True)
                    if s:
                        pe.wait_ge(added, u - 2 * SG + 1)
                    pe.matmul(k.ps[:, 4 + u % 2, GW:2 * GW], cf_[:, g, c * P:(c + 1) * P], states[:, d, g * GW:(g + 1) * GW],
                              start=True, stop=True)
                    pe.matmul(k.ps[:, 6 + u % 2, 0:GW], b_tok[:, c, g * SN:(g + 1) * SN],
                              xw[:, (u // SG) % 2, g * GW:(g + 1) * GW], start=True, stop=True).then_inc(summed, 1)

            @block.scalar
            def _(act):
                for u in range(len(units)):
                    act.wait_ge(segs, u + 1)
                    act.activation(seg[:, u % 2], seg[:, u % 2], ACT.Exp).then_inc(exps, 1)

            @block.vector
            def _(dve):
                def heads(ap):
                    return ap.rearrange("p (h e) -> p h e", e=SP_)

                def front(u):
                    s, d, c, g = units[u]
                    if g == 0:
                        v = (u // SG) % 2
                        if u >= 2 * SG:
                            dve.wait_ge(summed, u - SG)
                        dve.tensor_tensor(heads(xdt[:, v, :]), heads(xs_tok[:, c, :]),
                                          dt4[:, c, d, :].unsqueeze(2).broadcast_to([P, SH, SP_]), ALU.mult)
                        dve.drain()
                        dve.tensor_tensor(heads(xw[:, v, :]), heads(xdt[:, v, :]),
                                          to_end[:, c, d, :].unsqueeze(2).broadcast_to([P, SH, SP_]), ALU.mult)
                    dve.wait_ge(rows, u + 1)
                    if u >= 2:
                        dve.wait_ge(summed, u - 1)
                    a = acum[:, c, d, g * SREP:(g + 1) * SREP].unsqueeze(2).broadcast_to([P, SREP, P])
                    dve.tensor_tensor(cbm[:, u % 2, :], k.ps[:, 2 + u % 2, 0:P], tri[:, d, :], ALU.mult)
                    dve.tensor_tensor(seg[:, u % 2], k.ps[:, u % 2, :].rearrange("p (h l) -> p h l", h=SREP), a, ALU.min)
                    dve.drain()
                    dve.tensor_tensor(seg[:, u % 2], seg[:, u % 2], a, ALU.subtract).then_inc(segs, 1)

                def back(u):
                    s, d, c, g = units[u]
                    dve.wait_ge(summed, u + 1)
                    dve.tensor_tensor(heads(yo[:, :]), heads(k.ps[:, 4 + u % 2, GW:2 * GW]),
                                      eacum[:, c, d, g * SREP:(g + 1) * SREP].unsqueeze(2).broadcast_to([P, SREP, SP_]), ALU.mult)
                    yy = y[:, c, g * GW:(g + 1) * GW]
                    dve.tensor_tensor(yy, yy, k.ps[:, 4 + u % 2, 0:GW], ALU.add)
                    st = states[:, d, g * GW:(g + 1) * GW]
                    dve.tensor_tensor(heads(st), heads(st),
                                      cdec[:, c, d, g * SREP:(g + 1) * SREP].unsqueeze(2).broadcast_to([P, SREP, SP_]), ALU.mult)
                    dve.drain()
                    dve.tensor_tensor(yy, yy, yo[:, :], ALU.add)
                    dve.tensor_tensor(st, st, k.ps[:, 6 + u % 2, 0:GW], ALU.add).then_inc(added, 1)
                    dve.drain()

                front(0)
                for u in range(len(units)):
                    if u + 1 < len(units):
                        front(u + 1)
                    dve.wait_ge(exps, u + 1)
                    dve.tensor_tensor(seg[:, u % 2], seg[:, u % 2], cbm[:, u % 2, :].unsqueeze(1).broadcast_to([P, SREP, P]),
                                      ALU.mult).then_inc(mixed, 1)
                    if u:
                        back(u - 1)
                back(len(units) - 1)

    with stage_semaphores(nc, "ssd_out", *NORM_SEMS, "turned", "gated") as sems, \
            nc.Block(name="ssd_readout", no_gpsimd_drain=True) as block:
        norm, (turned, gated) = sems[:4], sems[4:]

        @block.tensor
        def _(pe):
            for m in range(KD):
                if m >= 4:
                    pe.wait_ge(gated, m - 3)
                for tt in range(TT):
                    mm = pe.transpose(k.ps[:, m % 4, tt * P:(tt + 1) * P], y[:, tt, m * P:(m + 1) * P], k.ident[:, :])
                mm.then_inc(turned, 1)
            norm_tensor(k, pe, norm, T2)

        @block.scalar
        def _(act):
            for m in range(KD):
                act.wait_ge(gated, m + 1)
                act.activation(k.sq[:, m, :], zs[:, m, :], ACT.Square).then_inc(norm[0], 1)
            act.wait_ge(norm[1], 1)
            act.activation(k.root[:, :], k.ps[:, NORM_BANK, :], ACT.Sqrt, scale=1.0 / D, bias=k.eps[:, 0:1]).then_inc(norm[2], 1)

        @block.vector
        def _(dve):
            for m in range(KD):
                dve.wait_ge(turned, m + 1)
                dve.tensor_tensor(zs[:, m, :], k.ps[:, m % 4, :], zs[:, m, :], ALU.mult).then_inc(gated, 1)
            norm_vector(k, dve, norm, zs, zs, col("ssd_norm_g"), T2)


def conformer_norm(k, cf, gain, bias):
    nc = k.nc
    with stage_semaphores(nc, "cf_norm", *NORM_SEMS, "mean_done", "centred") as sems, \
            nc.Block(name="conformer_norm", no_gpsimd_drain=True) as block:
        norm, (mean_done, centred) = sems[:4], sems[4:]

        @block.tensor
        def _(pe):
            for t in range(KD):
                mm = pe.matmul(k.ps[:, 0, :], k.ones[:, :], cf[:, t, :], start=(t == 0), stop=(t == KD - 1))
            mm.then_inc(mean_done, 1)
            norm_tensor(k, pe, norm, T2)

        @block.vector
        def _(dve):
            dve.wait_ge(mean_done, 1)
            for t in range(KD):
                dve.scalar_tensor_tensor(cf[:, t, :], k.ps[:, 0, :], -1.0 / D, cf[:, t, :], ALU.mult, ALU.add).then_inc(centred, 1)
            dve.wait_ge(norm[2], 1)
            dve.reciprocal(k.rstd[:, :], k.root[:, :])
            dve.drain()
            for t in range(KD):
                dve.tensor_tensor(cf[:, t, :], cf[:, t, :], k.rstd[:, :], ALU.mult).then_inc(norm[3], 1)

        @block.scalar
        def _(act):
            for t in range(KD):
                act.wait_ge(centred, t + 1)
                act.activation(k.sq[:, t, :], cf[:, t, :], ACT.Square).then_inc(norm[0], 1)
            act.wait_ge(norm[1], 1)
            act.activation(k.root[:, :], k.ps[:, NORM_BANK, :], ACT.Sqrt, scale=1.0 / D, bias=k.eps[:, 0:1]).then_inc(norm[2], 1)
            for t in range(KD):
                act.wait_ge(norm[3], t + 1)
                act.activation(cf[:, t, :], cf[:, t, :], ACT.Silu, scale=gain[:, t:t + 1], bias=bias[:, t:t + 1])


def even_out(k, x, zs, cf, gate):
    nc = k.nc
    per = 2
    first = k.take(KD * per)
    with stage_semaphores(nc, "even_out", "product") as (product,), nc.Block(name="even_out", no_gpsimd_drain=True) as block:

        @block.sync
        def _(sp):
            k.refill(sp, first, KD * per, product, per=per)

        @block.tensor
        def _(pe):
            for m in range(KD):
                for c, inp in enumerate((zs, cf)):
                    w = k.slot(pe, first + m * per + c)
                    for t in range(TILES):
                        mm = pe.matmul(k.ps[:, m, :], w[:, t, :], inp[:, t, :], start=(c + t == 0), stop=(c == 1 and t == TILES - 1))
                mm.then_inc(product, 1)

        @block.vector
        def _(dve):
            for m in range(KD):
                dve.wait_ge(product, m + 1)
                for s in range(SEGS):
                    xs = x[:, m, s * T:(s + 1) * T]
                    dve.scalar_tensor_tensor(xs, k.ps[:, m, s * T:(s + 1) * T], gate[:, m, s:s + 1], xs, ALU.mult, ALU.add)


def moe(k, x, segs, gain, shift, gate, router_w, router_b, slot_number, name):
    nc = k.nc
    n = len(segs) * T
    x0 = segs[0] * T
    tt_n = n // P
    first = k.take(EXPERTS * RING)
    with ExitStack() as local:
        def sb(nm, shape, dtype=F32):
            return local.enter_context(nc.sbuf_tensor(f"{name}_{nm}", shape, dtype))

        comb = sb("comb", [P, tt_n, EXPERTS])
        place = sb("place", [P, tt_n, EXPERTS])
        late = sb("late", [P, tt_n, EXPERTS])
        most = sb("most", [P, 1], I32)
        with nc.sbuf_tensor(f"{name}_token_rows", [P, tt_n, D], F32) as rows:
            moe_route(k, x, segs, gain, shift, router_w, router_b, name, n, tt_n, comb, place, late, most, rows)
            moe_experts(k, x, segs, gate, name, n, tt_n, first, comb, place, rows, slot_number)
        fullest = nc.values_load(most[0:1, 0:1], min_val=0, max_val=n,
                                 skip_runtime_bounds_check_because="a count of n tokens")
        moe_late(k, x, segs, gate, name + "_late", n, tt_n, first, late, fullest)


def moe_route(k, x, segs, gain, shift, router_w, router_b, name, n, tt_n, comb, place, late, most, rows):
    nc = k.nc
    x0 = segs[0] * T
    xin = x[:, :, x0:x0 + n]
    with ExitStack() as local:
        def sb(nm, shape, dtype=F32):
            return local.enter_context(nc.sbuf_tensor(f"{name}_{nm}", shape, dtype))

        score = sb("score", [P, tt_n, EGROUPS, EPG])
        sel = sb("sel", [P, tt_n, EGROUPS, EPG])
        chosen = sb("chosen", [P, tt_n, EXPERTS])
        w3 = sb("w3", [P, 8, tt_n * EGROUPS])
        rank = sb("rank", [P, tt_n, EGROUPS, EPG])
        top = sb("top", [P, 4, tt_n])
        with stage_semaphores(nc, f"{name}_route", *NORM_SEMS, "made", "ready", "routed", "scored", "picked", "placed",
                              "turned", "kept") as sems, nc.Block(name=f"{name}_route", no_gpsimd_drain=True) as block:
            norm, (made, ready, routed, scored, picked, placed, turned, kept) = sems[:4], sems[4:]
            UNITS, BANKS = 2 * tt_n, 4

            @block.tensor
            def _(pe):
                norm_tensor(k, pe, norm, n)
                pe.wait_ge(ready, KD * len(segs))
                for tt in range(tt_n):
                    for t in range(KD):
                        mm = pe.matmul(k.ps[:, 6, tt * EXPERTS:(tt + 1) * EXPERTS], k.h[:, t, tt * P:(tt + 1) * P],
                                       router_w[:, t, :], start=(t == 0), stop=(t == KD - 1))
                mm.then_inc(routed, 1)
                for u in range(UNITS):
                    if u >= BANKS:
                        pe.wait_ge(kept, u - BANKS + 1)
                    for j in range(4):
                        mm = pe.transpose(k.ps[:, u % BANKS, j * P:(j + 1) * P],
                                          k.h[:, u % 2 * 4 + j, u // 2 * P:(u // 2 + 1) * P], k.ident[:, :])
                    mm.then_inc(turned, 1)
                pe.wait_ge(picked, 1)
                for tt in range(tt_n):
                    for s in range(tt + 1):
                        pe.matmul(k.ps[:, NORM_BANK, tt * EXPERTS:(tt + 1) * EXPERTS], k.upto[:, :] if s == tt else k.ones[:, :],
                                  chosen[:, s, :], start=(s == 0), stop=(s == tt))
                for s in range(tt_n):
                    mm = pe.matmul(k.ps[:, NORM_BANK, tt_n * EXPERTS:(tt_n + 1) * EXPERTS], k.ones[:, :], chosen[:, s, :],
                                   start=(s == 0), stop=(s == tt_n - 1))
                mm.then_inc(placed, 1)

            @block.scalar
            def _(act):
                norm_scalar(k, act, norm, xin, n)
                mod_norm_shift(k, act, segs, shift, made, ready)
                act.wait_ge(routed, 1)
                act.activation(score[:, :, :, :].rearrange("p t g e -> p (t g e)"), k.ps[:, 6, 0:tt_n * EXPERTS], ACT.Sigmoid
                               ).then_inc(scored, 1)
                for u in range(UNITS):
                    act.wait_ge(turned, u + 1)
                    act.copy(rows[:, u // 2, u % 2 * 512:(u % 2 + 1) * 512], k.ps[:, u % BANKS, :]).then_inc(kept, 1)

            @block.vector
            def _(dve):
                mod_norm_vector(k, dve, norm, x, segs, gain, n, made)
                dve.wait_ge(scored, 1)
                G = tt_n * EGROUPS
                s4 = score[:, :, :, :].rearrange("p t g e -> p (t g) e")
                v4 = sel[:, :, :, :].rearrange("p t g e -> p (t g) e")
                r4 = rank[:, :, :, :].rearrange("p t g e -> p (t g) e")
                wk = [w3[:, i, :] for i in range(8)]

                def tt_(o, a, b, op):
                    dve.tensor_tensor(o, a, b, op)
                    dve.drain()

                tt_(sel[:, :, :, :].rearrange("p t g e -> p t (g e)"), score[:, :, :, :].rearrange("p t g e -> p t (g e)"),
                    router_b.unsqueeze(1).broadcast_to([P, tt_n, EXPERTS]), ALU.add)
                e = [v4[:, :, i] for i in range(EPG)]
                tt_(wk[0], e[0], e[1], ALU.max)
                tt_(wk[1], e[0], e[1], ALU.min)
                tt_(wk[2], e[2], e[3], ALU.max)
                tt_(wk[3], e[2], e[3], ALU.min)
                tt_(wk[4], wk[0], wk[2], ALU.max)
                tt_(wk[5], wk[0], wk[2], ALU.min)
                tt_(wk[6], wk[1], wk[3], ALU.max)
                tt_(wk[5], wk[5], wk[6], ALU.max)
                tt_(wk[4], wk[4], wk[5], ALU.add)
                gs = wk[4].rearrange("p (t g) -> p t g", g=EGROUPS)
                isg = wk[5].rearrange("p (t g) -> p t g", g=EGROUPS)
                dve.tensor_reduce(top[:, 0, :], gs, AX.X, ALU.max)
                dve.drain()
                tt_(isg, gs, top[:, 0, :].unsqueeze(2).broadcast_to([P, tt_n, EGROUPS]), ALU.is_equal)
                dve.memset(top[:, 1, :], 1.0)
                dve.drain()
                for g in range(EGROUPS):
                    tt_(isg[:, :, g], isg[:, :, g], top[:, 1, :], ALU.mult)
                    tt_(top[:, 1, :], top[:, 1, :], isg[:, :, g], ALU.subtract)
                dve.memset(rank[:, :, :, :], 0.0)
                dve.drain()
                for i in range(EPG):
                    for j in range(i + 1, EPG):
                        tt_(wk[0], e[j], e[i], ALU.is_gt)
                        tt_(r4[:, :, i], r4[:, :, i], wk[0], ALU.add)
                        dve.tensor_scalar(wk[1], wk[0], -1.0, 1.0, ALU.mult, ALU.add)
                        dve.drain()
                        tt_(r4[:, :, j], r4[:, :, j], wk[1], ALU.add)
                dve.tensor_scalar(rank[:, :, :, :], rank[:, :, :, :], TOPK - 0.5, None, ALU.is_lt)
                dve.drain()
                c4 = chosen[:, :, :].rearrange("p t (g e) -> p (t g) e", g=EGROUPS)
                tt_(c4, r4, wk[5].unsqueeze(2).broadcast_to([P, G, EPG]), ALU.mult)
                dve.sem_inc(picked, 1)
                tt_(r4, c4, s4, ALU.mult)
                dve.tensor_reduce(top[:, 2, :], rank[:, :, :, :].rearrange("p t g e -> p t (g e)"), AX.X, ALU.add)
                dve.drain()
                dve.reciprocal(top[:, 3, :], top[:, 2, :])
                dve.drain()
                tt_(comb[:, :, :], rank[:, :, :, :].rearrange("p t g e -> p t (g e)"),
                    top[:, 3, :].unsqueeze(2).broadcast_to([P, tt_n, EXPERTS]), ALU.mult)
                dve.wait_ge(placed, 1)
                upto = k.ps[:, NORM_BANK, 0:tt_n * EXPERTS].rearrange("p (t e) -> p t e", e=EXPERTS)
                tt_(place[:, :, :], upto, chosen[:, :, :], ALU.mult)
                dve.tensor_scalar(late[:, :, :], place[:, :, :], P + 0.5, None, ALU.is_gt)
                dve.tensor_scalar(place[:, :, :], place[:, :, :], -1.0, None, ALU.add)
                dve.tensor_reduce(top[:, 0, 0:1], k.ps[:, NORM_BANK, tt_n * EXPERTS:(tt_n + 1) * EXPERTS], AX.X, ALU.max)
                dve.drain()
                dve.tensor_copy(most[:, :], top[:, 0, 0:1])
                tt_(late[:, :, :], late[:, :, :], comb[:, :, :], ALU.mult)


def moe_experts(k, x, segs, gate, name, n, tt_n, first, comb, place, rows, slot_number):
    nc = k.nc
    GU = KD
    with ExitStack() as local:
        def sb(nm, shape, dtype=F32):
            return local.enter_context(nc.sbuf_tensor(f"{name}_{nm}", shape, dtype))

        WB = 4
        w_hi = sb("w_hi", [P, WB, 2, 512], F32R)
        w_lo = sb("w_lo", [P, WB, 2, 512], F32R)
        onehot = sb("onehot", [P, 2, tt_n, P])
        turned_hot = sb("turned_hot", [P, n], F32R)
        own = sb("own", [P, 2, KD, P], F32R)
        act_g = sb("act_g", [P, 512])
        hid = sb("hid", [P, 512])
        hid_t = sb("hid_t", [P, 2, KE, P], F32R)
        slot_w = sb("slot_w", [P, 1])
        y = sb("y", [P, 2, D], F32R)
        UP, GATHER, DOWN, TURN_HOT, TURN_HID, SCATTER = 0, 2, 4, 4, 5, 6
        gated_y = sb("gated_y", [P, 2, n])
        PRE = 2
        BEHIND = (0, 0, 2, 2, 1, 1, 1, 1)
        with stage_semaphores(nc, f"{name}_experts", "selected", "gathered", "own_rounded", "own_split", "used", "w_rounded",
                              "w_split", "gated", "hidden", "hid_turned", "hid_rounded", "hid_split", "hot_turned", "hot_kept",
                              "weighed", "weight_kept", "y_rounded", "y_split", "scattered", "taken",
                              "added") as sems, nc.Block(name=f"{name}_experts", no_gpsimd_drain=True) as block:
            (selected, gathered, own_rounded, own_split, used, w_rounded, w_split, gated, hidden, hid_turned, hid_rounded,
             hid_split, hot_turned, hot_kept, weighed, weight_kept, y_rounded, y_split, scattered, taken, added) = sems

            def rounds(engine, expert):
                for s in range(2):
                    expert(s, s, s == 0, False)
                with engine.Fori(1, EXPERTS // 2 - 1) as i:
                    for s in range(2):
                        expert(i * 2 + s, s, False, False)
                for s in range(2):
                    expert(EXPERTS - 2 + s, s, False, s == 1)

            @block.sync
            def _(sp):
                count = EXPERTS if first + EXPERTS * RING + RING <= k.n_slots else EXPERTS - 1

                def one(s, e):
                    sp.wait_ge(w_split, e * RING + s + 1)
                    at = (first + s) % RING
                    sp.dma_start(k.ring[:, at], k.weights[first + s + RING + e * RING]).then_inc(k.landed[at], 16)

                with sp.Fori(0, count) as e:
                    for s in range(RING):
                        one(s, e)
                if count < EXPERTS:
                    for s in range(k.n_slots - first - EXPERTS * RING):
                        one(s, EXPERTS - 1)

            @block.tensor
            def _(pe):
                def gather(e, s, half, first_one=False):
                    pe.wait_ge(selected, e + 1)
                    if not first_one:
                        pe.wait_ge(own_split, e * 2 + half - 1)
                    for f in range(4):
                        t = half * 4 + f
                        for tt in range(tt_n):
                            mm = pe.matmul(k.ps[:, GATHER + half, f * P:(f + 1) * P], rows[:, tt, t * P:(t + 1) * P],
                                           onehot[:, s, tt, :], start=(tt == 0), stop=(tt == tt_n - 1))
                    mm.then_inc(gathered, 1)

                def scatter(e, m):
                    if m == 0:
                        pe.wait_ge(y_split, e * 2 + 2)
                        pe.wait_ge(hot_kept, e + 1)
                    pe.wait_ge(taken, e * KD + m + 1)
                    for part in range(2):
                        mm = pe.matmul(k.ps[:, SCATTER + m % 2, 0:n], y[:, part, m * P:(m + 1) * P], turned_hot[:, :],
                                       start=(part == 0), stop=(part == 1))
                    mm.then_inc(scattered, 1)

                def slot(e, s, own_parts, bank, is_first, is_last):
                    pe.wait_ge(w_split, e * RING + s + 1)
                    for half in range(2):
                        out = k.ps[:, bank + half, :]
                        wh, wl = w_hi[:, s % WB, half, :], w_lo[:, s % WB, half, :]
                        mm = product_of_parts(pe, out, own_parts, (wh, wl), is_first, is_last)
                    mm.then_inc(used, 1)

                def expert(e, s, start, end):
                    pe.wait_ge(own_split, e * 2 + 2)
                    if not start:
                        pe.wait_ge(weight_kept, e)
                    m = 0
                    for t in range(GU):
                        slot(e, t, (own[:, 0, t, :], own[:, 1, t, :]), UP, t == 0, t == GU - 1)
                        if not start:
                            for _ in range(BEHIND[t]):
                                scatter(e - 1, m)
                                m += 1
                    for tt in range(tt_n):
                        mm = pe.transpose(k.ps[:, TURN_HOT, tt * P:(tt + 1) * P], onehot[:, s, tt, :], k.ident[:, :])
                    mm.then_inc(hot_turned, 1)
                    if not end:
                        gather(e + 1, 1 - s, 0)
                    pe.wait_ge(hidden, e + 1)
                    for j in range(KE):
                        mm = pe.transpose(k.ps[:, TURN_HID, j * P:(j + 1) * P], hid[:, j * P:(j + 1) * P], k.ident[:, :])
                    mm.then_inc(hid_turned, 1)
                    for tt in range(tt_n):
                        mm = pe.matmul(k.ps[:, UP, 0:1], onehot[:, s, tt, :], comb[:, tt, bass.ds(e, 1)],
                                       start=(tt == 0), stop=(tt == tt_n - 1))
                    mm.then_inc(weighed, 1)
                    if not end:
                        gather(e + 1, 1 - s, 1)
                    pe.wait_ge(hot_kept, e + 1)
                    pe.wait_ge(hid_split, e + 1)
                    for t in range(KE):
                        slot(e, GU + t, (hid_t[:, 0, t, :], hid_t[:, 1, t, :]), DOWN, t == 0, t == KE - 1)

                pe.sem_inc(used, WB)
                for half in range(2):
                    gather(0, 0, half, True)
                rounds(pe, expert)
                for m in range(KD):
                    scatter(EXPERTS - 1, m)

            @block.scalar
            def _(act):
                def split(e, s):
                    act.wait_ge(used, e * RING + s + 1)
                    act.copy(w_hi[:, s % WB].rearrange("p h f -> p (h f)"),
                             k.slot(act, first + s, e).rearrange("p a f -> p (a f)")).then_inc(w_rounded, 1)

                def round_own(e, half):
                    act.wait_ge(gathered, e * 2 + half + 1)
                    act.copy(own[:, 0, half * 4:(half + 1) * 4, :].rearrange("p a f -> p (a f)"), k.ps[:, GATHER + half, :]
                             ).then_inc(own_rounded, 1)

                def take(e, m):
                    act.wait_ge(scattered, e * KD + m + 1)
                    act.wait_ge(added, e * KD + m + 1)
                    for j, s in enumerate(segs):
                        part = slice(j * T, (j + 1) * T)
                        mu = act.mul(gated_y[:, m % 2, part], k.ps[:, SCATTER + m % 2, part], gate[:, m, s:s + 1])
                    mu.then_inc(taken, 1)

                def expert(e, s, start, end):
                    m = 0
                    for t in range(GU):
                        split(e, WB + t)
                        if not start:
                            for _ in range(BEHIND[t]):
                                take(e - 1, m)
                                m += 1
                    act.wait_ge(used, e * RING + GU + WB)
                    act.activation(act_g[:, :], k.ps[:, UP, :], ACT.Silu).then_inc(gated, 1)
                    act.wait_ge(hot_turned, e + 1)
                    act.copy(turned_hot[:, :], k.ps[:, TURN_HOT, 0:n]).then_inc(hot_kept, 1)
                    if not end:
                        round_own(e + 1, 0)
                    act.wait_ge(hid_turned, e + 1)
                    act.copy(hid_t[:, 0].rearrange("p a f -> p (a f)"), k.ps[:, TURN_HID, :]).then_inc(hid_rounded, 1)
                    act.wait_ge(weighed, e + 1)
                    act.copy(slot_w[:, :], k.ps[:, UP, 0:1]).then_inc(weight_kept, 1)
                    if not end:
                        round_own(e + 1, 1)
                        for t in range(WB):
                            split(e + 1, t)
                    act.wait_ge(weight_kept, e + 1)
                    act.wait_ge(used, e * RING + RING + WB)
                    for half in range(2):
                        act.mul(y[:, 0, half * 512:(half + 1) * 512], k.ps[:, DOWN + half, :], slot_w[:, 0:1]).then_inc(y_rounded, 1)

                act.sem_inc(taken, PRE)
                for t in range(WB):
                    split(0, t)
                for half in range(2):
                    round_own(0, half)
                rounds(act, expert)
                for m in range(KD):
                    take(EXPERTS - 1, m)

            @block.vector
            def _(dve):
                def select(e, s):
                    for tt in range(tt_n):
                        ts = dve.tensor_scalar(onehot[:, s, tt, :], slot_number, place[:, tt, bass.ds(e, 1)], None, ALU.is_equal)
                    ts.then_inc(selected, 1)

                def split(e, s):
                    dve.wait_ge(w_rounded, e * RING + s + 1)
                    dve.tensor_tensor(w_lo[:, s % WB].rearrange("p h f -> p (h f)"),
                                      k.ring[:, (first + s) % RING].rearrange("p a f -> p (a f)"),
                                      w_hi[:, s % WB].rearrange("p h f -> p (h f)"), ALU.subtract).then_inc(w_split, 1)

                def split_own(e, half):
                    dve.wait_ge(own_rounded, e * 2 + half + 1)
                    part = slice(half * 4, (half + 1) * 4)
                    dve.tensor_tensor(own[:, 1, part, :].rearrange("p a f -> p (a f)"), k.ps[:, GATHER + half, :],
                                      own[:, 0, part, :].rearrange("p a f -> p (a f)"), ALU.subtract).then_inc(own_split, 1)

                def expert(e, s, start, end):
                    if not end:
                        select(e + 1, 1 - s)
                    for t in range(GU):
                        split(e, WB + t)
                    dve.wait_ge(gated, e + 1)
                    dve.tensor_tensor(hid[:, :], act_g[:, :], k.ps[:, UP + 1, :], ALU.mult).then_inc(hidden, 1)
                    if not end:
                        split_own(e + 1, 0)
                    dve.wait_ge(hid_rounded, e + 1)
                    dve.tensor_tensor(hid_t[:, 1].rearrange("p a f -> p (a f)"), k.ps[:, TURN_HID, :],
                                      hid_t[:, 0].rearrange("p a f -> p (a f)"), ALU.subtract).then_inc(hid_split, 1)
                    if not end:
                        split_own(e + 1, 1)
                        for t in range(WB):
                            split(e + 1, t)
                    for half in range(2):
                        dve.wait_ge(y_rounded, e * 2 + half + 1)
                        part = slice(half * 512, (half + 1) * 512)
                        dve.scalar_tensor_tensor(y[:, 1, part], k.ps[:, DOWN + half, :], slot_w[:, 0:1], y[:, 0, part],
                                                 ALU.mult, ALU.subtract).then_inc(y_split, 1)

                select(0, 0)
                for t in range(WB):
                    split(0, t)
                for half in range(2):
                    split_own(0, half)
                rounds(dve, expert)

            @block.gpsimd
            def _(pool):
                pool.sem_inc(added, PRE)
                with pool.Fori(0, EXPERTS) as e:
                    for m in range(KD):
                        pool.wait_ge(taken, e * KD + m + 1 + PRE)
                        xs = x[:, m, segs[0] * T:segs[0] * T + n]
                        pool.tensor_tensor(xs, gated_y[:, m % 2, :], xs, ALU.add).then_inc(added, 1)
                pool.wait_ge(added, EXPERTS * KD + PRE)


def moe_late(k, x, segs, gate, name, n, tt_n, first, late, fullest):
    nc = k.nc
    with ExitStack() as local:
        def sb(nm, shape):
            return local.enter_context(nc.sbuf_tensor(f"{name}_{nm}", shape, F32))

        own_w = sb("weights", [P, RING, TILES, P])
        diag = sb("diag", [P, tt_n, P])
        hid = sb("hid", [P, KE, n])
        act_g = sb("act_g", [P, 2, n])
        with stage_semaphores(nc, name, "read", "spread", "diag_made", "product", "gated", "hidden", "down", "added"
                              ) as sems, nc.Block(name=name, no_gpsimd_drain=True) as block:
            read, spread, diag_made, product, gated, hidden, down, added = sems
            PRE = 2

            @block.sync
            def _(sp):
                with sp.If(fullest > P):
                    sp.sem_inc(down, KD)
                    with sp.Fori(0, EXPERTS) as e:
                        sp.wait_ge(down, e * KD + KD)
                        for s in range(RING):
                            sp.dma_start(own_w[:, s], k.weights[first + s + e * RING]).then_inc(read, 16)

            @block.tensor
            def _(pe):
                with pe.If(fullest > P):
                    with pe.Fori(0, EXPERTS) as e:
                        pe.wait_ge(read, e * (16 * RING) + 16 * RING)
                        for m in range(KE):
                            pe.wait_ge(hidden, e * KE + m + 1)
                            for half in range(2):
                                for t in range(KD):
                                    mm = pe.matmul(k.ps[:, m % 2 + 2 * half, 0:n], own_w[:, t, half * KE + m, :], k.h[:, t, 0:n],
                                                   start=(t == 0), stop=(t == KD - 1))
                            mm.then_inc(product, 1)
                            if m == 0:
                                pe.wait_ge(diag_made, e + 1)
                                for tt in range(tt_n):
                                    mm = pe.matmul(k.ps[:, 6, tt * P:(tt + 1) * P], k.ones[:, :], diag[:, tt, :], start=True, stop=True)
                                mm.then_inc(spread, 1)
                        pe.wait_ge(hidden, e * KE + KE + PRE)
                        for m in range(KD):
                            pe.wait_ge(added, e * KD + m + 1)
                            for t in range(KE):
                                mm = pe.matmul(k.ps[:, 4 + m % 2, 0:n], own_w[:, 2 * KE + t, m, :], hid[:, t, :],
                                               start=(t == 0), stop=(t == KE - 1))
                            mm.then_inc(down, 1)

            @block.scalar
            def _(act):
                with act.If(fullest > P):
                    with act.Fori(0, EXPERTS) as e:
                        for m in range(KE):
                            act.wait_ge(product, e * KE + m + 1)
                            act.wait_ge(hidden, e * KE + m + 1)
                            act.activation(act_g[:, m % 2, :], k.ps[:, m % 2, 0:n], ACT.Silu).then_inc(gated, 1)

            @block.vector
            def _(dve):
                with dve.If(fullest > P):
                    dve.sem_inc(hidden, PRE)
                    dve.sem_inc(added, PRE)
                    with dve.Fori(0, EXPERTS) as ex:
                        for tt in range(tt_n):
                            dg = dve.tensor_scalar(diag[:, tt, :], k.ident[:, :], late[:, tt, bass.ds(ex, 1)], None, ALU.mult)
                        dg.then_inc(diag_made, 1)
                        for m in range(KE):
                            dve.wait_ge(gated, ex * KE + m + 1)
                            dve.tensor_tensor(act_g[:, m % 2, :], act_g[:, m % 2, :], k.ps[:, m % 2 + 2, 0:n], ALU.mult)
                            dve.drain()
                            if m == 0:
                                dve.wait_ge(spread, ex + 1)
                            dve.tensor_tensor(hid[:, m, :], act_g[:, m % 2, :], k.ps[:, 6, 0:n], ALU.mult).then_inc(hidden, 1)
                        for m in range(KD):
                            dve.wait_ge(down, ex * KD + m + 1 + KD)
                            for j, s in enumerate(segs):
                                xs = x[:, m, s * T:(s + 1) * T]
                                ad = dve.scalar_tensor_tensor(xs, k.ps[:, 4 + m % 2, j * T:(j + 1) * T], gate[:, m, s:s + 1], xs,
                                                              ALU.mult, ALU.add)
                            ad.then_inc(added, 1)


def odd_mixer(k, x, col, gain, shift, gate, hmask, reset):
    nc = k.nc
    q_slots, g_slots, v_slots, f_slots, o_slots = k.take(8), k.take(8), k.take(8), k.take(16), k.take(8)
    H = k.sq
    outer = ExitStack()
    with outer:
        def sb(name, shape):
            return outer.enter_context(nc.sbuf_tensor(name, shape, F32))

        q = sb("hg_q", [P, GH, T])
        sg = sb("hg_g", [P, GH, T])
        v = sb("hg_v", [P, TT, GH * P])
        f = sb("hg_f", [P, 2, GH, T2])
        lb = sb("hg_lbs", [P, 3, GH])
        o = q
        lb_in = col("hg_lb")
        with stage_semaphores(nc, "odd_in", *NORM_SEMS, "made", "ready", "product", "kept", "v_used", "v_kept", "lb1", "lb2",
                              "lb_done", "forgot") as sems, nc.Block(name="odd_in", no_gpsimd_drain=True) as block:
            norm, (made, ready, product, kept, v_used, v_kept, lb1, lb2, lb_done, forgot) = sems[:4], sems[4:]

            @block.sync
            def _(sp):
                k.refill(sp, q_slots, 16, product)
                k.refill(sp, v_slots, 7, v_used)
                k.refill(sp, v_slots + 7, 1, product, mult=8, base=16)
                k.refill(sp, f_slots, 16, product, base=24)

            @block.tensor
            def _(pe):
                norm_tensor(k, pe, norm, T2)
                pe.wait_ge(ready, KD * SEGS)
                for m in range(16):
                    if m >= 4:
                        pe.wait_ge(kept, m - 3)
                    w = k.slot(pe, q_slots + m)
                    for t in range(KD):
                        mm = pe.matmul(k.ps[:, m % 4, 0:T], w[:, t, :], H[:, t, T:T2], start=(t == 0), stop=(t == KD - 1))
                    mm.then_inc(product, 1)
                pe.wait_ge(kept, 16)
                for t in range(KD):
                    w = k.slot(pe, v_slots + t).rearrange("p (a b) c -> p a (b c)", a=2)
                    for tt in range(TT):
                        for half in range(2):
                            mm = pe.matmul(k.ps[:, tt * 2 + half, :], H[:, t, tt * P:(tt + 1) * P], w[:, half, :],
                                           start=(t == 0), stop=(t == KD - 1))
                            if t == KD - 1:
                                mm.then_inc(product, 1)
                    if t < KD - 1:
                        mm.then_inc(v_used, 1)
                for m in range(16):
                    if m < 4:
                        pe.wait_ge(kept, 16 + m + 1)
                    else:
                        pe.wait_ge(kept, 24 + m - 3)
                    w = k.slot(pe, f_slots + m)
                    for t in range(KD):
                        mm = pe.matmul(k.ps[:, m % 4, :], w[:, t, :], H[:, t, :], start=(t == 0), stop=(t == KD - 1))
                    mm.then_inc(product, 1)

            @block.scalar
            def _(act):
                norm_scalar(k, act, norm, x, T2)
                act.wait_ge(norm[1], 1)
                mod_norm_shift(k, act, (0, 1), shift, made, ready, col_major=True)
                act.wait_ge(lb1, 1)
                act.activation(lb[:, 0:2, :], lb[:, 0:2, :], ACT.Exp).then_inc(lb2, 1)
                for m in range(16):
                    act.wait_ge(product, m + 1)
                    act.activation((q if m < 8 else sg)[:, m % 8, :], k.ps[:, m % 4, 0:T], ACT.Silu).then_inc(kept, 1)
                for n in range(8):
                    act.wait_ge(product, 16 + n + 1)
                    act.activation(v[:, n // 2, n % 2 * 512:(n % 2 + 1) * 512], k.ps[:, n, :], ACT.Copy).then_inc(kept, 1)
                for m in range(16):
                    act.wait_ge(product, 24 + m + 1)
                    act.activation(f[:, m // 8, m % 8, :], k.ps[:, m % 4, :], ACT.Sigmoid).then_inc(kept, 1)

            @block.vector
            def _(dve):
                dve.tensor_tensor(lb[:, 2, :], lb_in[:, 0:GH], lb_in[:, GH:], ALU.max)
                dve.drain()
                for i in range(2):
                    lw = dve.tensor_tensor(lb[:, i, :], lb_in[:, i * GH:(i + 1) * GH], lb[:, 2, :], ALU.subtract)
                lw.then_inc(lb1, 1)
                mod_norm_vector(k, dve, norm, x, (0, 1), gain, T2, made)
                dve.wait_ge(lb2, 1)
                dve.tensor_tensor(lb[:, 2, :], lb[:, 0, :], lb[:, 1, :], ALU.add)
                dve.drain()
                dve.reciprocal(lb[:, 2, :], lb[:, 2, :])
                dve.drain()
                dve.tensor_tensor(lb[:, 0, :], lb[:, 1, :], lb[:, 2, :], ALU.mult)
                dve.drain()
                dve.tensor_scalar(lb[:, 1, :], lb[:, 0, :], -1.0, 1.0, ALU.mult, ALU.add)
                dve.drain()
                for m in range(16):
                    dve.wait_ge(kept, 24 + m + 1)
                    ff = f[:, m // 8, m % 8, :]
                    dve.tensor_scalar(ff, ff, lb[:, 1, m % 8:m % 8 + 1], lb[:, 0, m % 8:m % 8 + 1], ALU.mult, ALU.add)

        lf = (k.h, k.sq)
        with nc.Block(name="log_forget", no_gpsimd_drain=True) as block:

            @block.scalar
            def _(act):
                for d in range(2):
                    act.activation(lf[d][:, :, :], f[:, d], ACT.Ln)

        with ExitStack() as local:
            def tb(name, shape):
                return local.enter_context(nc.sbuf_tensor(name, shape, F32))

            vh = x[:, 0:2, 0:T].rearrange("p a (b v) -> p a b v", b=2)
            g = tb("g_cum", [P, 2, T2])
            ke = tb("k_end", [P, 2, T2])
            kx = (k.root, k.rstd)
            rel = tb("rel", [P, 2, 5, T])
            QM, KM, QB, KB, QS = range(5)
            HC = GC // 2
            dec = tb("dec", [P, 2, 2 * NCH])
            ket = tb("k_end_tok", [P, 2, TT, P])
            att = tb("att", [P, 2, 2, P])
            sin = tb("s_in", [P, 2, NCH + 1, P])
            with stage_semaphores(nc, "hgrn", "cleared", "cum", "exps", "rels", "kends", "turned", "turn_kept", "atts",
                                  "att_kept", "states", "chained", "summed", "kept") as sems, \
                    nc.Block(name="hgrn_scan", no_gpsimd_drain=True) as block:
                cleared, cum, exps, rels, kends, turned, turn_kept, atts, att_kept, states, chained, summed, kept = sems

                def order(d):
                    ctx_ch = list(range(NCH))
                    lat_ch = list(range(NCH, 2 * NCH))
                    return (ctx_ch + lat_ch) if d == 0 else (ctx_ch[::-1] + lat_ch[::-1])

                @block.vector
                def _(dve):
                    dve.memset(att[:, :, :, :], 0.0)
                    dve.memset(sin[:, :, :, :], 0.0)
                    dve.sem_inc(turned, 2)
                    dve.sem_inc(summed, 1)
                    with dve.Fori(0, GH) as h:
                        dve.drain()
                        dve.wait_ge(summed, h * 2 + 1)
                        dve.tensor_copy(vh, v[:, :, bass.ds(h * P, P)].rearrange("p (a b) v -> p a b v", b=2))
                        for d in range(2):
                            u = h * 2 + d
                            gg, L = g[:, d, :], lf[d][:, bass.ds(h, 1), :].rearrange("p a t -> p (a t)")
                            F = f[:, d, bass.ds(h, 1), :].rearrange("p a t -> p (a t)")
                            dve.tensor_tensor_scan(gg, reset, L, 0.0, ALU.mult, ALU.add)
                            dve.tensor_scalar(kx[d][:, :], F, -1.0, 1.0, ALU.mult, ALU.add)
                            dve.drain()
                            chunks = gg.rearrange("p (c t) -> p c t", t=GC)
                            dve.tensor_copy(dec[:, d, :], chunks[:, :, GC - 1])
                            dve.drain()
                            end = dec[:, d, :].unsqueeze(2).broadcast_to([P, 2 * NCH, GC])
                            if d == 0:
                                dve.tensor_tensor(ke[:, d, :].rearrange("p (c t) -> p c t", t=GC), end, chunks, ALU.subtract)
                                mid, edge = HC // 2 - 1, HC - 1
                            else:
                                dve.tensor_tensor(ke[:, d, :], gg, L, ALU.subtract)
                                dve.drain()
                                dve.tensor_tensor(chunks, end, ke[:, d, :].rearrange("p (c t) -> p c t", t=GC), ALU.subtract)
                                dve.drain()
                                mid, edge = HC // 2, HC
                            lat = gg[:, T:].rearrange("p (c t) -> p c t", t=GC)
                            for q_at, k_at, size, ref in ((QM, KM, HC, mid), (QB, KB, GC, edge)):
                                own = gg[:, T:].rearrange("p (c t) -> p c t", t=size)
                                refs = own[:, :, ref:ref + 1].broadcast_to([P, T // size, size])
                                rq, rk = [rel[:, d, i, :].rearrange("p (c t) -> p c t", t=size) for i in (q_at, k_at)]
                                dve.tensor_tensor(rq, own, refs, ALU.subtract)
                                dve.tensor_tensor(rk, refs, own, ALU.subtract)
                            dve.drain()
                            dve.tensor_scalar(rel[:, d, QB:KB + 1, :], rel[:, d, QB:KB + 1, :], 0.0, None, ALU.min)
                            dve.tensor_copy(rel[:, d, QS, :], gg[:, T:]).then_inc(cum, 1)
                        for d in range(2):
                            u = h * 2 + d
                            dve.wait_ge(exps, u + 1)
                            dve.tensor_tensor(ke[:, d, :], ke[:, d, :], kx[d][:, :], ALU.mult).then_inc(kends, 1)
                            qh = q[:, bass.ds(h, 1), :].rearrange("p a t -> p (a t)")
                            for i, by in ((QM, qh), (QB, qh), (QS, qh), (KM, kx[d][:, T:]), (KB, kx[d][:, T:])):
                                last = dve.tensor_tensor(rel[:, d, i, :], rel[:, d, i, :], by, ALU.mult)
                            last.then_inc(rels, 1)
                        for d in range(2):
                            u = h * 2 + d
                            dve.wait_ge(states, u + 1)
                            od = order(d)
                            for i, c in enumerate(od[:-1]):
                                if i == 1:
                                    for j in range(2):
                                        if j:
                                            dve.drain()
                                        cp = dve.copy_predicated(
                                            att[:, d], hmask[:, 2 * j + d, :].bitcast(I32).unsqueeze(1).broadcast_to([P, 2, P]),
                                            k.ps[:, 1, 2 * j * P:2 * (j + 1) * P].rearrange("p (a l) -> p a l", a=2))
                                    cp.then_inc(att_kept, 1)
                                if i:
                                    dve.drain()
                                src = sin[:, d, 0, :] if i < NCH else sin[:, d, 1 + i - NCH, :]
                                dst = sin[:, d, 0, :] if i < NCH - 1 else sin[:, d, 1 + i + 1 - NCH, :]
                                cs_ = k.ps[:, 2 + c % 2, c // 2 * P:(c // 2 + 1) * P]
                                if i == 0:
                                    ch = dve.tensor_copy(dst, cs_)
                                else:
                                    ch = dve.scalar_tensor_tensor(dst, src, dec[:, d, c:c + 1], cs_, ALU.mult, ALU.add)
                            ch.then_inc(chained, 1)

                @block.scalar
                def _(act):
                    with act.Fori(0, GH) as h:
                        for d in range(2):
                            u = h * 2 + d
                            act.wait_ge(cum, u + 1)
                            act.activation(ke[:, d, :], ke[:, d, :], ACT.Exp)
                            act.activation(dec[:, d, :], dec[:, d, :], ACT.Exp)
                            act.activation(rel[:, d].rearrange("p i t -> p (i t)"), rel[:, d].rearrange("p i t -> p (i t)"),
                                           ACT.Exp).then_inc(exps, 1)
                        for d in range(2):
                            u = h * 2 + d
                            act.wait_ge(turned, u + 3)
                            act.activation(ket[:, d].rearrange("p a k -> p (a k)"), k.ps[:, 0, :], ACT.Copy).then_inc(turn_kept, 1)
                        act.wait_ge(summed, h * 2 + 3)
                        act.activation(o[:, bass.ds(h, 1), :].rearrange("p a t -> p (a t)"), k.ps[:, 6, 0:T], ACT.Copy
                                       ).then_inc(kept, 1)

                @block.tensor
                def _(pe):
                    with pe.Fori(0, GH) as h:
                        for d in range(2):
                            u = h * 2 + d
                            pe.wait_ge(kends, u + 1)
                            if d:
                                pe.wait_ge(turn_kept, u)
                            for a in range(TT):
                                mm = pe.transpose(k.ps[:, 0, a * P:(a + 1) * P], ke[:, d, a * P:(a + 1) * P], k.ident[:, :])
                            mm.then_inc(turned, 1)
                            pe.wait_ge(rels, u + 1)
                            if d:
                                pe.wait_ge(chained, u)
                            for j, (q_at, k_at) in enumerate(((QM, KM), (QB, KB))):
                                for a in range(2):
                                    mm = pe.matmul(k.ps[:, 1, (2 * j + a) * P:(2 * j + a + 1) * P],
                                                   rel[:, d, k_at, a * P:(a + 1) * P], rel[:, d, q_at, a * P:(a + 1) * P],
                                                   start=True, stop=True)
                            mm.then_inc(atts, 1)
                            pe.wait_ge(turn_kept, u + 1)
                            for i, c in enumerate(order(d)[:-1]):
                                a, r = c // 2, c % 2 * GC
                                mm = pe.matmul(k.ps[:, 2 + c % 2, c // 2 * P:(c // 2 + 1) * P], ket[r:r + GC, d, a, :],
                                               vh[r:r + GC, a // 2, a % 2, :], start=True, stop=True)
                            mm.then_inc(states, 1)
                            pe.wait_ge(att_kept, u + 1)
                            for a in range(2):
                                pe.matmul(k.ps[:, 6, a * P:(a + 1) * P], vh[:, 1, a, :], att[:, d, a, :],
                                          start=(d == 0 and a == 0), stop=False, skip_group_check=True)
                            pe.wait_ge(chained, u + 1)
                            for i, c in enumerate(order(d)[NCH:]):
                                cc = c - NCH
                                mm = pe.matmul(k.ps[:, 6, cc * GC:(cc + 1) * GC], sin[:, d, 1 + i, :],
                                               rel[:, d, QS, cc * GC:(cc + 1) * GC], start=False, stop=(d == 1 and i == NCH - 1),
                                               skip_group_check=True)
                            mm.then_inc(summed, 1)

        with stage_semaphores(nc, "hg_out", "squared", "summed", "rooted", "normed", "product") as sems, \
                nc.Block(name="hgrn_readout", no_gpsimd_drain=True) as block:
            squared, summed, rooted, normed, product = sems
            oo = o[:, :, :].rearrange("p (a b) t -> p a (b t)", b=2)
            gg = sg[:, :, :].rearrange("p (a b) t -> p a (b t)", b=2)

            @block.sync
            def _(sp):
                k.refill(sp, o_slots, 8, product)

            @block.scalar
            def _(act):
                for a in range(4):
                    act.activation(k.sq[:, a, :], oo[:, a, :], ACT.Square).then_inc(squared, 1)
                for a in range(4):
                    act.wait_ge(summed, a + 1)
                    act.activation(k.sq[:, 4 + a, :], k.ps[:, a, :], ACT.Sqrt, scale=1.0 / P, bias=k.eps[:, 0:1]).then_inc(rooted, 1)

            @block.tensor
            def _(pe):
                for a in range(4):
                    pe.wait_ge(squared, a + 1)
                    pe.matmul(k.ps[:, a, :], k.ones[:, :], k.sq[:, a, :], start=True, stop=True).then_inc(summed, 1)
                pe.wait_ge(normed, 4)
                for m in range(KD):
                    w = k.slot(pe, o_slots + m)
                    for t in range(KD):
                        mm = pe.matmul(k.ps[:, m, 0:T], w[:, t, :], o[:, t, :], start=(t == 0), stop=(t == KD - 1))
                    mm.then_inc(product, 1)

            @block.vector
            def _(dve):
                for a in range(4):
                    dve.wait_ge(rooted, a + 1)
                    dve.reciprocal(k.sq[:, 4 + a, :], k.sq[:, 4 + a, :])
                    dve.drain()
                    dve.scalar_tensor_tensor(oo[:, a, :], oo[:, a, :], col("hg_norm_g"), k.sq[:, 4 + a, :], ALU.mult, ALU.mult)
                    dve.drain()
                    dve.tensor_tensor(oo[:, a, :], oo[:, a, :], gg[:, a, :], ALU.mult).then_inc(normed, 1)
                for m in range(KD):
                    dve.wait_ge(product, m + 1)
                    xs = x[:, m, T:T2].rearrange("p (r w) -> p r w", r=ROWS)
                    dve.scalar_tensor_tensor(xs, k.ps[:, m, 0:T].rearrange("p (w r) -> p r w", r=ROWS), gate[:, m, 1:2], xs,
                                             ALU.mult, ALU.add)


def second_block_stream(a):
    out = [a["mod_w_2"].reshape(2, KD, P, 3, 2 * D).transpose(0, 3, 1, 2, 4)
           .reshape(6 * KD, P, 2, D).transpose(0, 2, 1, 3).reshape(-1, P, D)]
    w = a["ab_w_in_2"][0]
    xbc0, dt0 = SH * SP_, SH * SP_ + XBC * P
    cf0 = dt0 + 2 * SH
    tiles = out_tiles(np.concatenate([w[:, :dt0], w[:, cf0:]], axis=1))
    v0, g0 = 8 + XBC, 8 + XBC + 8
    order = [i for m in range(8) for i in (v0 + m, g0 + m)] + list(range(8 + XBC))
    out.append(tiles[order])
    out.append(out_tiles(a["ab_w_out_2"][0]))

    def experts(i):
        g = a["moe_w_gate_2"][i].reshape(EXPERTS, KD, P, KE * P)
        u = a["moe_w_up_2"][i].reshape(EXPERTS, KD, P, KE * P)
        gu = np.concatenate([g, u], axis=3)
        dn = a["moe_w_down_2"][i].reshape(EXPERTS, KE, P, TILES * P)
        return np.concatenate([gu, dn], axis=1).reshape(-1, P, TILES * P)

    out.append(experts(0))
    w = a["hg_w_in_2"][0]
    kd = GH * P
    out.append(out_tiles(w[:, :2 * kd]))
    out.append(w[:, 2 * kd:3 * kd].reshape(KD, P, kd))
    out.append(out_tiles(w[:, 3 * kd:]))
    out.append(out_tiles(a["hg_w_out_2"][0]))
    out.append(experts(1))
    return out


def second_block_cols(a, cl, at):
    def put(name, arr):
        at[name] = (sum(c.shape[1] for c in cl), arr.shape[1])
        cl.append(arr)

    def spread(row):
        return np.broadcast_to(np.asarray(row).reshape(1, -1), (P, np.asarray(row).size))

    put("cond", np.stack([a["c_ctx_2"], a["c_2"][0]], -1).reshape(KD, P, 2).transpose(1, 0, 2).reshape(P, -1))
    put("mod_b", np.concatenate([cols(a["mod_b_2"][i]) for i in range(2)], 1))
    put("mix_g", np.concatenate([cols(a["norm_mix_g_2"][i]) for i in range(2)], 1))
    put("ffn_g", np.concatenate([cols(a["norm_ffn_g_2"][i]) for i in range(2)], 1))
    put("router_w", a["router_w_2"].reshape(KD, P, EXPERTS).transpose(1, 0, 2).reshape(P, -1))
    put("router_b", spread(a["router_b_2"]))
    taps = np.concatenate([a["ssd_conv_w_2"][0], a["ssd_conv_b_2"]], 0)
    put("ssd_taps", taps.reshape(SCONV + 1, XBC, P).transpose(2, 1, 0).reshape(P, -1))
    taps = np.concatenate([a["cf_dw_w_2"][0], a["cf_dw_b_2"]], 0)
    put("cf_taps", taps.reshape(CFK + 1, KD, P).transpose(2, 1, 0).reshape(P, -1))
    dt0 = SH * SP_ + XBC * P
    put("dt_w", a["ab_w_in_2"][0][:, dt0:dt0 + 2 * SH].reshape(KD, P, 2 * SH).transpose(1, 0, 2).reshape(P, -1))
    put("dt_bias", spread(a["ssd_dt_bias_2"][0]))
    put("a_log", spread(a["ssd_a_log_2"][0]))
    put("ssd_d", spread(a["ssd_d_2"][0]))
    put("ssd_norm_g", cols(a["ssd_norm_g_2"][0]))
    put("ln_g", cols(a["cf_ln_g_2"][0]))
    put("ln_b", cols(a["cf_ln_b_2"][0]))
    put("hg_lb", np.concatenate([cols(a["hg_lb_2"][i]) for i in range(2)], 1))
    put("hg_norm_g", cols(a["hg_norm_g_2"][0]))
    put("final_g", cols(a["final_norm_g_2"]))


def second_block_shape_constants():
    i = np.arange(P)
    tri0 = (i[:, None] <= i[None]).astype(np.float32)
    half = i // (GC // 2)
    near = half[:, None] == half[None]
    same = (i[:, None] // GC == i[None] // GC) & ~near
    reset = (np.arange(T2) % GC != 0).astype(np.float32)
    return np.concatenate([tri0, tri0.T, tri0 * near, tri0.T * near, tri0 * same, tri0.T * same, np.broadcast_to(reset, (P, T2)),
                           np.broadcast_to(i.astype(np.float32), (P, P))], 1)


def second_block(k, x, col, tri, hmask, reset, slot_number, stop=None):
    k.upto = tri[:, 0, :]
    mods = k.sb("mods", [P, 2, N_MOD * KD, 2])
    gains = k.sb("gains", [P, 2, 2, KD, 2])
    modulation(k, col("cond").rearrange("p (t s) -> p t s", s=2), col("mod_b"), mods)
    scaled_gains(k, mods, (col("mix_g"), col("ffn_g")), gains)

    def part(layer, i):
        return mods[:, layer, i * KD:(i + 1) * KD, :]

    router_w = col("router_w").rearrange("p (t e) -> p t e", t=KD)
    with ExitStack() as local:
        def sb(name, shape):
            return local.enter_context(k.nc.sbuf_tensor(name, shape, F32))

        zs = sb("zs", [P, KD, T2])
        cf = k.h
        dt = sb("dt", [P, TT, 2 * SH])
        with k.nc.sbuf_tensor("xbc", [P, XBC, T2], F32) as xbc:
            even_in(k, x, col, gains[:, 0, 0], part(0, 0), zs, xbc, dt)
            ssd(k, col, tri, dt, zs, xbc)
        conformer_norm(k, cf, col("ln_g"), col("ln_b"))
        even_out(k, x, zs, cf, part(0, 2))
    if stop == "mix0":
        return
    moe(k, x, (0, 1), gains[:, 0, 1], part(0, 3), part(0, 5), router_w, col("router_b"), slot_number, "moe0")
    if stop == "moe0":
        return
    odd_mixer(k, x, col, gains[:, 1, 0], part(1, 0), part(1, 2), hmask, reset)
    if stop == "mix1":
        return
    moe(k, x, (1,), gains[:, 1, 1], part(1, 3), part(1, 5), router_w, col("router_b"), slot_number, "moe1")


def build_program(nc, ins, out, n_slots, col_at):
    with ExitStack() as ctx:
        k = Kit(nc, ctx, ins["weights"], n_slots)
        stored = ctx.enter_context(nc.semaphore("stored"))
        both = k.sb("both", [P, KD, T2])
        small = k.sb("cols", [P, ins["cols"].shape[1]])
        masks = k.sb("masks", [P, 7 * P + T2])
        rope = k.sb("rope", [P, 1 + ROT])
        x = both[:, :, T:T2]
        tri = masks[:, 0:2 * P].rearrange("p (d l) -> p d l", d=2)
        hmask = masks[:, 2 * P:6 * P].rearrange("p (d l) -> p d l", d=4)
        reset = masks[:, 6 * P:6 * P + T2]
        slot_number = masks[:, 6 * P + T2:]

        def col(name):
            at, n = col_at[name]
            return small[:, at:at + n]

        def taps(i):
            return col(f"taps{i}").rearrange("p (t f) -> p t f", f=4)

        constants(k, [(x, ins["x"]), (both[:, :, 0:T], ins["context"]), (small[:, :], ins["cols"]),
                      (masks[:, :], ins["masks"]), (rope[:, :], ins["rope"])])
        pool_mixer(k, x, col("norm_mix0"), col("pool_scale"), ins["rcount"])
        conv_ffn(k, x, col("norm_ffn0"), taps(0), "ffn0")
        ple(k, x, col("norm_ple0"), ins["ple_in"][0], "ple0")
        nsa(k, x, col("norm_kv"), col("norm_mix1"), ins["positions"], rope[:, 0:1], rope[:, 1:], ins["gate_w"],
            ins["cmp_w1"], ins["cmp_small"], ins["attn_masks"])
        conv_ffn(k, x, col("norm_ffn1"), taps(1), "ffn1")
        ple(k, x, col("norm_ple1"), ins["ple_in"][1], "ple1")
        final_norm(k, x, col("norm_final"), "norm_first")
        second_block(k, both, col, tri, hmask, reset, slot_number)
        final_norm(k, x, col("final_g"), "norm_second")
        with nc.Block(name="store") as block:

            @block.sync
            def _(sp):
                sp.dma_start(out, x).then_inc(stored, 16)
                sp.wait_ge(stored, 16)


def lay_out(a):
    first, parts, at = first_block_arrays(a)
    second_block_cols(a, parts, at)
    first.update(first_block_shape_constants())
    d = {
        "weights": np.concatenate(first_block_stream(a) + second_block_stream(a)),
        "cols": np.concatenate(parts, 1),
        "masks": second_block_shape_constants(),
        "x": first["x_in"], "context": a["ctx_2"][0].T.reshape(KD, P, T).transpose(1, 0, 2),
        "ple_in": first["p_in"], "positions": first["pos_in"], "gate_w": first["gate_w_in"],
        "cmp_w1": first["cmp_w1_in"], "cmp_small": first["cmp_small_in"], "rcount": first["rcount_in"],
        "rope": first["rope_in"], "attn_masks": first["masks_in"],
    }
    return {n: np.ascontiguousarray(v) for n, v in d.items()}, at


def kernel(**inputs):
    import concourse.bacc as bacc
    from concourse.bass_utils import run_bass_kernel_spmd

    arrays, at = lay_out({n: np.asarray(v) for n, v in inputs.items()})
    nc = bacc.Bacc("TRN2", target_bir_lowering=False, num_devices=1)
    ins = {n: nc.dram_tensor(f"in_{n}", v.shape, mybir.dt.from_np(v.dtype), kind="ExternalInput").ap()
           for n, v in arrays.items()}
    out = nc.dram_tensor("out", (P, KD, T), F32, kind="ExternalOutput").ap()
    build_program(nc, ins, out, arrays["weights"].shape[0], at)
    got = run_bass_kernel_spmd(nc, [{f"in_{n}": v for n, v in arrays.items()}], core_ids=[0])
    y = got.results[0]["out"]
    return y.transpose(1, 0, 2).reshape(D, T).T.reshape(1, T, D)
```
